# Optimizing a Trainium2 kernel written in Bass

```python
import jax
import jax.numpy as jnp
from jax import lax
import numpy as np
import math
import jax, jax.numpy as jnp

D_MODEL = 1024
BATCH = 1
SEQ = 256
DEPTH = 1

D_MIX = D_MODEL
D_ATT = D_MIX // 2
ATT_HEAD_DIM = 64
ATT_HEADS = D_ATT // ATT_HEAD_DIM
D_MLSTM = D_MIX - D_ATT
MLSTM_HEADS = 4
MLSTM_HEAD_DIM = D_MLSTM // MLSTM_HEADS
IN_WIDTH = 3 * D_ATT + 4 * D_MLSTM + 2 * MLSTM_HEADS

MOBA_BLOCK = 256
MOBA_TOPK = 3
MOBA_Q_CHUNK = 32
ROPE_THETA = 10000.0

MLSTM_CHUNK = 128
CONV_WIDTH = 4

N_GROUPS = 4
EXPERTS_PER_GROUP = 8
N_EXPERTS = N_GROUPS * EXPERTS_PER_GROUP
TOP_K_EXPERTS = 2
D_EXPERT = 512
MOE_BLOCK_ROWS = 256

NORM_EPS = 1e-6
NEG_INF = -1e30


def rms_norm(x, g):
    xf = x.astype(jnp.float32)
    y = xf * lax.rsqrt(jnp.mean(xf * xf, axis=-1, keepdims=True) + NORM_EPS)
    return (y * g.astype(jnp.float32)).astype(x.dtype)

def head_rms_norm(h, g, n_heads):
    b, s, w = h.shape
    hf = h.astype(jnp.float32).reshape(b, s, n_heads, w // n_heads)
    hf = hf * lax.rsqrt(jnp.mean(hf * hf, axis=-1, keepdims=True) + NORM_EPS)
    return (hf.reshape(b, s, w) * g.astype(jnp.float32)).astype(h.dtype)

def modulate(x, g, shift, scale):
    return rms_norm(x, g) * (1.0 + scale[:, None, :]) + shift[:, None, :]

def split_heads(t, n_heads):
    b, s, w = t.shape
    return t.reshape(b, s, n_heads, w // n_heads).transpose(0, 2, 1, 3)

def merge_heads(t):
    b, h, s, d = t.shape
    return t.transpose(0, 2, 1, 3).reshape(b, s, h * d)

def rope(t, positions):
    half = t.shape[-1] // 2
    inv_freq = ROPE_THETA ** (-jnp.arange(half, dtype=jnp.float32) / half)
    ang = positions.astype(jnp.float32)[:, None, :, None] * inv_freq
    cos, sin = jnp.cos(ang), jnp.sin(ang)
    tf = t.astype(jnp.float32)
    t1, t2 = tf[..., :half], tf[..., half:]
    return jnp.concatenate([t1 * cos - t2 * sin, t2 * cos + t1 * sin], axis=-1).astype(t.dtype)

def moba_attention(q, k, v):
    b, h, s, dh = q.shape
    nb = -(-s // MOBA_BLOCK)
    s_pad = nb * MOBA_BLOCK
    pad = ((0, 0), (0, 0), (0, s_pad - s), (0, 0))
    kb = jnp.pad(k, pad).reshape(b, h, nb, MOBA_BLOCK, dh)
    vb = jnp.pad(v, pad).reshape(b, h, nb, MOBA_BLOCK, dh)
    scale = dh ** -0.5

    k_mean = jnp.mean(kb.astype(jnp.float32), axis=3)
    gate = jnp.einsum('bhsd,bhnd->bhsn', q.astype(jnp.float32), k_mean)
    q_blk = jnp.arange(s) // MOBA_BLOCK
    past = jnp.arange(nb)[None, :] < q_blk[:, None]
    gate = jnp.where(past, gate, NEG_INF)
    topk = min(MOBA_TOPK, nb)
    _, sel = lax.top_k(gate, topk)
    sel_valid = sel < q_blk[:, None]

    nqc = s // MOBA_Q_CHUNK

    def to_chunks(t):
        t = t.reshape((b, h, nqc, MOBA_Q_CHUNK) + t.shape[3:])
        return jnp.moveaxis(t, 2, 0)

    bi = jnp.arange(b)[:, None, None]
    hi = jnp.arange(h)[None, :, None]

    def chunk(args):
        q_c, sel_c, valid_c, ci = args
        start = ci * MOBA_Q_CHUNK
        j = start // MOBA_BLOCK
        k_own = lax.dynamic_index_in_dim(kb, j, axis=2, keepdims=False)
        v_own = lax.dynamic_index_in_dim(vb, j, axis=2, keepdims=False)
        q_pos = start + jnp.arange(MOBA_Q_CHUNK)
        k_pos = j * MOBA_BLOCK + jnp.arange(MOBA_BLOCK)
        causal = k_pos[None, :] <= q_pos[:, None]
        qf = q_c.astype(jnp.float32) * scale
        s_own = jnp.where(causal, jnp.einsum('bhqd,bhkd->bhqk', qf, k_own.astype(jnp.float32)), NEG_INF)
        scores = [s_own]
        for r in range(topk):
            k_r = kb[bi, hi, sel_c[..., r]]
            s_r = jnp.einsum('bhqd,bhqkd->bhqk', qf, k_r.astype(jnp.float32))
            scores.append(jnp.where(valid_c[..., r, None], s_r, NEG_INF))
        s_all = jnp.stack(scores, axis=3)
        p = jax.nn.softmax(s_all.reshape(b, h, MOBA_Q_CHUNK, -1), axis=-1).reshape(s_all.shape)
        out = jnp.einsum('bhqk,bhkd->bhqd', p[..., 0, :], v_own.astype(jnp.float32))
        for r in range(topk):
            v_r = vb[bi, hi, sel_c[..., r]]
            out = out + jnp.einsum('bhqk,bhqkd->bhqd', p[..., r + 1, :], v_r.astype(jnp.float32))
        return out.astype(v.dtype)

    out = lax.map(chunk, (to_chunks(q), to_chunks(sel), to_chunks(sel_valid),
                          jnp.arange(nqc, dtype=jnp.int32)))
    return jnp.moveaxis(out, 0, 2).reshape(b, h, s, dh)

def mlstm_chunkwise(q, k, v, i_pre, f_pre):
    b, nh, s, dh = q.shape
    L = MLSTM_CHUNK
    nc = s // L
    q = q.reshape(b, nh, nc, L, dh)
    k = k.reshape(b, nh, nc, L, dh)
    v = v.reshape(b, nh, nc, L, dh)
    logf = jax.nn.log_sigmoid(f_pre).reshape(b, nh, nc, L)
    ig = i_pre.reshape(b, nh, nc, L)
    cum = jnp.cumsum(logf, axis=-1)
    a = cum[..., -1]

    g = a[..., None] - cum + ig
    m_loc = jnp.max(g, axis=-1)
    w = jnp.exp(g - m_loc[..., None])
    c_loc = jnp.einsum('bhcs,bhcse,bhcsd->bhced', w, v, k)
    n_loc = jnp.einsum('bhcs,bhcsd->bhcd', w, k)

    def step(carry, inp):
        c_st, n_st, m_st = carry
        a_c, m_loc_c, c_loc_c, n_loc_c = inp
        m_new = jnp.maximum(a_c + m_st, m_loc_c)
        s_prev = jnp.exp(a_c + m_st - m_new)
        s_loc = jnp.exp(m_loc_c - m_new)
        c_new = s_prev[..., None, None] * c_st + s_loc[..., None, None] * c_loc_c
        n_new = s_prev[..., None] * n_st + s_loc[..., None] * n_loc_c
        return (c_new, n_new, m_new), (c_st, n_st, m_st)

    init = (jnp.zeros((b, nh, dh, dh), jnp.float32),
            jnp.zeros((b, nh, dh), jnp.float32),
            jnp.zeros((b, nh), jnp.float32))
    xs = (jnp.moveaxis(a, 2, 0), jnp.moveaxis(m_loc, 2, 0),
          jnp.moveaxis(c_loc, 2, 0), jnp.moveaxis(n_loc, 2, 0))
    _, (c_prev, n_prev, m_prev) = lax.scan(step, init, xs)
    c_prev = jnp.moveaxis(c_prev, 0, 2)
    n_prev = jnp.moveaxis(n_prev, 0, 2)
    m_prev = jnp.moveaxis(m_prev, 0, 2)

    causal = jnp.tril(jnp.ones((L, L), dtype=bool))
    dmat = jnp.where(causal, cum[..., :, None] - cum[..., None, :] + ig[..., None, :], NEG_INF)
    inter = cum + m_prev[..., None]
    m_t = jnp.maximum(inter, jnp.max(dmat, axis=-1))
    s_qk = jnp.einsum('bhctd,bhcsd->bhcts', q, k) * jnp.exp(dmat - m_t[..., None])
    w_inter = jnp.exp(inter - m_t)
    num = (jnp.einsum('bhcts,bhcse->bhcte', s_qk, v)
           + w_inter[..., None] * jnp.einsum('bhced,bhctd->bhcte', c_prev, q))
    den = jnp.sum(s_qk, axis=-1) + w_inter * jnp.einsum('bhcd,bhctd->bhct', n_prev, q)
    h = num / jnp.maximum(jnp.abs(den), jnp.exp(-m_t))[..., None]
    return h.reshape(b, nh, s, dh)

def causal_conv(u, w, bias):
    ch = u.shape[-1]
    out = lax.conv_general_dilated(u, w[:, None, :], window_strides=(1,),
                                   padding=[(CONV_WIDTH - 1, 0)],
                                   dimension_numbers=('NWC', 'WIO', 'NWC'),
                                   feature_group_count=ch)
    return out + bias

def hier_moe(h, w_rg, b_rg, w_re, b_re, w1, w3, w2):
    t, d = h.shape
    gp = jax.nn.softmax((h @ w_rg + b_rg).astype(jnp.float32), axis=-1)
    g_w, g_idx = lax.top_k(gp, 1)
    el = (h @ w_re + b_re).astype(jnp.float32).reshape(t, N_GROUPS, EXPERTS_PER_GROUP)
    el_sel = jnp.take_along_axis(el, g_idx[:, :, None], axis=1)[:, 0]
    ep = jax.nn.softmax(el_sel, axis=-1)
    e_w, e_loc = lax.top_k(ep, TOP_K_EXPERTS)
    weights = g_w * e_w / jnp.sum(e_w, axis=-1, keepdims=True)
    expert_id = g_idx * EXPERTS_PER_GROUP + e_loc

    n_assign = t * TOP_K_EXPERTS
    flat_e = expert_id.reshape(-1)
    flat_w = weights.reshape(-1)
    flat_tok = jnp.repeat(jnp.arange(t, dtype=jnp.int32), TOP_K_EXPERTS)
    order = jnp.argsort(flat_e)
    sorted_e = flat_e[order]
    counts = jnp.bincount(flat_e, length=N_EXPERTS)
    padded = ((counts + MOE_BLOCK_ROWS - 1) // MOE_BLOCK_ROWS) * MOE_BLOCK_ROWS
    pad_end = jnp.cumsum(padded)
    pad_start = pad_end - padded
    cnt_start = jnp.cumsum(counts) - counts
    dest = pad_start[sorted_e] + (jnp.arange(n_assign) - cnt_start[sorted_e])
    n_rows = n_assign + N_EXPERTS * MOE_BLOCK_ROWS
    n_blocks = n_rows // MOE_BLOCK_ROWS
    row_tok = jnp.zeros((n_rows,), jnp.int32).at[dest].set(flat_tok[order])
    row_w = jnp.zeros((n_rows,), jnp.float32).at[dest].set(flat_w[order])
    block_e = jnp.minimum(jnp.searchsorted(pad_end, jnp.arange(n_blocks) * MOE_BLOCK_ROWS, side='right'),
                          N_EXPERTS - 1)
    xs = h[row_tok].reshape(n_blocks, MOE_BLOCK_ROWS, d)

    def expert_block(args):
        xb, e = args
        return (jax.nn.silu(xb @ w1[e]) * (xb @ w3[e])) @ w2[e]

    ys = lax.map(expert_block, (xs, block_e)).reshape(n_rows, d)
    ys = ys * row_w[:, None].astype(h.dtype)
    return jnp.zeros((t, d), h.dtype).at[row_tok].add(ys)

def first_inputs(seed: int = 0) -> dict:
    key = jax.random.key(seed)
    ks = jax.random.split(key, 24)

    def nrm(k, shape, scale):
        return jax.random.normal(k, shape, jnp.float32) * scale

    x = nrm(ks[0], (BATCH, SEQ, D_MODEL), 1.0)
    c = nrm(ks[1], (BATCH, D_MODEL), 1.0)
    positions = (jnp.arange(SEQ, dtype=jnp.int32)[None, :]
                 + jax.random.randint(ks[2], (BATCH, 1), 0, 1024, dtype=jnp.int32))
    w_ada = nrm(ks[3], (DEPTH, D_MODEL, 6 * D_MODEL), 0.5 * D_MODEL ** -0.5)
    b_ada = nrm(ks[4], (DEPTH, 6 * D_MODEL), 0.02)
    norm1_g = 1.0 + nrm(ks[5], (DEPTH, D_MODEL), 0.02)
    w_in = nrm(ks[6], (DEPTH, D_MODEL, IN_WIDTH), D_MODEL ** -0.5)
    b_gate = jnp.concatenate([
        nrm(ks[7], (DEPTH, MLSTM_HEADS), 0.1),
        jnp.linspace(3.0, 6.0, MLSTM_HEADS, dtype=jnp.float32)[None, :]
        + nrm(ks[8], (DEPTH, MLSTM_HEADS), 0.1)], axis=-1)
    conv_w = nrm(ks[9], (DEPTH, CONV_WIDTH, 2 * D_MLSTM), CONV_WIDTH ** -0.5)
    conv_b = nrm(ks[10], (DEPTH, 2 * D_MLSTM), 0.02)
    attn_out_g = 1.0 + nrm(ks[11], (DEPTH, D_ATT), 0.02)
    mlstm_out_g = 1.0 + nrm(ks[12], (DEPTH, D_MLSTM), 0.02)
    w_out = nrm(ks[13], (DEPTH, D_MIX, D_MODEL), D_MIX ** -0.5)
    norm2_g = 1.0 + nrm(ks[14], (DEPTH, D_MODEL), 0.02)
    w_rg = nrm(ks[15], (DEPTH, D_MODEL, N_GROUPS), D_MODEL ** -0.5)
    b_rg = nrm(ks[16], (DEPTH, N_GROUPS), 0.01)
    w_re = nrm(ks[17], (DEPTH, D_MODEL, N_EXPERTS), D_MODEL ** -0.5)
    b_re = nrm(ks[18], (DEPTH, N_EXPERTS), 0.01)
    w1 = nrm(ks[19], (DEPTH, N_EXPERTS, D_MODEL, D_EXPERT), D_MODEL ** -0.5)
    w3 = nrm(ks[20], (DEPTH, N_EXPERTS, D_MODEL, D_EXPERT), D_MODEL ** -0.5)
    w2 = nrm(ks[21], (DEPTH, N_EXPERTS, D_EXPERT, D_MODEL), D_EXPERT ** -0.5)
    norm_f_g = 1.0 + nrm(ks[22], (D_MODEL,), 0.02)
    return {"x": x, "c": c, "positions": positions, "w_ada": w_ada, "b_ada": b_ada,
            "norm1_g": norm1_g, "w_in": w_in, "b_gate": b_gate, "conv_w": conv_w,
            "conv_b": conv_b, "attn_out_g": attn_out_g, "mlstm_out_g": mlstm_out_g,
            "w_out": w_out, "norm2_g": norm2_g, "w_rg": w_rg, "b_rg": b_rg,
            "w_re": w_re, "b_re": b_re, "w1": w1, "w3": w3, "w2": w2, "norm_f_g": norm_f_g}

def first_block(x, c, positions, w_ada, b_ada, norm1_g, w_in, b_gate, conv_w, conv_b,
              attn_out_g, mlstm_out_g, w_out, norm2_g, w_rg, b_rg, w_re, b_re,
              w1, w3, w2, norm_f_g):
    b, s, d = x.shape
    offs = [D_ATT, 2 * D_ATT, 3 * D_ATT, 3 * D_ATT + 2 * D_MLSTM,
            3 * D_ATT + 3 * D_MLSTM, 3 * D_ATT + 4 * D_MLSTM]
    for l in range(DEPTH):
        mod = jax.nn.silu(c) @ w_ada[l] + b_ada[l]
        sh1, sc1, g1, sh2, sc2, g2 = jnp.split(mod, 6, axis=-1)

        h = modulate(x, norm1_g[l], sh1, sc1)
        proj = h @ w_in[l]
        q_a, k_a, v_a, qk_m, v_m, o_m, gates = jnp.split(proj, offs, axis=-1)

        qa = rope(split_heads(q_a, ATT_HEADS), positions)
        ka = rope(split_heads(k_a, ATT_HEADS), positions)
        attn = merge_heads(moba_attention(qa, ka, split_heads(v_a, ATT_HEADS)))
        attn = head_rms_norm(attn, attn_out_g[l], ATT_HEADS)

        qk_m = jax.nn.silu(causal_conv(qk_m, conv_w[l], conv_b[l]))
        q_m, k_m = jnp.split(qk_m, 2, axis=-1)
        gates = gates.astype(jnp.float32) + b_gate[l].astype(jnp.float32)
        i_pre = jnp.transpose(gates[..., :MLSTM_HEADS], (0, 2, 1))
        f_pre = jnp.transpose(gates[..., MLSTM_HEADS:], (0, 2, 1))
        hm = mlstm_chunkwise(split_heads(q_m, MLSTM_HEADS).astype(jnp.float32),
                             split_heads(k_m, MLSTM_HEADS).astype(jnp.float32) * MLSTM_HEAD_DIM ** -0.5,
                             split_heads(v_m, MLSTM_HEADS).astype(jnp.float32),
                             i_pre, f_pre)
        hm = head_rms_norm(merge_heads(hm), mlstm_out_g[l], MLSTM_HEADS)
        hm = (hm * jax.nn.sigmoid(o_m.astype(jnp.float32))).astype(x.dtype)

        y = jnp.concatenate([attn.astype(x.dtype), hm], axis=-1) @ w_out[l]
        x = x + g1[:, None, :] * y

        h2 = modulate(x, norm2_g[l], sh2, sc2)
        moe = hier_moe(h2.reshape(b * s, d), w_rg[l], b_rg[l], w_re[l], b_re[l],
                       w1[l], w3[l], w2[l]).reshape(b, s, d)
        x = x + g2[:, None, :] * moe
    return rms_norm(x, norm_f_g)


DEPTH_2 = 2

N_MEM = 256
EPS = 1e-6
SEQ_WIDTH = 2 * D_MODEL
XA_HEADS = 4
XA_HEAD_DIM = D_MODEL // XA_HEADS
XA_WIDTH = XA_HEADS * XA_HEAD_DIM
MIX_WIDTH = SEQ_WIDTH + XA_WIDTH
GLA_HEADS = 4
GLA_DK = (D_MODEL // 2) // GLA_HEADS
GLA_DV = SEQ_WIDTH // GLA_HEADS
GLA_RANK = 16
GLA_TAU = 16.0
GLA_CHUNK = 64
S5_GROUP = 16
S5_GROUPS = SEQ_WIDTH // S5_GROUP
S5_STATE = 64
S5_CHUNK = 128
S5_DT_MIN = 1e-3
S5_DT_MAX = 1e-1
GLA_IN = 2 * GLA_HEADS * GLA_DK + SEQ_WIDTH + GLA_RANK + MIX_WIDTH + XA_WIDTH
S5_IN = SEQ_WIDTH + MIX_WIDTH + XA_WIDTH
N_GLA = (DEPTH_2 + 1) // 2
N_S5 = DEPTH_2 // 2


def rms_norm_2(x, w):
    xf = x.astype(jnp.float32)
    y = xf * lax.rsqrt(jnp.mean(xf * xf, axis=-1, keepdims=True) + EPS)
    return (y * w.astype(jnp.float32)).astype(x.dtype)

def split_cols(t, sizes):
    idx = np.cumsum(sizes)[:-1].tolist()
    return jnp.split(t, idx, axis=-1)

def memory_attention(q, mem_n, w_kv):
    b_, l_, _ = q.shape
    k, v = jnp.split(mem_n @ w_kv, 2, axis=-1)
    qh = q.reshape(b_, l_, XA_HEADS, XA_HEAD_DIM)
    kh = k.reshape(b_, -1, XA_HEADS, XA_HEAD_DIM)
    vh = v.reshape(b_, -1, XA_HEADS, XA_HEAD_DIM)
    s = jnp.einsum('blhd,bmhd->bhlm', qh, kh).astype(jnp.float32) * (XA_HEAD_DIM ** -0.5)
    p = jax.nn.softmax(s, axis=-1).astype(v.dtype)
    o = jnp.einsum('bhlm,bmhd->blhd', p, vh)
    return o.reshape(b_, l_, XA_WIDTH)

def gla_chunked(q, k, v, g):
    b_, l_, h_, dk = q.shape
    dv = v.shape[-1]
    nc = l_ // GLA_CHUNK

    def to_chunks(t):
        return t.reshape(b_, nc, GLA_CHUNK, h_, t.shape[-1]).transpose(1, 0, 3, 2, 4)

    qc, kc, vc, gc = to_chunks(q), to_chunks(k), to_chunks(v), to_chunks(g)
    causal = jnp.tril(jnp.ones((GLA_CHUNK, GLA_CHUNK), dtype=bool))

    def step(state, inp):
        qi, ki, vi, gi = inp
        qf, kf, vf = qi.astype(jnp.float32), ki.astype(jnp.float32), vi.astype(jnp.float32)
        bcum = jnp.cumsum(gi.astype(jnp.float32), axis=-2)
        b_last = bcum[..., -1:, :]
        q_dec = qf * jnp.exp(bcum)
        k_inv = kf * jnp.exp(-bcum)
        k_end = kf * jnp.exp(b_last - bcum)
        att = jnp.where(causal, jnp.einsum('bhcd,bhsd->bhcs', q_dec, k_inv), 0.0)
        o = jnp.einsum('bhcs,bhse->bhce', att, vf) + jnp.einsum('bhcd,bhde->bhce', q_dec, state)
        state = jnp.exp(b_last[..., 0, :])[..., None] * state + jnp.einsum('bhcd,bhce->bhde', k_end, vf)
        return state, o.astype(v.dtype)

    s0 = jnp.zeros((b_, h_, dk, dv), jnp.float32)
    _, o = lax.scan(step, s0, (qc, kc, vc, gc))
    return o.transpose(1, 0, 3, 2, 4).reshape(b_, l_, h_, dv)

def gla_branch(h, w_in, w_gate_up, gate_bias, out_norm_w):
    b_, l_, _ = h.shape
    qk = GLA_HEADS * GLA_DK
    q, k, v, r, z, xq = split_cols(h @ w_in, [qk, qk, SEQ_WIDTH, GLA_RANK, MIX_WIDTH, XA_WIDTH])
    g = jax.nn.log_sigmoid((r @ w_gate_up + gate_bias).astype(jnp.float32)) / GLA_TAU
    o = gla_chunked(q.reshape(b_, l_, GLA_HEADS, GLA_DK) * (GLA_DK ** -0.5),
                    k.reshape(b_, l_, GLA_HEADS, GLA_DK),
                    v.reshape(b_, l_, GLA_HEADS, GLA_DV),
                    g.reshape(b_, l_, GLA_HEADS, GLA_DK))
    o = rms_norm_2(o, out_norm_w).reshape(b_, l_, SEQ_WIDTH)
    return o.astype(h.dtype), z, xq

def s5_discretize(lam_re, lam_im, log_step, b_re, b_im):
    lam_re = lam_re.astype(jnp.float32)
    lam_im = lam_im.astype(jnp.float32)
    dt = jnp.exp(log_step.astype(jnp.float32))[:, None]
    mag = jnp.exp(lam_re * dt)
    ab_re = mag * jnp.cos(lam_im * dt)
    ab_im = mag * jnp.sin(lam_im * dt)
    den = lam_re * lam_re + lam_im * lam_im
    nr, ni = ab_re - 1.0, ab_im
    coef_re = ((nr * lam_re + ni * lam_im) / den)[..., None]
    coef_im = ((ni * lam_re - nr * lam_im) / den)[..., None]
    br, bi = b_re.astype(jnp.float32), b_im.astype(jnp.float32)
    bb_re = coef_re * br - coef_im * bi
    bb_im = coef_re * bi + coef_im * br
    return ab_re, ab_im, bb_re, bb_im

def _linrec_combine(e1, e2):
    a1r, a1i, x1r, x1i = e1
    a2r, a2i, x2r, x2i = e2
    return (a1r * a2r - a1i * a2i,
            a1r * a2i + a1i * a2r,
            a2r * x1r - a2i * x1i + x2r,
            a2r * x1i + a2i * x1r + x2i)

def s5_chunked(u, ab_re, ab_im, bb_re, bb_im, c_re, c_im):
    b_, l_, g_, hg = u.shape
    nc = l_ // S5_CHUNK
    uc = u.reshape(b_, nc, S5_CHUNK, g_, hg).transpose(1, 0, 2, 3, 4)

    def step(carry, u_i):
        cr, ci = carry
        bu_re = jnp.einsum('bcgh,gph->bcgp', u_i, bb_re)
        bu_im = jnp.einsum('bcgh,gph->bcgp', u_i, bb_im)
        a_r = jnp.broadcast_to(ab_re, bu_re.shape)
        a_i = jnp.broadcast_to(ab_im, bu_im.shape)
        acum_r, acum_i, x_r, x_i = lax.associative_scan(_linrec_combine, (a_r, a_i, bu_re, bu_im), axis=1)
        x_r = x_r + acum_r * cr[:, None] - acum_i * ci[:, None]
        x_i = x_i + acum_r * ci[:, None] + acum_i * cr[:, None]
        y = jnp.einsum('bcgp,ghp->bcgh', x_r, c_re) - jnp.einsum('bcgp,ghp->bcgh', x_i, c_im)
        return (x_r[:, -1], x_i[:, -1]), y

    zeros = jnp.zeros((b_, g_, S5_STATE), jnp.float32)
    _, y = lax.scan(step, (zeros, zeros), uc)
    return y.transpose(1, 0, 2, 3, 4).reshape(b_, l_, g_, hg)

def s5_branch(h, w_in, lam_re, lam_im, log_step, b_re, b_im, c_re, c_im, d, w_glu, b_glu):
    b_, l_, _ = h.shape
    u, z, xq = split_cols(h @ w_in, [SEQ_WIDTH, MIX_WIDTH, XA_WIDTH])
    ab_re, ab_im, bb_re, bb_im = s5_discretize(lam_re, lam_im, log_step, b_re, b_im)
    uf = u.astype(jnp.float32)
    y = s5_chunked(uf.reshape(b_, l_, S5_GROUPS, S5_GROUP), ab_re, ab_im, bb_re, bb_im,
                   c_re.astype(jnp.float32), c_im.astype(jnp.float32))
    y = y.reshape(b_, l_, SEQ_WIDTH) + d.astype(jnp.float32) * uf
    y = jax.nn.gelu(y).astype(h.dtype)
    y = y * jax.nn.sigmoid(y @ w_glu + b_glu)
    return y, z, xq

def second_inputs(seed: int = 0) -> dict:
    key = jax.random.key(seed)
    ks = jax.random.split(key, 24)
    nrm = jax.random.normal
    inv = lambda n: 1.0 / math.sqrt(n)
    n_idx = jnp.arange(S5_STATE, dtype=jnp.float32)
    lam_re = -0.5 * jnp.exp(0.02 * nrm(ks[8], (N_S5, S5_GROUPS, S5_STATE), jnp.float32))
    lam_im = jnp.broadcast_to(math.pi * n_idx, (N_S5, S5_GROUPS, S5_STATE)).astype(jnp.float32)
    log_step = jax.random.uniform(ks[9], (N_S5, S5_GROUPS), jnp.float32,
                                  math.log(S5_DT_MIN), math.log(S5_DT_MAX))
    return {
        "x": nrm(ks[0], (BATCH, SEQ, D_MODEL), jnp.float32),
        "mem": nrm(ks[1], (BATCH, N_MEM, D_MODEL), jnp.float32),
        "norm_w": 1.0 + 0.02 * nrm(ks[2], (DEPTH_2, D_MODEL), jnp.float32),
        "mem_norm_w": 1.0 + 0.02 * nrm(ks[3], (D_MODEL,), jnp.float32),
        "gla_w_in": nrm(ks[4], (N_GLA, D_MODEL, GLA_IN), jnp.float32) * inv(D_MODEL),
        "gla_w_gate_up": nrm(ks[5], (N_GLA, GLA_RANK, GLA_HEADS * GLA_DK), jnp.float32) * inv(GLA_RANK),
        "gla_gate_bias": 0.1 * nrm(ks[6], (N_GLA, GLA_HEADS * GLA_DK), jnp.float32),
        "gla_out_norm_w": 1.0 + 0.02 * nrm(ks[7], (N_GLA, GLA_DV), jnp.float32),
        "s5_w_in": nrm(ks[10], (N_S5, D_MODEL, S5_IN), jnp.float32) * inv(D_MODEL),
        "s5_lam_re": lam_re,
        "s5_lam_im": lam_im,
        "s5_log_step": log_step,
        "s5_b_re": nrm(ks[11], (N_S5, S5_GROUPS, S5_STATE, S5_GROUP), jnp.float32) * inv(2 * S5_GROUP),
        "s5_b_im": nrm(ks[12], (N_S5, S5_GROUPS, S5_STATE, S5_GROUP), jnp.float32) * inv(2 * S5_GROUP),
        "s5_c_re": 0.5 * nrm(ks[13], (N_S5, S5_GROUPS, S5_GROUP, S5_STATE), jnp.float32),
        "s5_c_im": 0.5 * nrm(ks[14], (N_S5, S5_GROUPS, S5_GROUP, S5_STATE), jnp.float32),
        "s5_d": nrm(ks[15], (N_S5, SEQ_WIDTH), jnp.float32),
        "s5_w_glu": nrm(ks[16], (N_S5, SEQ_WIDTH, SEQ_WIDTH), jnp.float32) * inv(SEQ_WIDTH),
        "s5_b_glu": 0.01 * nrm(ks[17], (N_S5, SEQ_WIDTH), jnp.float32),
        "xa_w_kv": nrm(ks[18], (DEPTH_2, D_MODEL, 2 * XA_WIDTH), jnp.float32) * inv(D_MODEL),
        "w_out": nrm(ks[19], (DEPTH_2, MIX_WIDTH, D_MODEL), jnp.float32) * inv(MIX_WIDTH),
        "final_norm_w": 1.0 + 0.02 * nrm(ks[20], (D_MODEL,), jnp.float32),
    }

def second_block(x, mem, norm_w, mem_norm_w, gla_w_in, gla_w_gate_up, gla_gate_bias, gla_out_norm_w,
              s5_w_in, s5_lam_re, s5_lam_im, s5_log_step, s5_b_re, s5_b_im, s5_c_re, s5_c_im,
              s5_d, s5_w_glu, s5_b_glu, xa_w_kv, w_out, final_norm_w):
    mem_n = rms_norm_2(mem, mem_norm_w)
    for i in range(DEPTH_2):
        h = rms_norm_2(x, norm_w[i])
        j = i // 2
        if i % 2 == 0:
            seq_out, z, xq = gla_branch(h, gla_w_in[j], gla_w_gate_up[j], gla_gate_bias[j], gla_out_norm_w[j])
        else:
            seq_out, z, xq = s5_branch(h, s5_w_in[j], s5_lam_re[j], s5_lam_im[j], s5_log_step[j],
                                       s5_b_re[j], s5_b_im[j], s5_c_re[j], s5_c_im[j],
                                       s5_d[j], s5_w_glu[j], s5_b_glu[j])
        xa = memory_attention(xq, mem_n, xa_w_kv[i])
        y = jnp.concatenate([seq_out.astype(x.dtype), xa.astype(x.dtype)], axis=-1) * jax.nn.silu(z)
        x = x + y @ w_out[i]
    return rms_norm_2(x, final_norm_w)


def setup_inputs(seed=0):
    out = dict(first_inputs(seed))
    for name, value in second_inputs(seed + 1).items():
        if name != "x":
            out[name + "_2"] = value
    return out


def reference(
    x, c, positions, w_ada, b_ada, norm1_g, w_in, b_gate, conv_w, conv_b, attn_out_g,
    mlstm_out_g, w_out, norm2_g, w_rg, b_rg, w_re, b_re, w1, w3, w2, norm_f_g, mem_2, norm_w_2,
    mem_norm_w_2, gla_w_in_2, gla_w_gate_up_2, gla_gate_bias_2, gla_out_norm_w_2, s5_w_in_2,
    s5_lam_re_2, s5_lam_im_2, s5_log_step_2, s5_b_re_2, s5_b_im_2, s5_c_re_2, s5_c_im_2, s5_d_2,
    s5_w_glu_2, s5_b_glu_2, xa_w_kv_2, w_out_2, final_norm_w_2,
):
    x = first_block(
        x, c, positions, w_ada, b_ada, norm1_g, w_in, b_gate, conv_w, conv_b, attn_out_g,
        mlstm_out_g, w_out, norm2_g, w_rg, b_rg, w_re, b_re, w1, w3, w2, norm_f_g,
    )
    return second_block(
        x, mem_2, norm_w_2, mem_norm_w_2, gla_w_in_2, gla_w_gate_up_2, gla_gate_bias_2,
        gla_out_norm_w_2, s5_w_in_2, s5_lam_re_2, s5_lam_im_2, s5_log_step_2, s5_b_re_2,
        s5_b_im_2, s5_c_re_2, s5_c_im_2, s5_d_2, s5_w_glu_2, s5_b_glu_2, xa_w_kv_2, w_out_2,
        final_norm_w_2,
    )


_drawn_inputs = setup_inputs


def setup_inputs(seed=0):
    import zlib

    import numpy as np

    out = dict(_drawn_inputs(seed))
    spreads = {}
    factors = {'norm1_g': 5.428,
     'conv_b': 8.0,
     'attn_out_g': 7.101,
     'mlstm_out_g': 8.0,
     'norm2_g': 3.912,
     'b_rg': 8.0,
     'b_re': 7.808,
     'norm_w_2': 3.109,
     'mem_norm_w_2': 8.0,
     'gla_gate_bias_2': 2.916,
     'gla_out_norm_w_2': 6.811,
     's5_lam_re_2': 200.0,
     's5_b_glu_2': 64.0,
     'final_norm_w_2': 22.489,
     's5_lam_im_2': 25.304,
     's5_log_step_2': 27.68,
     's5_b_re_2': 35.664,
     's5_b_im_2': 35.544,
     's5_c_re_2': 35.08,
     's5_c_im_2': 35.136}
    for name, (base, spread) in spreads.items():
        noise = np.random.default_rng([zlib.crc32(name.encode()), seed]).standard_normal(out[name].shape)
        drawn = base * np.exp(spread * noise) if base else spread * noise
        out[name] = jnp.asarray(drawn.astype(out[name].dtype))
    for name, factor in factors.items():
        out[name] = (out[name] * factor).astype(out[name].dtype)
    return out
```

```python
from contextlib import ExitStack

import numpy as np
import concourse.bass as bass
from concourse import mybir

F32 = mybir.dt.float32
I32 = mybir.dt.int32
U32 = mybir.dt.uint32
ALU = mybir.AluOpType
ACT = mybir.ActivationFunctionType
AX = mybir.AxisListType.X

P = 128
TOK = 256
TT = TOK // P
D = 1024
KD = D // P
EPS = 1e-6
NEG = -1e30
RING = 3
TILE = 4096
PI = 3.1415925
TWO_PI = 2.0 * np.pi
TWO_PI_A = 6.28125
TWO_PI_B = float(np.float32(int((TWO_PI - TWO_PI_A) * 2 ** 21) / 2 ** 21))
TWO_PI_C = float(np.float32(TWO_PI - TWO_PI_A - TWO_PI_B))
ROUND = 12582912.0

N_ADA, N_IN, N_OUT, N_EXP = 12, 7, 2, 32
T_ADA = 0
T_IN = T_ADA + N_ADA
T_OUT = T_IN + N_IN
T_MOE = T_OUT + N_OUT
T_GLA = T_MOE + 3 * N_EXP
T_GLA_OUT = T_GLA + 18
T_S5 = T_GLA_OUT + 6
T_GLU = T_S5 + 16
T_S5_OUT = T_GLU + 8
T_END = T_S5_OUT + 6

CONSTS = {}
_at = 0
for _name, _n in (("ident", 128), ("causal", 512), ("causal_t", 128), ("inv_freq", 32), ("iota32", 32),
                  ("one_hot4", 512), ("chunk_tri", 128), ("chunk_suffix", 128), ("chunk_ind", 2),
                  ("iota256", 256), ("minus_half", 16)):
    CONSTS[_name] = (_at, _at + _n)
    _at += _n
N_CONST = _at

COLS = {}
_at = 0
for _name, _n in (("c", 8), ("b_ada", 32), ("norm1_g", 8), ("norm2_g", 8), ("conv_w", 32), ("conv_b", 8),
                  ("norm_w_2", 16), ("mem_norm_w", 8), ("s5_d", 16), ("s5_b_glu", 16), ("b_gate", 2)):
    COLS[_name] = (_at, _at + _n)
    _at += _n
N_COLS = _at

ROWS = {}
_at = 0
for _name, _n in (("b_g1", 1024), ("b_g2", 1024), ("attn_out_g", 512), ("mlstm_out_g", 512), ("norm_f_g", 1024),
                  ("b_router", 36), ("gla_bias", 512), ("gla_out_g", 512), ("final_norm", 1024)):
    ROWS[_name] = (_at, _at + _n)
    _at += _n
N_ROWS = _at


class Core:

    def __init__(self, nc, ctx, dram):
        self.nc, self.ctx, self.dram = nc, ctx, dram
        self.ring = self.sb("ring", [P, RING, TILE])
        self.const = self.sb("const", [P, N_CONST])
        self.cols = self.sb("cols", [P, N_COLS])
        self.rows = self.sb("rows", [P, N_ROWS])
        self.x = self.sb("x", [P, TT, D])
        self.hT = self.sb("hT", [P, KD, TOK])
        self.memT = self.sb("memT", [P, KD, TOK])
        self.small = self.sb("small", [P, 64])
        self.sin = self.sb("sin", [P, TT, 32])
        self.cos = self.sb("cos", [P, TT, 32])
        self.mod = self.sb("mod", [P, 32])
        self.ps = ctx.enter_context(nc.psum_tensor("ps", [P, 8, 512], F32))
        self.stage_sems = None
        self.landed = [self.sem(f"weights_landed_{j}") for j in range(RING)]
        self.tile_done = self.sem("tile_done")
        self.stage_sems = []

    def sb(self, name, shape, dt=F32, ctx=None):
        return (ctx or self.ctx).enter_context(self.nc.sbuf_tensor(name, shape, dt))

    def sem(self, name):
        if self.stage_sems is None:
            return self.ctx.enter_context(self.nc.semaphore(name))
        self.stage_sems.append(self.nc.alloc_semaphore(name))
        return self.stage_sems[-1]

    def clear_stage_sems(self):
        self.nc.clear_and_free_semaphores(self.stage_sems)
        self.nc.all_engine_barrier()
        self.stage_sems = []

    def c(self, name):
        a, b = CONSTS[name]
        return self.const[:, a:b]

    def col(self, name, i=0, n=1):
        a = COLS[name][0] + i
        return self.cols[:, a:a + n]

    def row(self, name):
        a, b = ROWS[name]
        return self.rows[:, a:b]

    def slot(self, n, k=8):
        return self.ring[:, n % RING, :].rearrange("p (k n) -> p k n", k=k)

    def wait_tile(self, pe, n):
        pe.wait_ge(self.landed[n % RING], 16 * (n // RING + 1))


def bc(ap, axis, n):
    ap = ap.unsqueeze(axis)
    shape = list(ap.shape)
    shape[axis] = n
    return ap.broadcast_to(shape)


def stream(k, sp, used_from, used_to):
    n0, n1 = max(used_from, 1) + RING - 1 if used_from else RING, min(used_to + RING, T_END)
    n0 = used_from + RING

    def load(n, j):
        sp.wait_ge(k.tile_done, n - (RING - 1))
        sp.dma_start(k.ring[:, j, :], k.dram["weights"][n]).then_inc(k.landed[j], 16)

    body = (n1 - n0) // RING
    if body > 1:
        with sp.Fori(0, body) as i:
            for j in range(RING):
                sp.wait_ge(k.tile_done, i * RING + (n0 + j - (RING - 1)))
                sp.dma_start(k.ring[:, (n0 + j) % RING, :],
                             k.dram["weights"][bass.ds(i * RING + (n0 + j), 1)].rearrange("a p n -> (a p) n")
                             ).then_inc(k.landed[(n0 + j) % RING], 16)
        n0 += body * RING
    for n in range(n0, n1):
        load(n, n % RING)


def tm_tile(k, pe, n, lhs, out, k0=0):
    k.wait_tile(pe, n)
    w = k.slot(n)
    for t in range(TT):
        for kk in range(KD):
            last = pe.matmul(out[:, t, :], lhs[:, k0 + kk, t * P:(t + 1) * P], w[:, kk, :],
                             start=(kk == 0), stop=(kk == KD - 1))
    last.then_inc(k.tile_done, 1)


def fm_tile(k, pe, n, rhs, out, k0=0):
    k.wait_tile(pe, n)
    w = k.slot(n)
    for f in range(4):
        for kk in range(KD):
            last = pe.matmul(out[:, f, :], w[:, kk, f * P:(f + 1) * P], rhs[:, k0 + kk, :],
                             start=(kk == 0), stop=(kk == KD - 1))
    last.then_inc(k.tile_done, 1)


def pair(k, m):
    j = m % 3
    return k.ps[:, 2 * j:2 * j + 2, :]


def pair_fm(k, m):
    return pair(k, m).rearrange("p b (f t) -> p (b f) t", f=2)


class NormT:

    def __init__(self, k, name, x, ctx, xn):
        self.k, self.x, self.xn = k, x, xn
        self.ss = k.sb(f"{name}_ss", [P, TT], ctx=ctx)
        self.rstd = k.sb(f"{name}_rstd", [P, TT], ctx=ctx)
        self.summed = k.sem(f"{name}_squares_summed")
        self.rstd_ready = k.sem(f"{name}_rstd_ready")
        self.scaled = k.sem(f"{name}_scaled")
        self.turned = k.sem(f"{name}_turned")
        self.done = k.sem(f"{name}_done")

    def act(self, act):
        for t in range(TT):
            act.activation(self.xn[:, t, :], self.x[:, t, :], ACT.Square,
                           accum_out=self.ss[:, t:t + 1]).then_inc(self.summed, 1)

    def pool(self, pool):
        pool.wait_ge(self.summed, TT)
        rsqrt_mean(self.k, pool, self.rstd[:], self.ss[:], D).then_inc(self.rstd_ready, 1)

    def dve_scale(self, dve):
        dve.wait_ge(self.rstd_ready, 1)
        for t in range(TT):
            dve.tensor_scalar(self.xn[:, t, :], self.x[:, t, :], self.rstd[:, t:t + 1], None,
                              ALU.mult).then_inc(self.scaled, 1)

    def pe(self, pe):
        pe.wait_ge(self.scaled, TT)
        turn(self.k, pe, self.xn, KD, self.k.ps[:, 0:4, :].rearrange("p b (f t) -> p (b f) t", f=2), self.turned)

    def dve_out(self, dve, out, scale, shift=None):
        dve.wait_ge(self.turned, KD)
        src = self.k.ps[:, 0:4, :].rearrange("p b (f t) -> p (b f) t", f=2)
        for f in range(KD):
            dve.tensor_scalar(out[:, f, :], src[:, f, :], scale[:, f:f + 1],
                              None if shift is None else shift[:, f:f + 1], ALU.mult,
                              *(() if shift is None else (ALU.add,))).then_inc(self.done, 1)


def rsqrt_mean(k, pool, out, ss, width, eps=EPS):
    pool.tensor_scalar(out, ss, 1.0 / width, eps, ALU.mult, ALU.add)
    pool.drain()
    n = out.shape[-1]
    return pool.tensor_tensor(out=out, in0=out, in1=k.c("minus_half")[:, 0:n], op=ALU.pow)


def turn(k, pe, src, nf, dst, turned):
    for f in range(nf):
        for t in range(TT):
            last = pe.transpose(dst[:, f, t * P:(t + 1) * P], src[:, t, f * P:(f + 1) * P], k.c("ident"))
        last.then_inc(turned, 1)


def range_reduce(dve, r, n, ang):
    dve.tensor_scalar(n, ang, 1.0 / TWO_PI, ROUND, ALU.mult, ALU.add)
    dve.drain()
    dve.tensor_scalar(n, n, -ROUND, None, ALU.add)
    dve.drain()
    dve.scalar_tensor_tensor(out=r, in0=n, scalar=-TWO_PI_A, in1=ang, op0=ALU.mult, op1=ALU.add)
    dve.drain()
    dve.scalar_tensor_tensor(out=r, in0=n, scalar=-TWO_PI_B, in1=r, op0=ALU.mult, op1=ALU.add)
    dve.drain()
    dve.scalar_tensor_tensor(out=r, in0=n, scalar=-TWO_PI_C, in1=r, op0=ALU.mult, op1=ALU.add)
    dve.drain()
    return dve.tensor_scalar(r, r, PI, -PI, ALU.min, ALU.max)


def quarter_turn(dve, r, n, angle):
    dve.tensor_scalar(n, angle, PI / 2, -TWO_PI, ALU.is_gt, ALU.mult)
    dve.tensor_scalar(r, angle, float(np.pi / 2), None, ALU.add)
    dve.drain()
    dve.tensor_tensor(r, r, n, ALU.add)
    dve.drain()
    return dve.tensor_scalar(r, r, PI, -PI, ALU.min, ALU.max)


def stage_modulation(k):
    nc, d = k.nc, k.dram
    with ExitStack() as ctx:
        csil = k.sb("csil", [P, KD], ctx=ctx)
        cexp = k.sb("cexp", [P, KD], ctx=ctx)
        crep = k.sb("crep", [P, KD, P], ctx=ctx)
        pos = k.sb("pos", [P, TT], I32, ctx=ctx)
        posf = k.sb("posf", [P, TT], ctx=ctx)
        ang = k.sb("ang", [P, TT, 32], ctx=ctx)
        red = k.sb("red", [P, TT, 32], ctx=ctx)
        redc = k.sb("redc", [P, TT, 32], ctx=ctx)
        turns = k.sb("turns", [P, TT, 32], ctx=ctx)
        mem = k.sb("mem", [P, TT, D], ctx=ctx)
        xn = k.sb("xn0", [P, TT, D], ctx=ctx)
        memn = k.sb("memn", [P, TT, D], ctx=ctx)
        norm_m = NormT(k, "mem_norm", mem, ctx, memn)
        norm_x = NormT(k, "norm1", k.x, ctx, xn)
        small_in, rows_in, x_in, mem_in, pos_in = (k.sem(s) for s in ("small_in", "rows_in", "x_in", "mem_in", "pos_in"))
        cexp_ready, csil_ready, row_out, angles_ready, tables_ready, cols_done = (
            k.sem(s) for s in ("cexp_ready", "csil_ready", "gate_rows_out", "angles_ready", "tables_ready", "cols_done"))
        mod_ps, row_ps = k.ps[:, 6, :], k.ps[:, 4:6, :]

        with nc.Block() as block:
            @block.sync
            def _(sp):
                sp.dma_start(k.cols[:], d["cols"]).then_inc(small_in, 16)
                sp.dma_start(k.const[:], d["consts"]).then_inc(small_in, 16)
                for n in range(RING):
                    sp.dma_start(k.ring[:, n, :], d["weights"][n]).then_inc(k.landed[n], 16)
                sp.dma_start(pos[:], d["positions"]).then_inc(pos_in, 16)
                sp.dma_start(mem[:], d["mem"]).then_inc(mem_in, 16)
                sp.dma_start(k.x[:], d["x"]).then_inc(x_in, 16)
                sp.dma_start(k.rows[:], d["rows"].partition_broadcast(P)).then_inc(rows_in, 16)
                stream(k, sp, T_ADA, T_ADA + N_ADA)

            @block.scalar
            def _(act):
                act.wait_ge(small_in, 32)
                act.activation(cexp[:], k.col("c", 0, KD), ACT.Exp, scale=-1.0).then_inc(cexp_ready, 1)
                act.wait_ge(mem_in, 16)
                norm_m.act(act)
                act.wait_ge(x_in, 16)
                norm_x.act(act)
                act.wait_ge(angles_ready, 2)
                act.activation(k.sin[:], red[:], ACT.Sin).then_inc(tables_ready, 1)
                act.activation(k.cos[:], redc[:], ACT.Sin).then_inc(tables_ready, 1)

            @block.gpsimd
            def _(pool):
                norm_m.pool(pool)
                norm_x.pool(pool)

            @block.vector
            def _(dve):
                dve.wait_ge(cexp_ready, 1)
                dve.tensor_scalar(cexp[:], cexp[:], 1.0, None, ALU.add)
                dve.drain()
                dve.reciprocal(cexp[:], cexp[:])
                dve.drain()
                dve.tensor_tensor(csil[:], cexp[:], k.col("c", 0, KD), ALU.mult)
                dve.drain()
                dve.tensor_copy(crep[:], bc(csil[:], 2, P)).then_inc(csil_ready, 1)
                dve.sem_inc(row_out, 1)
                dve.wait_ge(pos_in, 16)
                dve.tensor_copy(posf[:], pos[:])
                dve.drain()
                for t in range(TT):
                    dve.tensor_scalar(ang[:, t, :], k.c("inv_freq"), posf[:, t:t + 1], None, ALU.mult)
                dve.drain()
                range_reduce(dve, red[:], turns[:], ang[:]).then_inc(angles_ready, 1)
                dve.drain()
                quarter_turn(dve, redc[:], turns[:], red[:]).then_inc(angles_ready, 1)
                norm_m.dve_scale(dve)
                norm_x.dve_scale(dve)
                dve.wait_ge(rows_in, 16)
                for half, gate in enumerate(("b_g1", "b_g2")):
                    for j in range(2):
                        dve.wait_ge(k.tile_done, 6 * half + 5 + j)
                        g = k.row(gate)[:, j * 512:(j + 1) * 512]
                        last = dve.tensor_tensor(g, row_ps[:, j, :], g, ALU.add)
                    last.then_inc(row_out, 1)
                dve.tensor_tensor(k.mod[:], mod_ps[:, 0:32], k.col("b_ada", 0, 32), ALU.add)
                dve.drain()
                for i, g in ((8, "norm1_g"), (24, "norm2_g")):
                    dve.scalar_tensor_tensor(out=k.mod[:, i:i + 8], in0=k.mod[:, i:i + 8], scalar=1.0,
                                             in1=k.col(g, 0, 8), op0=ALU.add, op1=ALU.mult)
                dve.drain()
                norm_m.dve_out(dve, k.memT, k.col("mem_norm_w", 0, KD))
                norm_x.dve_out(dve, k.hT, k.mod[:, 8:16], k.mod[:, 0:8])

            @block.tensor
            def _(pe):
                pe.wait_ge(csil_ready, 1)
                with pe.Fori(0, 2) as half:
                    for j in range(6):
                        slot = j % RING
                        pe.wait_ge(k.landed[slot], half * 32 + 16 * (j // RING + 1))
                        w = k.ring[:, slot, :].rearrange("p (k n) -> p k n", k=KD)
                        if j == 4:
                            pe.wait_ge(row_out, half + 1)
                        if j < 4:
                            for f in range(4):
                                for kk in range(KD):
                                    last = pe.matmul(mod_ps[:, bass.ds(half * 16 + (4 * j + f), 1)],
                                                     w[:, kk, f * P:(f + 1) * P], csil[:, kk:kk + 1],
                                                     start=(kk == 0), stop=(kk == KD - 1))
                        else:
                            for kk in range(KD):
                                last = pe.matmul(row_ps[:, j - 4, :], crep[:, kk, :], w[:, kk, :],
                                                 start=(kk == 0), stop=(kk == KD - 1))
                        last.then_inc(k.tile_done, 1)
                norm_m.pe(pe)
                pe.wait_ge(norm_m.done, KD)
                norm_x.pe(pe)


def stage_in_projection(k, a):
    nc = k.nc
    evac = k.sem("in_proj_out")
    gates_done = k.sem("gates_done")
    wg_in = k.sem("w_gate_in")
    with nc.Block() as block:
        @block.sync
        def _(sp):
            sp.dma_start(a["w_gate"][:], k.dram["w_gate"]).then_inc(wg_in, 16)
            stream(k, sp, T_IN, T_IN + N_IN)

        @block.tensor
        def _(pe):
            for m in range(N_IN):
                if m >= 3:
                    pe.wait_ge(evac, m - 2)
                if m in (3, 4):
                    fm_tile(k, pe, T_IN + m, k.hT, pair_fm(k, m))
                else:
                    tm_tile(k, pe, T_IN + m, k.hT, pair(k, m))
            pe.wait_ge(wg_in, 16)
            for g in range(2):
                for kk in range(KD):
                    last = pe.matmul(k.ps[0:4, 6 + g, 0:TOK], a["w_gate"][:, kk, 4 * g:4 * g + 4], k.hT[:, kk, :],
                                     start=(kk == 0), stop=(kk == KD - 1))
            last.then_inc(gates_done, 1)

        @block.vector
        def _(dve):
            dve.memset(a["v_aug"][:], 1.0)
            dve.memset(a["qk_mT"][:, :, 0:3], 0.0)
            dve.drain()
            for m in range(N_IN):
                dve.wait_ge(k.tile_done, T_IN + m + 1)
                if m < 3:
                    ins = dve.tensor_copy(a["qkv"][:, :, m * 512:(m + 1) * 512], pair(k, m))
                elif m < 5:
                    ins = dve.tensor_copy(a["qk_mT"][:, 4 * (m - 3):4 * (m - 3) + 4, 3:3 + TOK], pair_fm(k, m))
                elif m == 5:
                    for t in range(TT):
                        ins = dve.tensor_copy(a["v_aug"][:, t, :, 0:128],
                                              pair(k, m)[:, t, :].rearrange("p (h e) -> p h e", h=4))
                else:
                    ins = dve.tensor_copy(a["o_m"][:], pair(k, m))
                ins.then_inc(evac, 1)
            dve.wait_ge(gates_done, 1)
            for g in range(2):
                dve.tensor_scalar(a["gate_rows"][0:4, g, :], k.ps[0:4, 6 + g, 0:TOK], k.col("b_gate", g)[0:4], None, ALU.add)


def stage_attention(k, a):
    nc = k.nc
    with ExitStack() as ctx:
        rot = k.sb("rot", [P, TT, D], ctx=ctx)
        swp = k.sb("swp", [P, 16, 2, 32], ctx=ctx)
        qkT = k.sb("qkT", [P, KD, TOK], ctx=ctx)
        scores = k.sb("scores", [P, 2, 2, TT, TOK], ctx=ctx)
        pT = k.sb("pT", [P, 2, 2, TT, TOK], ctx=ctx)
        mx = k.sb("mx", [P, 4, 4], ctx=ctx)
        rs = k.sb("rs", [P, 4, 4], ctx=ctx)
        rotated, turned, qkT_ready, scored, masked, expd, p_turned, pT_ready, pv_done = (
            k.sem(s) for s in ("qk_rotated", "qk_turned", "qkT_ready", "scored", "masked", "exp_done", "p_turned",
                               "pT_ready", "pv_done"))
        spair = [k.ps[:, 0:2, :], k.ps[:, 2:4, :]]
        tps = k.ps[:, 4:6, :].rearrange("p h (kt q) -> p h kt q", kt=2)
        ops = k.ps[:, 6:8, :].rearrange("p b (g t e) -> p (b g) t e", t=TT, e=64)
        with nc.Block() as block:
            @block.vector
            def _(dve):
                for t in range(TT):
                    src = a["qkv"][:, t, 0:1024].rearrange("p (h g e) -> p h g e", g=2, e=32)
                    dst = rot[:, t, :].rearrange("p (h g e) -> p h g e", g=2, e=32)
                    cos, sin = k.cos[:, t, :], k.sin[:, t, :]
                    for g in range(2):
                        dve.tensor_tensor(dst[:, :, g, :], src[:, :, g, :], bc(cos, 1, 16), ALU.mult)
                        dve.tensor_tensor(swp[:, :, g, :], src[:, :, 1 - g, :], bc(sin, 1, 16), ALU.mult)
                    dve.drain()
                    dve.tensor_tensor(dst[:, :, 0, :], dst[:, :, 0, :], swp[:, :, 0, :], ALU.subtract)
                    dve.tensor_tensor(dst[:, :, 1, :], dst[:, :, 1, :], swp[:, :, 1, :], ALU.add).then_inc(rotated, 1)
                    dve.drain()
                dve.wait_ge(turned, KD)
                dve.tensor_copy(qkT[:, :, :], k.ps[:, 0:4, :].rearrange("p b (f t) -> p (b f) t", f=2)).then_inc(qkT_ready, 1)

                def mask(hp):
                    dve.wait_ge(scored, hp + 1)
                    for h in range(2):
                        dve.scalar_tensor_tensor(out=scores[:, hp % 2, h], scalar=0.125, op0=ALU.mult, op1=ALU.add,
                                                 in0=spair[hp % 2][:, h, :].rearrange("p (t q) -> p t q", t=TT),
                                                 in1=k.c("causal").rearrange("p (t q) -> p t q", t=TT))
                    dve.drain()
                    dve.tensor_reduce(mx[:, hp, :], scores[:, hp % 2].rearrange("p h t q -> p (h t) q"), AX, ALU.max)
                    dve.drain()
                    dve.tensor_scalar(mx[:, hp, :], mx[:, hp, :], -1.0, None, ALU.mult).then_inc(masked, 1)

                for hp in range(4):
                    if hp == 0:
                        mask(0)
                    dve.wait_ge(p_turned, hp + 1)
                    if hp >= 2:
                        dve.wait_ge(pv_done, hp - 1)
                    dve.tensor_copy(pT[:, hp % 2], tps[:]).then_inc(pT_ready, 1)
                    if hp < 3:
                        mask(hp + 1)
                dve.reciprocal(rs[:], rs[:])
                dve.drain()
                dve.wait_ge(pv_done, 4)
                dst = a["mix"][:, :, 0:512].rearrange("p t (h e) -> p h t e", e=64)
                r = rs[:].rearrange("p a (h t) -> p (a h) t", h=2)
                for t in range(TT):
                    dve.tensor_tensor(dst[:, :, t, :], ops[:, :, t, :], bc(r[:, :, t], 2, 64), ALU.mult)

            @block.scalar
            def _(act):
                for hp in range(4):
                    act.wait_ge(masked, hp + 1)
                    if hp >= 2:
                        act.wait_ge(p_turned, hp - 1)
                    for h in range(2):
                        for t in range(TT):
                            i = 2 * h + t
                            last = act.activation(scores[:, hp % 2, h, t, :], scores[:, hp % 2, h, t, :], ACT.Exp,
                                                  bias=mx[:, hp, i:i + 1], accum_out=rs[:, hp, i:i + 1])
                    last.then_inc(expd, 1)

            @block.tensor
            def _(pe):
                pe.wait_ge(rotated, TT)
                turn(k, pe, rot, KD, k.ps[:, 0:4, :].rearrange("p b (f t) -> p (b f) t", f=2), turned)
                pe.wait_ge(qkT_ready, 1)

                def score(hp):
                    if hp >= 2:
                        pe.wait_ge(masked, hp - 1)
                    for h in range(2):
                        r = slice(64 * h, 64 * h + 64)
                        for t in range(TT):
                            last = pe.matmul(spair[hp % 2][:, h, t * TOK:(t + 1) * TOK], qkT[r, hp, t * P:(t + 1) * P],
                                             qkT[r, 4 + hp, :], start=True, stop=True)
                    last.then_inc(scored, 1)

                score(0)
                for hp in range(4):
                    if hp < 3:
                        score(hp + 1)
                    pe.wait_ge(expd, hp + 1)
                    if hp >= 1:
                        pe.wait_ge(pT_ready, hp)
                    for h in range(2):
                        for kt in range(2):
                            for t in range(TT):
                                last = pe.transpose(tps[:, h, kt, t * P:(t + 1) * P],
                                                    scores[:, hp % 2, h, t, kt * P:(kt + 1) * P], k.c("ident"))
                    last.then_inc(p_turned, 1)
                    pe.wait_ge(pT_ready, hp + 1)
                    for h in range(2):
                        v = slice(1024 + (2 * hp + h) * 64, 1024 + (2 * hp + h) * 64 + 64)
                        for t in range(TT):
                            for kt in range(t + 1):
                                last = pe.matmul(ops[:, 2 * hp + h, t, :], pT[:, hp % 2, h, kt, t * P:(t + 1) * P],
                                                 a["qkv"][:, kt, v], start=(kt == 0), stop=(kt == t))
                    last.then_inc(pv_done, 1)


def stage_conv(k, a):
    nc = k.nc
    with ExitStack() as ctx:
        acc = k.sb("conv_acc", [P, KD, TOK], ctx=ctx)
        ex = k.sb("conv_exp", [P, KD, TOK], ctx=ctx)
        t4 = k.sb("gate_tmp", [4, 8, TOK], ctx=ctx)
        q4 = k.sb("gate_quads", [P, TOK], ctx=ctx)
        sc = k.sb("gate_small", [4, 8], ctx=ctx)
        conv_done, silu_exp, f_ready, f_exp, m_ready, e_ready, quads_ready, cols_ready, arow = (
            k.sem(s) for s in ("conv_done", "silu_exp", "f_ready", "f_exp", "m_ready", "m_exp", "quads_ready",
                               "gate_cols_ready", "a_rows_ready"))
        logf, cum, b, pm, mt, tmp, one = (t4[:, i, :] for i in range(7))
        ig = a["gate_rows"][0:4, 0, :]
        fg = a["gate_rows"][0:4, 1, :]
        with nc.Block() as block:
            @block.gpsimd
            def _(pool):
                pool.memset(q4[:], 0.0).then_inc(arow, 1)

            @block.scalar
            def _(act):
                act.wait_ge(f_ready, 1)
                act.activation(tmp, tmp, ACT.Exp, scale=-1.0)
                act.drain()
                act.activation(tmp, tmp, ACT.Ln, bias=1.0).then_inc(f_exp, 1)
                for f in range(KD):
                    act.wait_ge(conv_done, f + 1)
                    act.activation(ex[:, f, :], acc[:, f, :], ACT.Exp, scale=-1.0).then_inc(silu_exp, 1)
                act.wait_ge(m_ready, 1)
                act.wait_ge(arow, 1)
                act.activation(q4[32:36, :], one, ACT.Exp)
                act.activation(q4[64:68, :], mt, ACT.Exp, scale=-1.0)
                act.activation(q4[96:100, 0:P], b[:, 0:P], ACT.Exp, bias=sc[:, 2:3]).then_inc(e_ready, 1)

            @block.vector
            def _(dve):
                dve.scalar_tensor_tensor(out=tmp, in0=fg, scalar=-1.0, in1=fg, op0=ALU.mult, op1=ALU.max).then_inc(f_ready, 1)
                for f in range(KD):
                    w = [k.col("conv_w", 4 * f + i) for i in range(4)]
                    dve.tensor_scalar(acc[:, f, :], a["qk_mT"][:, f, 0:TOK], w[0], k.col("conv_b", f), ALU.mult, ALU.add)
                    dve.drain()
                    for i in range(1, 4):
                        ins = dve.scalar_tensor_tensor(out=acc[:, f, :], in0=a["qk_mT"][:, f, i:i + TOK], scalar=w[i],
                                                       in1=acc[:, f, :], op0=ALU.mult, op1=ALU.add)
                        if i == 3:
                            ins.then_inc(conv_done, 1)
                        else:
                            dve.drain()
                dve.wait_ge(f_exp, 1)
                dve.tensor_scalar(logf, fg, 0.0, None, ALU.min)
                dve.memset(one, 1.0)
                dve.drain()
                dve.tensor_tensor(logf, logf, tmp, ALU.subtract)
                dve.drain()
                for c in range(2):
                    s = slice(c * P, (c + 1) * P)
                    dve.tensor_tensor_scan(cum[:, s], one[:, s], logf[:, s], 0.0, ALU.mult, ALU.add)
                dve.drain()
                dve.tensor_tensor(b, ig, cum, ALU.subtract)
                dve.drain()
                for c in range(2):
                    s = slice(c * P, (c + 1) * P)
                    dve.tensor_tensor_scan(pm[:, s], one[:, s], b[:, s], -3e38, ALU.mult, ALU.max)
                dve.drain()
                total = cum[:, P - 1:P]
                dve.tensor_tensor(sc[:, 1:2], total, pm[:, P - 1:P], ALU.add)
                dve.drain()
                dve.tensor_tensor(sc[:, 0:1], sc[:, 1:2], total, ALU.max)
                dve.drain()
                dve.tensor_tensor(sc[:, 2:3], total, sc[:, 0:1], ALU.subtract)
                dve.tensor_copy(tmp[:, 0:P], cum[:, 0:P])
                dve.tensor_scalar(tmp[:, P:], cum[:, P:], sc[:, 0:1], None, ALU.add)
                dve.tensor_tensor(mt, cum, pm, ALU.add)
                dve.drain()
                dve.tensor_tensor(mt, mt, tmp, ALU.max)
                dve.drain()
                dve.tensor_tensor(one, tmp, mt, ALU.subtract)
                dve.tensor_tensor(a["a_rows"][:], cum, mt, ALU.subtract)
                dve.drain()
                dve.wait_ge(arow, 1)
                dve.tensor_copy(q4[0:4, :], b).then_inc(m_ready, 1)
                dve.wait_ge(silu_exp, KD)
                dve.tensor_scalar(ex[:], ex[:], 1.0, None, ALU.add)
                dve.drain()
                dve.reciprocal(ex[:], ex[:])
                dve.drain()
                dve.tensor_tensor(a["qk_mT"][:, :, 3:3 + TOK], acc[:], ex[:], ALU.mult)
                dve.wait_ge(quads_ready, 1)
                for t in range(TT):
                    dve.tensor_copy(a["gcol"][:, t, :], k.ps[:, t, 0:P])
                dve.drain()
                dve.tensor_scalar(a["gcol"][:, 0, 96:100], a["gcol"][:, 0, 96:100], 128 ** -0.5, None, ALU.mult)

            @block.tensor
            def _(pe):
                pe.wait_ge(m_ready, 1)
                pe.wait_ge(e_ready, 1)
                for t in range(TT):
                    last = pe.transpose(k.ps[:, t, 0:P], q4[:, t * P:(t + 1) * P], k.c("ident"))
                last.then_inc(quads_ready, 1)


def stage_mlstm(k, a):
    nc = k.nc
    with ExitStack() as ctx:
        dm = k.sb("dmat", [P, 4, TOK], ctx=ctx)
        st = k.sb("s_t", [P, 4, TOK], ctx=ctx)
        kw = k.sb("k_weighted", [P, 4, P], ctx=ctx)
        cst = k.sb("c_state", [P, 4, 129], ctx=ctx)
        num = k.sb("num", [P, TT, 4, 129], ctx=ctx)
        den = k.sb("den", [P, TT, 4, 1], ctx=ctx)
        a_bc, masked, d_exp, s_raw, s_ready, kt, kw_ready, c_done, c_out, num0, num1, inter = (
            k.sem(s) for s in ("a_bc", "d_masked", "d_exp", "s_raw", "s_ready", "k_turned", "kw_ready", "c_done", "c_out",
                               "num0_done", "num1_done", "inter_done"))
        abc = k.ps[:, 0:2, :].rearrange("p b (h t) -> p (b h) t", h=2)
        sps = k.ps[:, 2:4, :].rearrange("p b (h t) -> p (b h) t", h=2)
        qT = lambda h, t: a["qk_mT"][:, h, 3 + t * P:3 + (t + 1) * P]
        kT = lambda h, t: a["qk_mT"][:, 4 + h, 3 + t * P:3 + (t + 1) * P]
        b_col = lambda h, t: a["gcol"][:, t, h:h + 1]
        acc = lambda i, h: k.ps[:, i + h // 2, 256 * (h % 2):256 * (h % 2) + 129]
        with nc.Block() as block:
            @block.tensor
            def _(pe):
                for h in range(4):
                    last = pe.matmul(abc[:, h, :], k.c("one_hot4")[0:4, h * P:(h + 1) * P], a["a_rows"][:],
                                     start=True, stop=True)
                last.then_inc(a_bc, 1)
                for h in range(4):
                    for t in range(TT):
                        last = pe.matmul(sps[:, h, t * P:(t + 1) * P], kT(h, t), qT(h, t), start=True, stop=True)
                last.then_inc(s_raw, 1)
                for h in range(4):
                    last = pe.transpose(k.ps[:, 4, h * P:(h + 1) * P], kT(h, 0), k.c("ident"))
                last.then_inc(kt, 1)
                pe.wait_ge(kw_ready, 1)
                for h in range(4):
                    last = pe.matmul(acc(5, h), kw[:, h, :], a["v_aug"][:, 0, h, :], start=True, stop=True)
                last.then_inc(c_done, 1)
                pe.wait_ge(s_ready, 1)
                for t in range(TT):
                    for h in range(4):
                        last = pe.matmul(acc(2 * t, h), st[:, h, t * P:(t + 1) * P], a["v_aug"][:, t, h, :],
                                         start=True, stop=True)
                last.then_inc(num0, 1)
                pe.wait_ge(c_out, 1)
                for h in range(4):
                    last = pe.matmul(acc(5, h), qT(h, 1), cst[:, h, :], start=True, stop=True)
                last.then_inc(inter, 1)

            @block.scalar
            def _(act):
                act.wait_ge(masked, 1)
                for h in range(4):
                    for t in range(TT):
                        s = slice(t * P, (t + 1) * P)
                        last = act.activation(dm[:, h, s], dm[:, h, s], ACT.Exp, bias=b_col(h, t))
                last.then_inc(d_exp, 1)

            @block.vector
            def _(dve):
                dve.wait_ge(a_bc, 1)
                for t in range(TT):
                    s = slice(t * P, (t + 1) * P)
                    last = dve.tensor_tensor(dm[:, :, s], abc[:, :, s], bc(k.c("causal_t"), 1, 4), ALU.add)
                last.then_inc(masked, 1)
                dve.wait_ge(kt, 1)
                dve.tensor_tensor(kw[:], k.ps[:, 4, :].rearrange("p (h d) -> p h d", h=4),
                                  bc(a["gcol"][:, 0, 96:100], 2, P), ALU.mult).then_inc(kw_ready, 1)
                dve.wait_ge(d_exp, 1)
                dve.wait_ge(s_raw, 1)
                dve.scalar_tensor_tensor(out=st[:], in0=sps[:], scalar=128 ** -0.5, in1=dm[:], op0=ALU.mult,
                                         op1=ALU.mult).then_inc(s_ready, 1)
                dve.wait_ge(c_done, 1)
                for h in range(4):
                    last = dve.tensor_copy(cst[:, h, :], acc(5, h))
                last.then_inc(c_out, 1)
                dve.wait_ge(num0, 1)
                for t in range(TT):
                    for h in range(4):
                        dve.tensor_copy(num[:, t, h, :], acc(2 * t, h))
                dve.drain()
                dve.wait_ge(inter, 1)
                for h in range(4):
                    dve.scalar_tensor_tensor(out=num[:, 1, h, :], in0=acc(5, h), scalar=a["gcol"][:, 1, 32 + h:33 + h],
                                             in1=num[:, 1, h, :], op0=ALU.mult, op1=ALU.add)
                dve.drain()
                dve.scalar_tensor_tensor(out=den[:, :, :, 0], in0=num[:, :, :, 128], scalar=-1.0, in1=num[:, :, :, 128],
                                         op0=ALU.mult, op1=ALU.max)
                dve.drain()
                for t in range(TT):
                    dve.tensor_tensor(den[:, t, :, 0], den[:, t, :, 0], a["gcol"][:, t, 64:68], ALU.max)
                dve.drain()
                dve.reciprocal(den[:], den[:])
                dve.drain()
                for t in range(TT):
                    dve.tensor_tensor(a["mix"][:, t, 512:1024].rearrange("p (h e) -> p h e", h=4), num[:, t, :, 0:128],
                                      den[:, t, :, :].broadcast_to([P, 4, 128]), ALU.mult)


def stage_out_projection(k, a):
    nc = k.nc
    with ExitStack() as ctx:
        sq = k.sb("mix_sq", [P, TT, D], ctx=ctx)
        ss = k.sb("head_ss", [P, TT, 12], ctx=ctx)
        rstd = k.sb("head_rstd", [P, TT, 12], ctx=ctx)
        sig = k.sb("sig", [P, TT, 512], ctx=ctx)
        mixT = k.sb("mixT", [P, KD, TOK], ctx=ctx)
        xn = k.sb("xn1", [P, TT, D], ctx=ctx)
        w_router = k.sb("w_router", [P, KD, 36], ctx=ctx)
        norm = NormT(k, "norm2", k.x, ctx, xn)
        squares, rstd_ready, sig_exp, mix_ready, mix_turned, mixT_ready, x_ready, logits, router_in = (
            k.sem(s) for s in ("mix_squares", "head_rstd_ready", "sig_exp", "mix_ready", "mix_turned", "mixT_ready",
                               "x_ready", "logits_done", "router_in"))
        tps = k.ps[:, 0:4, :].rearrange("p b (f t) -> p (b f) t", f=2)
        groups = ((0, 512, 64, 0, 8, "attn_out_g"), (512, 1024, 128, 8, 12, "mlstm_out_g"))
        with nc.Block() as block:
            @block.sync
            def _(sp):
                sp.dma_start(w_router[:], k.dram["w_router"]).then_inc(router_in, 16)
                stream(k, sp, T_OUT, T_OUT + N_OUT)

            @block.scalar
            def _(act):
                act.activation(sig[:], a["o_m"][:], ACT.Exp, scale=-1.0).then_inc(sig_exp, 1)
                act.wait_ge(x_ready, 1)
                norm.act(act)

            @block.gpsimd
            def _(pool):
                pool.wait_ge(squares, 1)
                pool.tensor_scalar(rstd[:, :, 0:8], ss[:, :, 0:8], 1.0 / 64, EPS, ALU.mult, ALU.add)
                pool.tensor_scalar(rstd[:, :, 8:12], ss[:, :, 8:12], 1.0 / 128, EPS, ALU.mult, ALU.add)
                pool.drain()
                for t in range(TT):
                    last = pool.tensor_tensor(out=rstd[:, t, :], in0=rstd[:, t, :], in1=k.c("minus_half")[:, 0:12],
                                              op=ALU.pow)
                last.then_inc(rstd_ready, 1)
                norm.pool(pool)

            @block.vector
            def _(dve):
                dve.tensor_tensor(sq[:], a["mix"][:], a["mix"][:], ALU.mult)
                dve.drain()
                for c0, c1, w, s0, s1, _g in groups:
                    for t in range(TT):
                        last = dve.tensor_reduce(ss[:, t, s0:s1], sq[:, t, c0:c1].rearrange("p (h e) -> p h e", e=w),
                                                 AX, ALU.add)
                last.then_inc(squares, 1)
                dve.wait_ge(sig_exp, 1)
                dve.tensor_scalar(sig[:], sig[:], 1.0, None, ALU.add)
                dve.drain()
                dve.reciprocal(sig[:], sig[:])
                dve.drain()
                dve.tensor_tensor(sig[:], sig[:], bc(k.row("mlstm_out_g"), 1, TT), ALU.mult)
                dve.wait_ge(rstd_ready, 1)
                for c0, c1, w, s0, s1, _g in groups:
                    for t in range(TT):
                        v = a["mix"][:, t, c0:c1].rearrange("p (h e) -> p h e", e=w)
                        dve.tensor_tensor(v, v, bc(rstd[:, t, s0:s1], 2, w), ALU.mult)
                dve.drain()
                dve.tensor_tensor(a["mix"][:, :, 0:512], a["mix"][:, :, 0:512], bc(k.row("attn_out_g"), 1, TT), ALU.mult)
                dve.tensor_tensor(a["mix"][:, :, 512:1024], a["mix"][:, :, 512:1024], sig[:], ALU.mult).then_inc(mix_ready, 1)
                dve.wait_ge(mix_turned, KD)
                dve.tensor_copy(mixT[:], tps[:]).then_inc(mixT_ready, 1)
                for n in range(N_OUT):
                    dve.wait_ge(k.tile_done, T_OUT + n + 1)
                    s = slice(n * 512, (n + 1) * 512)
                    dve.tensor_tensor(sq[:, :, s], k.ps[:, 4 + 2 * n:6 + 2 * n, :], bc(k.row("b_g1")[:, s], 1, TT), ALU.mult)
                dve.drain()
                dve.tensor_tensor(k.x[:], k.x[:], sq[:], ALU.add).then_inc(x_ready, 1)
                norm.dve_scale(dve)
                norm.dve_out(dve, k.hT, k.mod[:, 24:32], k.mod[:, 16:24])
                dve.wait_ge(logits, 1)
                dve.tensor_tensor(a["logits"][:], k.ps[:, 4:6, 0:36], bc(k.row("b_router"), 1, TT), ALU.add)

            @block.tensor
            def _(pe):
                pe.wait_ge(mix_ready, 1)
                turn(k, pe, a["mix"], KD, tps, mix_turned)
                pe.wait_ge(mixT_ready, 1)
                for n in range(N_OUT):
                    tm_tile(k, pe, T_OUT + n, mixT, k.ps[:, 4 + 2 * n:6 + 2 * n, :])
                norm.pe(pe)
                pe.wait_ge(norm.done, KD)
                pe.wait_ge(router_in, 16)
                for t in range(TT):
                    for kk in range(KD):
                        last = pe.matmul(k.ps[:, 4 + t, 0:36], k.hT[:, kk, t * P:(t + 1) * P], w_router[:, kk, :],
                                         start=(kk == 0), stop=(kk == KD - 1))
                last.then_inc(logits, 1)


def stage_route(k, a):
    nc = k.nc
    with ExitStack() as ctx:
        g8 = k.sb("g8", [P, TT, 8], ctx=ctx)
        gm = k.sb("g_top", [P, TT, 8], ctx=ctx)
        gi = k.sb("g_idx", [P, TT, 8], U32, ctx=ctx)
        gf = k.sb("g_idx_f", [P, TT, 8], ctx=ctx)
        ge = k.sb("g_exp", [P, TT, 4], ctx=ctx)
        gs = k.sb("g_sum", [P, TT], ctx=ctx)
        gmask = k.sb("g_mask", [P, TT, 4], ctx=ctx)
        em = k.sb("e_masked", [P, TT, 32], ctx=ctx)
        et = k.sb("e_top", [P, TT, 8], ctx=ctx)
        ei = k.sb("e_idx", [P, TT, 8], U32, ctx=ctx)
        ef = k.sb("e_idx_f", [P, TT, 8], ctx=ctx)
        dl = k.sb("e_gap", [P, TT], ctx=ctx)
        w1 = k.sb("w_first", [P, TT], ctx=ctx)
        w2 = k.sb("w_second", [P, TT], ctx=ctx)
        gap_ready, exp_done = k.sem("gap_ready"), k.sem("route_exp_done")
        with nc.Block() as block:
            @block.vector
            def _(dve):
                dve.memset(g8[:], -3e38)
                dve.drain()
                dve.tensor_copy(g8[:, :, 0:4], a["logits"][:, :, 0:4])
                dve.drain()
                for t in range(TT):
                    dve.max(gm[:, t, :], g8[:, t, :])
                dve.drain()
                for t in range(TT):
                    dve.max_index(gi[:, t, :], gm[:, t, :], g8[:, t, :])
                    dve.tensor_scalar(ge[:, t, :], a["logits"][:, t, 0:4], gm[:, t, 0:1], None, ALU.subtract)
                dve.drain()
                dve.tensor_copy(gf[:], gi[:])
                dve.drain()
                for t in range(TT):
                    dve.tensor_scalar(gmask[:, t, :], k.c("iota32")[:, 0:4], gf[:, t, 0:1], None, ALU.is_equal)
                dve.drain()
                for t in range(TT):
                    dve.tensor_tensor(em[:, t, :].rearrange("p (g e) -> p g e", g=4),
                                      a["logits"][:, t, 4:36].rearrange("p (g e) -> p g e", g=4),
                                      bc(gmask[:, t, :], 2, 8), ALU.mult)
                dve.drain()
                dve.tensor_scalar(gmask[:], gmask[:], -NEG, NEG, ALU.mult, ALU.add)
                dve.drain()
                for t in range(TT):
                    v = em[:, t, :].rearrange("p (g e) -> p g e", g=4)
                    dve.tensor_tensor(v, v, bc(gmask[:, t, :], 2, 8), ALU.add)
                dve.drain()
                for t in range(TT):
                    dve.max(et[:, t, :], em[:, t, :])
                dve.drain()
                for t in range(TT):
                    dve.max_index(ei[:, t, :], et[:, t, :], em[:, t, :])
                dve.tensor_tensor(dl[:], et[:, :, 1], et[:, :, 0], ALU.subtract).then_inc(gap_ready, 1)
                dve.drain()
                dve.tensor_copy(ef[:], ei[:])
                dve.wait_ge(exp_done, 1)
                dve.tensor_reduce(gs[:], ge[:], AX, ALU.add)
                dve.tensor_scalar(w1[:], dl[:], 1.0, None, ALU.add)
                dve.drain()
                dve.tensor_tensor(w1[:], w1[:], gs[:], ALU.mult)
                dve.drain()
                dve.reciprocal(w1[:], w1[:])
                dve.drain()
                dve.tensor_tensor(w2[:], w1[:], dl[:], ALU.mult)
                dve.drain()
                for t in range(TT):
                    dve.tensor_scalar(a["comb"][:, t, :], k.c("iota32"), ef[:, t, 0:1], w1[:, t:t + 1], ALU.is_equal, ALU.mult)
                    dve.tensor_scalar(em[:, t, :], k.c("iota32"), ef[:, t, 1:2], w2[:, t:t + 1], ALU.is_equal, ALU.mult)
                dve.drain()
                dve.tensor_tensor(a["comb"][:], a["comb"][:], em[:], ALU.add)
                dve.memset(a["moe"][:], 0.0)

            @block.scalar
            def _(act):
                act.wait_ge(gap_ready, 1)
                act.activation(ge[:], ge[:], ACT.Exp)
                act.activation(dl[:], dl[:], ACT.Exp).then_inc(exp_done, 1)


def stage_experts(k, a):
    nc = k.nc
    with ExitStack() as ctx:
        gate = k.sb("gate", [P, 4, TOK], ctx=ctx)
        act_t = k.sb("act_t", [P, 4, TOK], ctx=ctx)
        silu_done, a_ready, y_done, y_out = (k.sem(s) for s in ("silu_done", "act_ready", "y_done", "y_out"))
        h1, h3 = (k.ps[:, 2 * i:2 * i + 2, :].rearrange("p b (f t) -> p (b f) t", f=2) for i in range(2))
        y = k.ps[:, 4:8, :].rearrange("p (n t) c -> p n t c", n=2)
        t0 = T_MOE // RING
        with nc.Block() as block:
            @block.sync
            def _(sp):
                stream(k, sp, T_MOE, T_GLA)

            @block.tensor
            def _(pe):
                with pe.Fori(0, N_EXP) as e:
                    for j, out in ((0, h1), (1, h3)):
                        pe.wait_ge(k.landed[j], e * 16 + 16 * (t0 + 1))
                        pe.wait_ge(a_ready, e + 1)
                        w = k.ring[:, j, :].rearrange("p (k n) -> p k n", k=KD)
                        for f in range(4):
                            for kk in range(KD):
                                last = pe.matmul(out[:, f, :], w[:, kk, f * P:(f + 1) * P], k.hT[:, kk, :],
                                                 start=(kk == 0), stop=(kk == KD - 1))
                        last.then_inc(k.tile_done, 1)
                    pe.wait_ge(k.landed[2], e * 16 + 16 * (t0 + 1))
                    pe.wait_ge(a_ready, e + 2)
                    pe.wait_ge(y_out, e + 1)
                    w = k.ring[:, 2, :].rearrange("p (k n) -> p k n", k=4)
                    for n in range(2):
                        for t in range(TT):
                            for f in range(4):
                                last = pe.matmul(y[:, n, t, :], act_t[:, f, t * P:(t + 1) * P], w[:, f, n * 512:(n + 1) * 512],
                                                 start=(f == 0), stop=(f == 3))
                    last.then_inc(k.tile_done, 1)

            @block.scalar
            def _(act):
                with act.Fori(0, N_EXP) as e:
                    act.wait_ge(k.tile_done, e * 3 + T_MOE + 1)
                    act.wait_ge(a_ready, e + 1)
                    act.activation(gate[:], h1, ACT.Silu).then_inc(silu_done, 1)

            @block.vector
            def _(dve):
                dve.sem_inc(a_ready, 1)
                dve.sem_inc(y_out, 1)
                with dve.Fori(0, N_EXP) as e:
                    dve.wait_ge(silu_done, e + 1)
                    dve.wait_ge(k.tile_done, e * 3 + T_MOE + 2)
                    dve.tensor_tensor(act_t[:], gate[:], h3, ALU.mult).then_inc(a_ready, 1)
                    dve.wait_ge(k.tile_done, e * 3 + T_MOE + 3)
                    for t in range(TT):
                        for n in range(2):
                            o = a["moe"][:, t, n * 512:(n + 1) * 512]
                            last = dve.scalar_tensor_tensor(out=o, in0=y[:, n, t, :], in1=o, op0=ALU.mult, op1=ALU.add,
                                                            scalar=a["comb"][:, t, bass.ds(e, 1)])
                    last.then_inc(y_out, 1)


def stage_first_end(k, a):
    nc = k.nc
    with ExitStack() as ctx:
        xn = k.sb("xn2", [P, TT, D], ctx=ctx)
        f = NormT(k, "norm_f", k.x, ctx, xn)
        g = NormT(k, "gla_norm", k.x, ctx, xn)
        x_ready, x_normed = k.sem("moe_added"), k.sem("x_normed")
        with nc.Block() as block:
            @block.vector
            def _(dve):
                dve.tensor_tensor(a["moe"][:], a["moe"][:], bc(k.row("b_g2"), 1, TT), ALU.mult)
                dve.drain()
                dve.tensor_tensor(k.x[:], k.x[:], a["moe"][:], ALU.add).then_inc(x_ready, 1)
                dve.wait_ge(f.rstd_ready, 1)
                for t in range(TT):
                    last = dve.scalar_tensor_tensor(out=k.x[:, t, :], in0=k.x[:, t, :], scalar=f.rstd[:, t:t + 1],
                                                    in1=k.row("norm_f_g"), op0=ALU.mult, op1=ALU.mult)
                last.then_inc(x_normed, 1)
                dve.drain()
                g.dve_scale(dve)
                g.dve_out(dve, k.hT, k.col("norm_w_2", 0, KD))

            @block.scalar
            def _(act):
                act.wait_ge(x_ready, 1)
                f.act(act)
                act.wait_ge(x_normed, 1)
                g.act(act)

            @block.gpsimd
            def _(pool):
                f.pool(pool)
                g.pool(pool)

            @block.tensor
            def _(pe):
                g.pe(pe)


def first_block(k):
    stage_modulation(k)
    with ExitStack() as ctx:
        a = {
            "w_gate": k.sb("w_gate", [P, KD, 8], ctx=ctx),
            "qkv": k.sb("qkv", [P, TT, 1536], ctx=ctx),
            "qk_mT": k.sb("qk_mT", [P, KD, 3 + TOK], ctx=ctx),
            "v_aug": k.sb("v_aug", [P, TT, 4, 129], ctx=ctx),
            "o_m": k.sb("o_m", [P, TT, 512], ctx=ctx),
            "gate_rows": k.sb("gate_rows", [4, 2, TOK], ctx=ctx),
            "a_rows": k.sb("a_rows", [4, TOK], ctx=ctx),
            "gcol": k.sb("gcol", [P, TT, P], ctx=ctx),
            "mix": k.sb("mix", [P, TT, D], ctx=ctx),
            "logits": k.sb("logits", [P, TT, 36], ctx=ctx),
        }
        stage_in_projection(k, a)
        stage_attention(k, a)
        stage_conv(k, a)
        stage_mlstm(k, a)
        stage_out_projection(k, a)
        a["comb"] = k.sb("comb", [P, TT, 32], ctx=ctx)
        a["moe"] = k.sb("moe", [P, TT, D], ctx=ctx)
        stage_route(k, a)
        stage_experts(k, a)
        stage_first_end(k, a)


def stage_tiles(k, name, first, specs, sp_extra=None, pe_extra=None, dve_extra=None):
    outs = {e: k.sem(f"{name}_out_{e}") for e in ("dve", "act")}
    nth = [sum(s[3] == spec[3] for s in specs[:m + 1]) for m, spec in enumerate(specs)]
    with k.nc.Block() as block:
        @block.sync
        def _(sp):
            if sp_extra:
                sp_extra(sp)
            stream(k, sp, first, first + len(specs))

        @block.tensor
        def _(pe):
            for m, (kind, src, k0, _engine, _write) in enumerate(specs):
                if m >= 3:
                    pe.wait_ge(outs[specs[m - 3][3]], nth[m - 3])
                if kind == "tm":
                    tm_tile(k, pe, first + m, src, pair(k, m), k0)
                else:
                    fm_tile(k, pe, first + m, src, pair_fm(k, m), k0)
            if pe_extra:
                pe_extra(pe)

        def write_out(engine, which):
            for m, (kind, _src, _k0, owner, write) in enumerate(specs):
                if owner == which:
                    engine.wait_ge(k.tile_done, first + m + 1)
                    write(engine, pair(k, m) if kind == "tm" else pair_fm(k, m)).then_inc(outs[which], 1)

        @block.vector
        def _(dve):
            write_out(dve, "dve")
            if dve_extra:
                dve_extra(dve)

        @block.scalar
        def _(act):
            write_out(act, "act")


def copy_to(dst):
    return lambda dve, src: dve.tensor_copy(dst, src)


def silu_to(dst):
    return lambda act, src: act.activation(dst, src, ACT.Silu)


def add_after(dst):
    def write(dve, src):
        dve.drain()
        return dve.tensor_tensor(dst, dst, src, ALU.add)
    return write


def stage_gla_gate(k, a):
    with ExitStack() as ctx:
        rT = k.sb("rT", [16, TOK], ctx=ctx)
        g = k.sb("g_log", [P, TT, 512], ctx=ctx)
        lg = k.sb("g_tmp", [P, TT, 512], ctx=ctx)
        eq, ek = (k.sb(n, [P, TT, 512], ctx=ctx) for n in ("exp_q", "exp_k"))
        ee = lg
        r_done, rT_ready, g_pre, abs_ready, log_ready, g_ready, cum_done, exp_done, dec_ready, turned = (
            k.sem(s) for s in ("r_done", "rT_ready", "g_pre", "g_abs_ready", "g_log_ready", "g_ready", "cum_done",
                               "decay_exp_done", "decayed", "gla_turned"))
        q, key = a["qk"][:, :, 0:512], a["qk"][:, :, 512:1024]
        with k.nc.Block() as block:
            @block.tensor
            def _(pe):
                for kk in range(KD):
                    last = pe.matmul(k.ps[0:16, 7, 0:TOK], a["w_rank"][:, kk, :], k.hT[:, kk, :],
                                     start=(kk == 0), stop=(kk == KD - 1))
                last.then_inc(r_done, 1)
                pe.wait_ge(rT_ready, 1)
                for t in range(TT):
                    last = pe.matmul(k.ps[:, t, :], rT[:, t * P:(t + 1) * P], a["w_up"][:], start=True, stop=True)
                last.then_inc(g_pre, 1)
                pe.wait_ge(g_ready, 1)
                for t in range(TT):
                    pe.matmul(k.ps[:, 2 + t, :], k.c("chunk_tri"), g[:, t, :], start=True, stop=True)
                    pe.matmul(k.ps[:, 4 + t, :], k.c("chunk_suffix"), g[:, t, :], start=True, stop=True)
                    for h in range(4):
                        i = 2 * (4 * t + h)
                        last = pe.matmul(k.ps[:, 6, i:i + 2], g[:, t, h * P:(h + 1) * P], k.c("chunk_ind"),
                                         start=True, stop=True)
                last.then_inc(cum_done, 1)
                pe.wait_ge(dec_ready, 1)
                turn(k, pe, q, 4, k.ps[:, 0:2, :].rearrange("p b (f t) -> p (b f) t", f=2), turned)
                turn(k, pe, a["k_inv"], 4, k.ps[:, 2:4, :].rearrange("p b (f t) -> p (b f) t", f=2), turned)

            @block.scalar
            def _(act):
                act.wait_ge(abs_ready, 1)
                act.activation(lg[:], lg[:], ACT.Exp, scale=-1.0)
                act.drain()
                act.activation(lg[:], lg[:], ACT.Ln, bias=1.0).then_inc(log_ready, 1)
                act.wait_ge(cum_done, 1)
                act.activation(eq[:], k.ps[:, 2:4, :], ACT.Exp)
                act.activation(ek[:], k.ps[:, 2:4, :], ACT.Exp, scale=-1.0)
                act.activation(ee[:], k.ps[:, 4:6, :], ACT.Exp)
                act.activation(a["decay"][:], k.ps[:, 6, 0:16], ACT.Exp).then_inc(exp_done, 1)

            @block.vector
            def _(dve):
                dve.memset(a["att"][:], 0.0)
                dve.wait_ge(r_done, 1)
                dve.tensor_copy(rT[:], k.ps[0:16, 7, 0:TOK]).then_inc(rT_ready, 1)
                dve.wait_ge(g_pre, 1)
                dve.tensor_tensor(g[:], k.ps[:, 0:2, :], bc(k.row("gla_bias"), 1, TT), ALU.add)
                dve.drain()
                dve.scalar_tensor_tensor(out=lg[:], in0=g[:], scalar=-1.0, in1=g[:], op0=ALU.mult,
                                         op1=ALU.max).then_inc(abs_ready, 1)
                dve.wait_ge(log_ready, 1)
                dve.scalar_tensor_tensor(out=g[:], in0=g[:], scalar=0.0, in1=lg[:], op0=ALU.min, op1=ALU.subtract)
                dve.drain()
                dve.tensor_scalar(g[:], g[:], 1.0 / 16.0, None, ALU.mult).then_inc(g_ready, 1)
                dve.wait_ge(exp_done, 1)
                dve.scalar_tensor_tensor(out=q, in0=q, scalar=128 ** -0.5, in1=eq[:], op0=ALU.mult, op1=ALU.mult)
                dve.tensor_tensor(a["k_inv"][:], key, ek[:], ALU.mult)
                dve.drain()
                dve.tensor_tensor(key, key, ee[:], ALU.mult).then_inc(dec_ready, 1)
                dve.wait_ge(turned, 8)
                dve.tensor_copy(a["qT"][:], k.ps[:, 0:2, :].rearrange("p b (f t) -> p (b f) t", f=2))
                dve.tensor_copy(a["kT"][:], k.ps[:, 2:4, :].rearrange("p b (f t) -> p (b f) t", f=2))


def stage_gla(k, a):
    HT = TOK // 2
    with ExitStack() as ctx:
        junk = k.sb("o_sq", [P, 512], ctx=ctx)
        ss = k.sb("o_ss", [P, 8], ctx=ctx)
        rstd = k.sb("o_rstd", [P, 8], ctx=ctx)
        att_done, att_ready, upd_done, state_ready, tile_out, o_ready, o_copied, summed, rstd_ready, o_normed, turned, gated = (
            k.sem(s) for s in ("att_done", "att_ready", "state_update_done", "state_ready", "o_tile_out", "o_ready",
                               "o_copied", "o_summed", "o_rstd_ready", "o_normed", "o_turned", "o_gated"))
        state, v, key = a["state"], a["v"], a["qk"][:, :, 512:1024]
        half = lambda c: slice(64 * c, 64 * c + 64)
        ups = lambda h: k.ps[:, 4 + h, :]
        with k.nc.Block() as block:
            @block.tensor
            def _(pe):
                for h in range(4):
                    for t in range(TT):
                        s = slice(t * P, (t + 1) * P)
                        last = pe.matmul(k.ps[:, 4 + h // 2, 256 * (h % 2) + t * P:256 * (h % 2) + (t + 1) * P],
                                         a["kT"][:, h, s], a["qT"][:, h, s], start=True, stop=True)
                last.then_inc(att_done, 1)
                pe.wait_ge(att_ready, 1)

                def inter(t, c, stop):
                    for h in range(4):
                        pe.wait_ge(state_ready, 4 * (2 * t + c - 1) + h + 1)
                        last = pe.matmul(k.ps[half(c), h, :], a["qT"][:, h, t * P + 64 * c:t * P + 64 * c + 64],
                                         state[:, h, :], start=False, stop=stop, skip_group_check=True)
                    return last

                def update(t, c):
                    for h in range(4):
                        if 2 * t + c:
                            pe.wait_ge(state_ready, 4 * (2 * t + c - 1) + h + 1)
                        last = pe.matmul(ups(h), key[half(c), t, h * P:(h + 1) * P], v[half(c), t, h * 512:(h + 1) * 512],
                                         start=True, stop=True)
                        last.then_inc(upd_done, 1)

                for t in range(TT):
                    if t:
                        pe.wait_ge(tile_out, 1)
                    for h in range(4):
                        last = pe.matmul(k.ps[:, h, :], a["att"][:, 2 * h + t, :], v[:, t, h * 512:(h + 1) * 512],
                                         start=True, stop=False, skip_group_check=True)
                    if t:
                        inter(t, 0, False)
                    update(t, 0)
                    last = inter(t, 1, True)
                    if t == 0:
                        update(t, 1)
                    last.then_inc(o_ready, 1) if t else pe.sem_inc(o_ready, 1)
                for r in range(2):
                    pe.wait_ge(o_normed, 1)
                    turn(k, pe, v[:, :, r * 1024:(r + 1) * 1024], KD,
                         k.ps[:, 4 * r:4 * r + 4, :].rearrange("p b (f t) -> p (b f) t", f=2), turned)

            @block.vector
            def _(dve):
                dve.wait_ge(att_done, 1)
                dve.copy_predicated(a["att"][:], bc(k.c("chunk_tri"), 1, 8).bitcast(U32),
                                    k.ps[:, 4:6, :].rearrange("p b (i t) -> p (b i) t", i=4)).then_inc(att_ready, 1)
                for t, c in ((0, 0), (0, 1), (1, 0)):
                    for h in range(4):
                        i = 2 * t + c
                        dve.wait_ge(upd_done, 4 * i + h + 1)
                        if i == 0:
                            ins = dve.tensor_copy(state[:, h, :], ups(h))
                        else:
                            j = 2 * (4 * t + h) + c
                            ins = dve.scalar_tensor_tensor(out=state[:, h, :], in0=state[:, h, :],
                                                           scalar=a["decay"][:, j:j + 1], in1=ups(h),
                                                           op0=ALU.mult, op1=ALU.add)
                        ins.then_inc(state_ready, 1)
                    dve.drain()
                    if (t, c) == (0, 1):
                        dve.wait_ge(o_ready, 1)
                        dve.tensor_copy(v[:, 0, :].rearrange("p (h e) -> p h e", h=4), k.ps[:, 0:4, :]).then_inc(tile_out, 1)
                dve.wait_ge(o_ready, 2)
                dve.tensor_copy(v[:, 1, :].rearrange("p (h e) -> p h e", h=4), k.ps[:, 0:4, :]).then_inc(o_copied, 1)
                dve.wait_ge(rstd_ready, 1)
                for t in range(TT):
                    for h in range(4):
                        o = v[:, t, h * 512:(h + 1) * 512]
                        i = 4 * t + h
                        last = dve.scalar_tensor_tensor(out=o, in0=o, scalar=rstd[:, i:i + 1], in1=k.row("gla_out_g"),
                                                        op0=ALU.mult, op1=ALU.mult)
                last.then_inc(o_normed, 1)
                for r in range(2):
                    dve.wait_ge(turned, KD * (r + 1))
                    z = a["zT"][:, 8 * r:8 * r + 8, :]
                    dve.tensor_tensor(z, z, k.ps[:, 4 * r:4 * r + 4, :].rearrange("p b (f t) -> p (b f) t", f=2), ALU.mult)

            @block.scalar
            def _(act):
                act.wait_ge(tile_out, 1)
                act.wait_ge(o_copied, 1)
                for t in range(TT):
                    for h in range(4):
                        i = 4 * t + h
                        act.activation(junk[:], v[:, t, h * 512:(h + 1) * 512], ACT.Square,
                                       accum_out=ss[:, i:i + 1]).then_inc(summed, 1)
                        act.drain()

            @block.gpsimd
            def _(pool):
                pool.wait_ge(summed, 8)
                rsqrt_mean(k, pool, rstd[:], ss[:], 512).then_inc(rstd_ready, 1)


def stage_memory_attention(k, a, name):
    with ExitStack() as ctx:
        p = k.sb(f"{name}_p", [P, 8, TOK], ctx=ctx)
        pT = k.sb(f"{name}_pT", [P, 4, 2, TOK], ctx=ctx)
        mx = k.sb(f"{name}_mx", [P, 8], ctx=ctx)
        rs = k.sb(f"{name}_rs", [P, 8], ctx=ctx)
        scored, max_ready, exp_done, p_ready, turned, pT_ready, out_done = (
            k.sem(f"{name}_{s}") for s in ("scored", "max_ready", "exp_done", "p_ready", "p_turned", "pT_ready", "out_done"))
        s_ps = k.ps[:, 0:4, :].rearrange("p h (t m) -> p (h t) m", t=2)
        t_ps = k.ps[:, 4:8, :].rearrange("p h (m t) -> p h m t", m=2)
        o_ps = k.ps[:, 0:4, :].rearrange("p b (f t) -> p (b f) t", f=2)
        with k.nc.Block() as block:
            @block.tensor
            def _(pe):
                for h in range(4):
                    for t in range(TT):
                        for c in range(2):
                            last = pe.matmul(s_ps[:, 2 * h + t, :], a["xqT"][:, 2 * h + c, t * P:(t + 1) * P],
                                             a["kmT"][:, 2 * h + c, :], start=(c == 0), stop=(c == 1))
                last.then_inc(scored, 1)
                pe.wait_ge(p_ready, 1)
                for h in range(4):
                    for m in range(2):
                        for t in range(TT):
                            last = pe.transpose(t_ps[:, h, m, t * P:(t + 1) * P], p[:, 2 * h + t, m * P:(m + 1) * P],
                                                k.c("ident"))
                last.then_inc(turned, 1)
                pe.wait_ge(pT_ready, 1)
                for f in range(8):
                    for m in range(2):
                        last = pe.matmul(o_ps[:, f, :], a["vm"][:, m, f * P:(f + 1) * P], pT[:, f // 2, m, :],
                                         start=(m == 0), stop=(m == 1))
                last.then_inc(out_done, 1)

            @block.scalar
            def _(act):
                act.wait_ge(max_ready, 1)
                for i in range(8):
                    last = act.activation(p[:, i, :], s_ps[:, i, :], ACT.Exp, bias=mx[:, i:i + 1], scale=1.0 / 16.0,
                                          accum_out=rs[:, i:i + 1])
                last.then_inc(exp_done, 1)

            @block.vector
            def _(dve):
                dve.wait_ge(scored, 1)
                dve.tensor_reduce(mx[:], s_ps[:], AX, ALU.max)
                dve.drain()
                dve.tensor_scalar(mx[:], mx[:], -1.0 / 16.0, None, ALU.mult).then_inc(max_ready, 1)
                dve.wait_ge(exp_done, 1)
                dve.reciprocal(rs[:], rs[:])
                dve.drain()
                for i in range(8):
                    last = dve.tensor_scalar(p[:, i, :], p[:, i, :], rs[:, i:i + 1], None, ALU.mult)
                last.then_inc(p_ready, 1)
                dve.wait_ge(turned, 1)
                dve.tensor_copy(pT[:], t_ps[:]).then_inc(pT_ready, 1)
                dve.wait_ge(out_done, 1)
                z = a["zT"][:, 16:24, :]
                dve.tensor_tensor(z, z, o_ps[:], ALU.mult)


def out_specs(k, zT):
    return [("tm", zT, 8 * kb, "dve", add_after(k.x[:, :, n * 512:(n + 1) * 512])) for n in range(2) for kb in range(3)]


def gla_layer(k):
    with ExitStack() as ctx:
        sb = lambda n, s: k.sb(n, s, ctx=ctx)
        a = {"zT": sb("gla_zT", [P, 24, TOK])}
        with ExitStack() as mid:
            sm = lambda n, s: k.sb(n, s, ctx=mid)
            a |= {"xqT": sm("gla_xqT", [P, 8, TOK]), "kmT": sm("gla_kmT", [P, 8, TOK]), "vm": sm("gla_vm", [P, TT, 1024])}
            with ExitStack() as inner:
                si = lambda n, s: k.sb(n, s, ctx=inner)
                a |= {"w_rank": si("w_rank", [P, KD, 16]), "w_up": si("w_up", [16, 512]),
                      "qk": si("gla_qk", [P, TT, 1024]), "v": si("gla_v", [P, TT, 2048])}
                low_in = k.sem("low_rank_in")

                def load(sp):
                    sp.dma_start(a["w_rank"][:], k.dram["w_rank"]).then_inc(low_in, 16)
                    sp.dma_start(a["w_up"][:], k.dram["w_up"]).then_inc(low_in, 16)
                    sp.wait_ge(low_in, 32)

                zf = lambda m: a["zT"][:, 4 * m:4 * m + 4, :]
                specs = [("tm", k.hT, 0, "dve", copy_to(a["qk"][:, :, m * 512:(m + 1) * 512])) for m in range(2)]
                specs += [("tm", k.hT, 0, "dve", copy_to(a["v"][:, :, m * 512:(m + 1) * 512])) for m in range(4)]
                specs += [("fm", k.hT, 0, "act", silu_to(zf(m))) for m in range(6)]
                specs += [("fm", k.hT, 0, "dve", copy_to(a["xqT"][:, 4 * m:4 * m + 4, :])) for m in range(2)]
                specs += [("fm", k.memT, 0, "dve", copy_to(a["kmT"][:, 4 * m:4 * m + 4, :])) for m in range(2)]
                specs += [("tm", k.memT, 0, "dve", copy_to(a["vm"][:, :, m * 512:(m + 1) * 512])) for m in range(2)]
                stage_tiles(k, "gla_in", T_GLA, specs, sp_extra=load)
                with ExitStack() as rec:
                    sr = lambda n, s: k.sb(n, s, ctx=rec)
                    a |= {"k_inv": sr("k_inv", [P, TT, 512]), "decay": sr("decay", [P, 16]),
                          "state": None, "qT": k.hT[:, 0:4, :], "kT": k.hT[:, 4:8, :], "att": sr("att", [P, 8, P])}
                    stage_gla_gate(k, a)
                    a["state"] = sr("state", [P, 4, 512])
                    stage_gla(k, a)
            stage_memory_attention(k, a, "xa0")
        stage_tiles(k, "gla_out", T_GLA_OUT, out_specs(k, a["zT"]))
        xn = k.sb("xn3", [P, TT, D], ctx=ctx)
        norm_stage(k, NormT(k, "s5_norm", k.x, ctx, xn), k.col("norm_w_2", 8, KD))


def norm_stage(k, norm, gain):
    with k.nc.Block() as block:
        @block.scalar
        def _(act):
            norm.act(act)

        @block.gpsimd
        def _(pool):
            norm.pool(pool)

        @block.vector
        def _(dve):
            norm.dve_scale(dve)
            norm.dve_out(dve, k.hT, gain)

        @block.tensor
        def _(pe):
            norm.pe(pe)


def stage_s5_discretize(k, a):
    n = 1024
    with ExitStack() as ctx:
        sb = lambda name, w: k.sb(name, [P, w], ctx=ctx)
        lr, li, ls, dt = sb("lam_re", n), sb("lam_im", n), sb("log_step", 16), sb("dt", 16)
        mag, th, s, c, t1, t2 = (sb(f"s5_{x}", n) for x in ("mag", "th", "sin", "cos", "t1", "t2"))
        lrs, lis, lss = sb("lam_re_s", 64), sb("lam_im_s", 64), sb("log_step_s", 64)
        ts, red = sb("theta_s", 64), sb("theta_red", 64)
        lam_in, dt_ready, args_ready, trig_ready = (k.sem(x) for x in ("lam_in", "dt_ready", "s5_args_ready", "s5_trig_ready"))
        by_tile = lambda x: x[:].rearrange("p (f s) -> p f s", f=16)
        with k.nc.Block() as block:
            @block.sync
            def _(sp):
                for dst, name in ((lr, "lam_re_f"), (li, "lam_im_f"), (ls, "log_step_f"), (lrs, "lam_re_s"),
                                  (lis, "lam_im_s"), (lss, "log_step_s")):
                    sp.dma_start(dst[:], k.dram[name]).then_inc(lam_in, 16)

            @block.scalar
            def _(act):
                act.wait_ge(lam_in, 96)
                act.activation(dt[:], ls[:], ACT.Exp)
                act.activation(lss[:], lss[:], ACT.Exp).then_inc(dt_ready, 1)
                act.wait_ge(args_ready, 1)
                act.activation(mag[:], mag[:], ACT.Exp)
                act.activation(a["decay"][:], a["decay"][:], ACT.Exp)
                act.activation(s[:], th[:], ACT.Sin)
                act.activation(c[:], c[:], ACT.Sin).then_inc(trig_ready, 1)

            @block.vector
            def _(dve):
                dve.wait_ge(dt_ready, 1)
                dtb = bc(dt[:], 2, 64)
                dve.tensor_tensor(by_tile(mag), by_tile(lr), dtb, ALU.mult)
                dve.tensor_tensor(by_tile(t1), by_tile(li), dtb, ALU.mult)
                dve.tensor_tensor(a["decay"][:], lrs[:], lss[:], ALU.mult)
                dve.tensor_tensor(ts[:], lis[:], lss[:], ALU.mult)
                dve.drain()
                range_reduce(dve, th[:], t2[:], t1[:])
                dve.drain()
                quarter_turn(dve, c[:], t2[:], th[:])
                dve.drain()
                range_reduce(dve, red[:], lss[:], ts[:])
                dve.drain()
                dve.tensor_scalar(a["turns"][:], red[:], 1.0 / TWO_PI, None, ALU.mult).then_inc(args_ready, 1)
                dve.wait_ge(trig_ready, 1)
                dve.tensor_tensor(c[:], c[:], mag[:], ALU.mult)
                dve.tensor_tensor(s[:], s[:], mag[:], ALU.mult)
                dve.tensor_tensor(t1[:], lr[:], lr[:], ALU.mult)
                dve.tensor_tensor(t2[:], li[:], li[:], ALU.mult)
                dve.drain()
                dve.tensor_scalar(c[:], c[:], -1.0, None, ALU.add)
                dve.tensor_tensor(t1[:], t1[:], t2[:], ALU.add)
                dve.drain()
                dve.reciprocal(t1[:], t1[:])
                dve.tensor_tensor(mag[:], c[:], lr[:], ALU.mult)
                dve.tensor_tensor(th[:], s[:], li[:], ALU.mult)
                dve.drain()
                dve.tensor_tensor(mag[:], mag[:], th[:], ALU.add)
                dve.tensor_tensor(s[:], s[:], lr[:], ALU.mult)
                dve.tensor_tensor(c[:], c[:], li[:], ALU.mult)
                dve.drain()
                dve.tensor_tensor(a["coef_re"][:], mag[:], t1[:], ALU.mult)
                dve.tensor_tensor(s[:], s[:], c[:], ALU.subtract)
                dve.drain()
                dve.tensor_tensor(a["coef_im"][:], s[:], t1[:], ALU.mult)


def stage_s5_scan(k, a):
    with ExitStack() as ctx:
        sb = lambda name, s: k.sb(name, s, ctx=ctx)
        braw, bb = sb("b_raw", [P, 2, 2, P]), sb("b_bar", [P, 2, 2, P])
        craw = sb("c_raw", [P, 2, 4, 2, 32])
        bt = sb("b_tmp", [P, P])
        ang, frac, sin, cos = (sb(f"s5_{x}", [P, 4, TOK]) for x in ("angle", "frac", "sin_t", "cos_t"))
        p1, p2, zr, zi, xr, xi = (sb(f"s5_{x}", [P, 4, TOK]) for x in ("p1", "p2", "z_re", "z_im", "x_re", "x_im"))
        bc_in = [k.sem(f"bc_in_{i}") for i in range(2)]
        bb_ready, bu_done, u_staged, frac_ready, trig, x_ready, y_done, y_out = (
            k.sem(f"s5_{x}") for x in ("b_bar_ready", "bu_done", "u_staged", "frac_ready", "trig", "x_ready", "y_done", "y_out"))
        iota = bc(k.c("iota256"), 1, 4)
        with k.nc.Block() as block:
            @block.sync
            def _(sp):
                with sp.Fori(0, 8) as i:
                    for j in range(2):
                        f = i * 2 + j
                        sp.wait_ge(y_out, i * 2 + (1 + j))
                        sp.dma_start(braw[:, j], k.dram["s5_b"][bass.ds(f, 1)].rearrange("a p c s -> (a p) c s")).then_inc(bc_in[j], 16)
                        sp.dma_start(craw[:, j], k.dram["s5_c"][bass.ds(f, 1)].rearrange("a p q c h -> (a p) q c h")).then_inc(bc_in[j], 16)

            @block.gpsimd
            def _(pool):
                with pool.Fori(0, 8) as i:
                    for j in range(2):
                        pool.wait_ge(bc_in[j], i * 32 + 32)
                        pool.wait_ge(y_out, i * 2 + (1 + j))
                        cr, ci = (bc(a[x][:, bass.ds(i * 128 + 64 * j, 64)], 1, 2) for x in ("coef_re", "coef_im"))
                        b_re, b_im = (braw[:, j, x].rearrange("p (g s) -> p g s", g=2) for x in range(2))
                        o_re, o_im = (bb[:, j, x].rearrange("p (g s) -> p g s", g=2) for x in range(2))
                        tmp = bt[:].rearrange("p (g s) -> p g s", g=2)
                        pool.tensor_tensor(o_re, b_re, cr, ALU.mult)
                        pool.tensor_tensor(tmp, b_im, ci, ALU.mult)
                        pool.drain()
                        pool.tensor_tensor(o_re, o_re, tmp, ALU.subtract)
                        pool.drain()
                        pool.tensor_tensor(o_im, b_im, cr, ALU.mult)
                        pool.tensor_tensor(tmp, b_re, ci, ALU.mult)
                        pool.drain()
                        pool.tensor_tensor(o_im, o_im, tmp, ALU.add).then_inc(bb_ready, 1)
                        pool.drain()

            @block.tensor
            def _(pe):
                with pe.Fori(0, 8) as i:
                    for j in range(2):
                        pe.wait_ge(bb_ready, i * 2 + (1 + j))
                        pe.wait_ge(u_staged, i * 2 + (1 + j))
                        for q in range(4):
                            r = slice(32 * q, 32 * q + 32)
                            for c in range(2):
                                last = pe.matmul(k.ps[:, q, c * TOK:(c + 1) * TOK], bb[r, j, c, :], a["u_stage"][r, j, :],
                                                 start=True, stop=True)
                        last.then_inc(bu_done, 1)
                        pe.wait_ge(x_ready, i * 2 + (1 + j))
                        for q in range(4):
                            o = k.ps[32 * q:32 * q + 32, 4 + j, 0:TOK]
                            pe.matmul(o, craw[:, j, q, 0, :], xr[:, q, :], start=True, stop=False)
                            last = pe.matmul(o, craw[:, j, q, 1, :], xi[:, q, :], start=False, stop=True)
                        last.then_inc(y_done, 1)

            @block.scalar
            def _(act):
                with act.Fori(0, 8) as i:
                    for j in range(2):
                        act.wait_ge(frac_ready, i * 2 + (1 + j))
                        act.activation(sin[:], frac[:], ACT.Sin, scale=6.2831845)
                        act.activation(cos[:], ang[:], ACT.Sin, scale=-6.2831845, bias=a["half_pi"][:]).then_inc(trig, 1)

            @block.vector
            def _(dve):
                dve.sem_inc(y_out, 2)
                with dve.Fori(0, 8) as i:
                    for j in range(2):
                        dve.tensor_tensor(ang[:], bc(a["turns"][:, bass.ds(i * 8 + 4 * j, 4)], 2, TOK), iota, ALU.mult)
                        dve.tensor_copy(a["u_stage"][:, j, :], a["uT"][:, bass.ds(i * 2 + j, 1), :].rearrange("p a t -> p (a t)")).then_inc(u_staged, 1)
                        dve.drain()
                        dve.tensor_scalar(frac[:], ang[:], ROUND, -ROUND, ALU.add, ALU.add)
                        dve.drain()
                        dve.tensor_tensor(frac[:], ang[:], frac[:], ALU.subtract)
                        dve.drain()
                        dve.scalar_tensor_tensor(out=ang[:], in0=frac[:], scalar=-1.0, in1=frac[:], op0=ALU.mult,
                                                 op1=ALU.max).then_inc(frac_ready, 1)
                        dve.wait_ge(trig, i * 2 + (1 + j))
                        dve.wait_ge(bu_done, i * 2 + (1 + j))
                        bur, bui = (k.ps[:, 0:4, c * TOK:(c + 1) * TOK] for c in range(2))
                        dve.tensor_tensor(p1[:], bur, cos[:], ALU.mult)
                        dve.tensor_tensor(p2[:], bui, sin[:], ALU.mult)
                        dve.tensor_tensor(zi[:], bui, cos[:], ALU.mult)
                        dve.tensor_tensor(zr[:], bur, sin[:], ALU.mult)
                        dve.drain()
                        dve.tensor_tensor(zi[:], zi[:], zr[:], ALU.subtract)
                        dve.drain()
                        dve.tensor_tensor(zr[:], p1[:], p2[:], ALU.add)
                        dve.drain()
                        for q in range(4):
                            r = a["decay"][:, bass.ds(i * 8 + (4 * j + q), 1)].broadcast_to([P, TOK])
                            dve.tensor_tensor_scan(p1[:, q, :], r, zr[:, q, :], 0.0, ALU.mult, ALU.add)
                            dve.tensor_tensor_scan(p2[:, q, :], r, zi[:, q, :], 0.0, ALU.mult, ALU.add)
                        dve.drain()
                        dve.tensor_tensor(xr[:], p1[:], cos[:], ALU.mult)
                        dve.tensor_tensor(zr[:], p2[:], sin[:], ALU.mult)
                        dve.tensor_tensor(xi[:], p2[:], cos[:], ALU.mult)
                        dve.tensor_tensor(zi[:], p1[:], sin[:], ALU.mult)
                        dve.drain()
                        dve.tensor_tensor(xr[:], xr[:], zr[:], ALU.subtract)
                        dve.scalar_tensor_tensor(out=xi[:], in0=xi[:], scalar=-1.0, in1=zi[:], op0=ALU.mult,
                                                 op1=ALU.subtract).then_inc(x_ready, 1)
                        dve.wait_ge(y_done, i * 2 + (1 + j))
                        u = a["uT"][:, bass.ds(i * 2 + j, 1), :].rearrange("p a t -> p (a t)")
                        dve.scalar_tensor_tensor(out=u, in0=u, scalar=k.cols[:, bass.ds(i * 2 + (COLS["s5_d"][0] + j), 1)],
                                                 in1=k.ps[:, 4 + j, 0:TOK], op0=ALU.mult, op1=ALU.add).then_inc(y_out, 1)


def stage_glu_gate(k, a):
    sig_ready, gated = k.sem("sig_ready"), k.sem("y_gated")
    with k.nc.Block() as block:
        @block.scalar
        def _(act):
            for f in range(16):
                act.activation(a["glu"][:, f, :], a["glu"][:, f, :], ACT.Sigmoid, bias=k.col("s5_b_glu", f)).then_inc(sig_ready, 1)

        @block.vector
        def _(dve):
            z = a["zT"][:, 0:16, :]
            dve.tensor_tensor(z, z, a["uT"][:], ALU.mult)
            dve.wait_ge(sig_ready, 16)
            dve.drain()
            dve.tensor_tensor(z, z, a["glu"][:], ALU.mult)


def stage_gelu(k, a):
    with k.nc.Block() as block:
        @block.scalar
        def _(act):
            act.activation(a["uT"][:], a["uT"][:], ACT.Gelu_apprx_tanh)


def s5_layer(k):
    with ExitStack() as ctx:
        uT = k.sb("uT", [P, 16, TOK], ctx=ctx)
        a = {"uT": uT}
        stage_tiles(k, "s5_u", T_S5, [("fm", k.hT, 0, "dve", copy_to(uT[:, 4 * m:4 * m + 4, :])) for m in range(4)])
        with ExitStack() as rec:
            for n in ("coef_re", "coef_im"):
                a[n] = k.sb(n, [P, 1024], ctx=rec)
            a["decay"], a["turns"] = k.sb("s5_decay", [P, 64], ctx=rec), k.sb("s5_turns", [P, 64], ctx=rec)
            a["half_pi"] = k.sb("half_pi", [P, 1], ctx=rec)
            a["u_stage"] = k.sb("u_stage", [P, 2, TOK], ctx=rec)
            with k.nc.Block() as block:
                @block.vector
                def _(dve):
                    dve.memset(a["half_pi"][:], float(np.pi / 2))
            stage_s5_discretize(k, a)
            stage_s5_scan(k, a)
        stage_gelu(k, a)
        a["zT"] = k.sb("s5_zT", [P, 24, TOK], ctx=ctx)
        with ExitStack() as mid:
            sm = lambda n, s: k.sb(n, s, ctx=mid)
            a |= {"xqT": sm("s5_xqT", [P, 8, TOK]), "kmT": sm("s5_kmT", [P, 8, TOK]), "vm": sm("s5_vm", [P, TT, 1024])}
            zf = lambda m: a["zT"][:, 4 * m:4 * m + 4, :]
            specs = [("fm", k.hT, 0, "act", silu_to(zf(m))) for m in range(6)]
            specs += [("fm", k.hT, 0, "dve", copy_to(a["xqT"][:, 4 * m:4 * m + 4, :])) for m in range(2)]
            specs += [("fm", k.memT, 0, "dve", copy_to(a["kmT"][:, 4 * m:4 * m + 4, :])) for m in range(2)]
            specs += [("tm", k.memT, 0, "dve", copy_to(a["vm"][:, :, m * 512:(m + 1) * 512])) for m in range(2)]
            stage_tiles(k, "s5_in", T_S5 + 4, specs)
            stage_memory_attention(k, a, "xa1")
        a["glu"] = k.sb("glu", [P, 16, TOK], ctx=ctx)
        specs = []
        for n in range(4):
            g = a["glu"][:, 4 * n:4 * n + 4, :]
            specs += [("fm", uT, 0, "dve", copy_to(g)), ("fm", uT, 8, "dve", add_after(g))]
        stage_tiles(k, "glu", T_GLU, specs)
        stage_glu_gate(k, a)
        stage_tiles(k, "s5_out", T_S5_OUT, out_specs(k, a["zT"]))


def final_norm(k):
    with ExitStack() as ctx:
        xn = k.sb("xn4", [P, TT, D], ctx=ctx)
        norm = NormT(k, "final", k.x, ctx, xn)
        with k.nc.Block() as block:
            @block.scalar
            def _(act):
                norm.act(act)

            @block.gpsimd
            def _(pool):
                norm.pool(pool)

            @block.vector
            def _(dve):
                dve.wait_ge(norm.rstd_ready, 1)
                for t in range(TT):
                    dve.scalar_tensor_tensor(out=k.x[:, t, :], in0=k.x[:, t, :], scalar=norm.rstd[:, t:t + 1],
                                             in1=k.row("final_norm"), op0=ALU.mult, op1=ALU.mult)


def build(nc, dram, out):
    with ExitStack() as ctx:
        k = Core(nc, ctx, dram)
        first_block(k)
        k.clear_stage_sems()
        gla_layer(k)
        s5_layer(k)
        final_norm(k)
        store(k, out)


def store(k, out):
    stored = k.sem("stored")
    with k.nc.Block() as block:
        @block.sync
        def _(sp):
            sp.dma_start(out.rearrange("a (t p) d -> p (a t) d", p=P), k.x[:]).then_inc(stored, 16)
            sp.wait_ge(stored, 16)



def constants():
    c = np.zeros((P, N_CONST), np.float32)
    p = np.arange(P)

    def put(name, value):
        a, b = CONSTS[name]
        c[:, a:b] = np.asarray(value, np.float32).reshape(P, -1)

    put("ident", np.eye(P))
    q = p[:, None, None] + P * np.arange(TT)[None, :, None]
    put("causal", np.where(np.arange(TOK)[None, None, :] <= q, 0.0, NEG))
    put("causal_t", np.where(p[:, None] <= p[None, :], 0.0, NEG))
    put("inv_freq", np.tile(np.float32(10000.0) ** (-np.arange(32, dtype=np.float32) / np.float32(32)), (P, 1)))
    put("iota32", np.tile(np.arange(32), (P, 1)))
    hot = np.zeros((P, 4, P))
    for h in range(4):
        hot[h, h] = 1.0
    put("one_hot4", hot)
    same = p[:, None] // 64 == p[None, :] // 64
    put("chunk_tri", same & (p[:, None] <= p[None, :]))
    put("chunk_suffix", same & (p[:, None] > p[None, :]))
    put("chunk_ind", p[:, None] // 64 == np.arange(2)[None, :])
    put("iota256", np.tile(np.arange(TOK), (P, 1)))
    put("minus_half", np.full((P, 16), -0.5))
    return c


def s5_arrays(g):
    lam_re, lam_im, step = g["s5_lam_re_2"][0], g["s5_lam_im_2"][0], g["s5_log_step_2"][0]

    def feature(v):
        v = v.reshape(16, 8, 1, -1)
        return np.broadcast_to(v, (16, 8, 16, v.shape[-1])).transpose(1, 2, 0, 3).reshape(P, -1)

    def state(v):
        return v.reshape(64, 2, 64).transpose(1, 2, 0).reshape(P, 64)

    b = np.zeros((16, 4, 2, 16, 2, 2, 64), np.float32)
    c = np.zeros((16, 2, 64, 4, 2, 2, 16), np.float32)
    for part, (bv, cv) in enumerate(((g["s5_b_re_2"][0], g["s5_c_re_2"][0]), (g["s5_b_im_2"][0], g["s5_c_im_2"][0]))):
        bv = bv.reshape(16, 4, 2, 64, 16)
        cv = cv.reshape(16, 4, 2, 16, 64)
        for q in range(2):
            b[:, :, q, :, part, q, :] = bv[:, :, q].transpose(0, 1, 3, 2)
            c[:, q, :, :, part, q, :] = cv[:, :, q].transpose(0, 3, 1, 2)
    return {
        "lam_re_f": feature(lam_re), "lam_im_f": feature(lam_im), "log_step_f": feature(step[:, None]),
        "lam_re_s": state(lam_re), "lam_im_s": state(lam_im),
        "log_step_s": state(np.broadcast_to(step[:, None], (P, 64))),
        "s5_b": b.reshape(16, P, 2, P), "s5_c": c.reshape(16, P, 4, 2, 32),
    }


def kernel(**inputs):
    import concourse.bacc as bacc
    from concourse.bass_utils import run_bass_kernel_spmd

    g = {n: np.asarray(v) for n, v in inputs.items()}

    def wide(w, rows=1024, width=512):
        kt, nt = w.shape[0] // rows, w.shape[1] // width
        w = w.reshape(kt, rows // P, P, nt, width).transpose(3, 0, 2, 1, 4)
        return w.reshape(nt * kt, P, TILE)

    w_in = g["w_in"][0]
    gla = g["gla_w_in_2"][0]
    ada = wide(g["w_ada"][0])
    kv = [wide(g["xa_w_kv_2"][i]) for i in range(2)]
    groups = [
        ada, wide(w_in[:, :3584]), wide(g["w_out"][0]),
        np.stack([g["w1"][0].reshape(N_EXP, KD, P, 512).transpose(0, 2, 1, 3).reshape(N_EXP, P, TILE),
                  g["w3"][0].reshape(N_EXP, KD, P, 512).transpose(0, 2, 1, 3).reshape(N_EXP, P, TILE),
                  g["w2"][0].reshape(N_EXP, 4, P, 1024).transpose(0, 2, 1, 3).reshape(N_EXP, P, TILE)],
                 axis=1).reshape(3 * N_EXP, P, TILE),
        wide(gla[:, :3072]), wide(gla[:, 3088:]), kv[0], wide(g["w_out_2"][0]),
        wide(g["s5_w_in_2"][0]), kv[1], wide(g["s5_w_glu_2"][0]), wide(g["w_out_2"][1]),
    ]
    weights = np.concatenate(groups, axis=0)
    assert weights.shape[0] == T_END

    def by_feature(v, n):
        return v.reshape(n, P).T

    cols = np.zeros((P, N_COLS), np.float32)

    def put_col(name, value):
        a, b = COLS[name]
        cols[:value.shape[0], a:b] = value

    put_col("c", by_feature(g["c"][0], 8))
    b_ada = g["b_ada"][0].reshape(6, 1024)
    put_col("b_ada", by_feature(np.concatenate([b_ada[0], b_ada[1], b_ada[3], b_ada[4]]), 32))
    put_col("norm1_g", by_feature(g["norm1_g"][0], 8))
    put_col("norm2_g", by_feature(g["norm2_g"][0], 8))
    put_col("conv_w", g["conv_w"][0].reshape(4, 8, P).transpose(2, 1, 0).reshape(P, 32))
    put_col("conv_b", by_feature(g["conv_b"][0], 8))
    put_col("norm_w_2", by_feature(g["norm_w_2"], 16))
    put_col("mem_norm_w", by_feature(g["mem_norm_w_2"], 8))
    put_col("s5_d", by_feature(g["s5_d_2"][0], 16))
    put_col("s5_b_glu", by_feature(g["s5_b_glu_2"][0], 16))
    put_col("b_gate", g["b_gate"][0].reshape(2, 4).T)

    rows = np.concatenate([b_ada[2], b_ada[5], g["attn_out_g"][0], g["mlstm_out_g"][0], g["norm_f_g"], g["b_rg"][0],
                           g["b_re"][0], g["gla_gate_bias_2"][0], g["gla_out_norm_w_2"][0], g["final_norm_w_2"]])
    arrays = {
        "weights": weights, "cols": cols, "rows": rows, "consts": constants(),
        "positions": g["positions"].reshape(TT, P).T,
        "x": g["x"].reshape(TT, P, D).transpose(1, 0, 2), "mem": g["mem_2"].reshape(TT, P, D).transpose(1, 0, 2),
        "w_gate": w_in[:, 3584:].reshape(KD, P, 8).transpose(1, 0, 2),
        "w_router": np.concatenate([g["w_rg"][0], g["w_re"][0]], axis=1).reshape(KD, P, 36).transpose(1, 0, 2),
        "w_rank": gla[:, 3072:3088].reshape(KD, P, 16).transpose(1, 0, 2), "w_up": g["gla_w_gate_up_2"][0],
        **s5_arrays(g),
    }
    nc = bacc.Bacc("TRN2", target_bir_lowering=False, num_devices=1)
    fed, dram = {}, {}
    for name, value in arrays.items():
        fed[f"in_{name}"] = np.ascontiguousarray(value)
        dram[name] = nc.dram_tensor(f"in_{name}", value.shape, mybir.dt.from_np(value.dtype), kind="ExternalInput").ap()
    out = nc.dram_tensor("out_0", (1, TOK, D), F32, kind="ExternalOutput").ap()
    build(nc, dram, out)
    return run_bass_kernel_spmd(nc, [fed], core_ids=[0]).results[0]["out_0"]
```

```python
from contextlib import ExitStack

import numpy as np
import concourse.bass as bass
from concourse import mybir

F32 = mybir.dt.float32
I32 = mybir.dt.int32
U32 = mybir.dt.uint32
ALU = mybir.AluOpType
ACT = mybir.ActivationFunctionType
AX = mybir.AxisListType.X

P = 128
TOK = 256
TT = TOK // P
D = 1024
KD = D // P
EPS = 1e-6
NEG = -1e30
SLOTS = 64
RING = 3
TILE = 4096
PI = 3.1415925
TWO_PI = 2.0 * np.pi
TWO_PI_A = 6.28125
TWO_PI_B = float(np.float32(int((TWO_PI - TWO_PI_A) * 2 ** 21) / 2 ** 21))
TWO_PI_C = float(np.float32(TWO_PI - TWO_PI_A - TWO_PI_B))
ROUND = 12582912.0

N_ADA, N_IN, N_OUT, N_EXP = 12, 7, 2, 32
T_ADA = 0
T_IN = T_ADA + N_ADA
T_OUT = T_IN + N_IN
T_GLA = T_OUT + N_OUT
T_GLA_OUT = T_GLA + 18
T_S5 = T_GLA_OUT + 6
T_GLU = T_S5 + 16
T_S5_OUT = T_GLU + 8
T_END = T_S5_OUT + 6

CONSTS = {}
_at = 0
for _name, _n in (("ident", 128), ("causal", 512), ("causal_t", 128), ("inv_freq", 32), ("iota64", 64),
                  ("one_hot4", 512), ("chunk_tri", 128), ("chunk_suffix", 128), ("chunk_ind", 2),
                  ("iota256", 256), ("minus_half", 16),
                  ("before", 128), ("ones", 128), ("slot_limits", 3)):
    CONSTS[_name] = (_at, _at + _n)
    _at += _n
N_CONST = _at

COLS = {}
_at = 0
for _name, _n in (("c", 8), ("b_ada", 32), ("norm1_g", 8), ("norm2_g", 8), ("conv_w", 32), ("conv_b", 8),
                  ("norm_w_2", 16), ("mem_norm_w", 8), ("s5_d", 16), ("s5_b_glu", 16), ("b_gate", 2)):
    COLS[_name] = (_at, _at + _n)
    _at += _n
N_COLS = _at

ROWS = {}
_at = 0
for _name, _n in (("b_g1", 1024), ("b_g2", 1024), ("attn_out_g", 512), ("mlstm_out_g", 512), ("norm_f_g", 1024),
                  ("b_router", 36), ("gla_bias", 512), ("gla_out_g", 512), ("final_norm", 1024)):
    ROWS[_name] = (_at, _at + _n)
    _at += _n
N_ROWS = _at


class Core:

    def __init__(self, nc, ctx, dram):
        self.nc, self.ctx, self.dram = nc, ctx, dram
        self.ring = self.sb("ring", [P, RING, TILE])
        self.const = self.sb("const", [P, N_CONST])
        self.cols = self.sb("cols", [P, N_COLS])
        self.x = self.sb("x", [P, TT, D])
        self.hT = self.sb("hT", [P, KD, TOK])
        self.memT = self.sb("memT", [P, KD, TOK])
        self.small = self.sb("small", [P, 64])
        self.sin = self.sb("sin", [P, TT, 32])
        self.cos = self.sb("cos", [P, TT, 32])
        self.mod = self.sb("mod", [P, 32])
        self.ps = ctx.enter_context(nc.psum_tensor("ps", [P, 8, 512], F32))
        self.stage_sems = None
        self.landed = [self.sem(f"weights_landed_{j}") for j in range(RING)]
        self.tile_done = self.sem("tile_done")
        self.stage_sems = []

    def sb(self, name, shape, dt=F32, ctx=None):
        return (ctx or self.ctx).enter_context(self.nc.sbuf_tensor(name, shape, dt))

    def sem(self, name):
        if self.stage_sems is None:
            return self.ctx.enter_context(self.nc.semaphore(name))
        self.stage_sems.append(self.nc.alloc_semaphore(name))
        return self.stage_sems[-1]

    def clear_stage_sems(self):
        self.nc.clear_and_free_semaphores(self.stage_sems)
        self.nc.all_engine_barrier()
        self.stage_sems = []

    def c(self, name):
        a, b = CONSTS[name]
        return self.const[:, a:b]

    def col(self, name, i=0, n=1):
        a = COLS[name][0] + i
        return self.cols[:, a:a + n]

    def hold_rows(self, names, ctx):
        self.row_base, end = ROWS[names[0]][0], ROWS[names[-1]][1]
        self.rows = self.sb(f"rows_{names[0]}", [P, end - self.row_base], ctx=ctx)
        return self.rows[:], self.dram["rows"][self.row_base:end].partition_broadcast(P)

    def row(self, name):
        a, b = ROWS[name]
        return self.rows[:, a - self.row_base:b - self.row_base]

    def slot(self, n, k=8):
        return self.ring[:, n % RING, :].rearrange("p (k n) -> p k n", k=k)

    def wait_tile(self, pe, n):
        pe.wait_ge(self.landed[n % RING], 16 * (n // RING + 1))


def bc(ap, axis, n):
    ap = ap.unsqueeze(axis)
    shape = list(ap.shape)
    shape[axis] = n
    return ap.broadcast_to(shape)


def stream(k, sp, used_from, used_to):
    n0, n1 = used_from + RING, min(used_to + RING, T_END)
    if used_to < T_GLA:
        n1 = min(n1, T_GLA)

    def load(n, j):
        sp.wait_ge(k.tile_done, n - (RING - 1))
        sp.dma_start(k.ring[:, j, :], k.dram["weights"][n]).then_inc(k.landed[j], 16)

    body = (n1 - n0) // RING
    if body > 1:
        with sp.Fori(0, body) as i:
            for j in range(RING):
                sp.wait_ge(k.tile_done, i * RING + (n0 + j - (RING - 1)))
                sp.dma_start(k.ring[:, (n0 + j) % RING, :],
                             k.dram["weights"][bass.ds(i * RING + (n0 + j), 1)].rearrange("a p n -> (a p) n")
                             ).then_inc(k.landed[(n0 + j) % RING], 16)
        n0 += body * RING
    for n in range(n0, n1):
        load(n, n % RING)


def tm_tile(k, pe, n, lhs, out, k0=0):
    k.wait_tile(pe, n)
    w = k.slot(n)
    for t in range(TT):
        for kk in range(KD):
            last = pe.matmul(out[:, t, :], lhs[:, k0 + kk, t * P:(t + 1) * P], w[:, kk, :],
                             start=(kk == 0), stop=(kk == KD - 1))
    last.then_inc(k.tile_done, 1)


def fm_tile(k, pe, n, rhs, out, k0=0):
    k.wait_tile(pe, n)
    w = k.slot(n)
    for f in range(4):
        for kk in range(KD):
            last = pe.matmul(out[:, f, :], w[:, kk, f * P:(f + 1) * P], rhs[:, k0 + kk, :],
                             start=(kk == 0), stop=(kk == KD - 1))
    last.then_inc(k.tile_done, 1)


def pair(k, m):
    j = m % 3
    return k.ps[:, 2 * j:2 * j + 2, :]


def pair_fm(k, m):
    return pair(k, m).rearrange("p b (f t) -> p (b f) t", f=2)


class NormT:

    def __init__(self, k, name, x, ctx, xn):
        self.k, self.x, self.xn = k, x, xn
        self.ss = k.sb(f"{name}_ss", [P, TT], ctx=ctx)
        self.rstd = k.sb(f"{name}_rstd", [P, TT], ctx=ctx)
        self.summed = k.sem(f"{name}_squares_summed")
        self.rstd_ready = k.sem(f"{name}_rstd_ready")
        self.scaled = k.sem(f"{name}_scaled")
        self.turned = k.sem(f"{name}_turned")
        self.done = k.sem(f"{name}_done")

    def act(self, act):
        for t in range(TT):
            act.activation(self.xn[:, t, :], self.x[:, t, :], ACT.Square,
                           accum_out=self.ss[:, t:t + 1]).then_inc(self.summed, 1)

    def pool(self, pool):
        pool.wait_ge(self.summed, TT)
        rsqrt_mean(self.k, pool, self.rstd[:], self.ss[:], D).then_inc(self.rstd_ready, 1)

    def dve_scale(self, dve):
        dve.wait_ge(self.rstd_ready, 1)
        for t in range(TT):
            dve.tensor_scalar(self.xn[:, t, :], self.x[:, t, :], self.rstd[:, t:t + 1], None,
                              ALU.mult).then_inc(self.scaled, 1)

    def pe(self, pe):
        pe.wait_ge(self.scaled, TT)
        turn(self.k, pe, self.xn, KD, self.k.ps[:, 0:4, :].rearrange("p b (f t) -> p (b f) t", f=2), self.turned)

    def dve_out(self, dve, out, scale, shift=None):
        dve.wait_ge(self.turned, KD)
        src = self.k.ps[:, 0:4, :].rearrange("p b (f t) -> p (b f) t", f=2)
        for f in range(KD):
            dve.tensor_scalar(out[:, f, :], src[:, f, :], scale[:, f:f + 1],
                              None if shift is None else shift[:, f:f + 1], ALU.mult,
                              *(() if shift is None else (ALU.add,))).then_inc(self.done, 1)


def rsqrt_mean(k, pool, out, ss, width, eps=EPS):
    pool.tensor_scalar(out, ss, 1.0 / width, eps, ALU.mult, ALU.add)
    pool.drain()
    n = out.shape[-1]
    return pool.tensor_tensor(out=out, in0=out, in1=k.c("minus_half")[:, 0:n], op=ALU.pow)


def turn(k, pe, src, nf, dst, turned):
    for f in range(nf):
        for t in range(TT):
            last = pe.transpose(dst[:, f, t * P:(t + 1) * P], src[:, t, f * P:(f + 1) * P], k.c("ident"))
        last.then_inc(turned, 1)


def range_reduce(dve, r, n, ang):
    dve.tensor_scalar(n, ang, 1.0 / TWO_PI, ROUND, ALU.mult, ALU.add)
    dve.drain()
    dve.tensor_scalar(n, n, -ROUND, None, ALU.add)
    dve.drain()
    dve.scalar_tensor_tensor(out=r, in0=n, scalar=-TWO_PI_A, in1=ang, op0=ALU.mult, op1=ALU.add)
    dve.drain()
    dve.scalar_tensor_tensor(out=r, in0=n, scalar=-TWO_PI_B, in1=r, op0=ALU.mult, op1=ALU.add)
    dve.drain()
    dve.scalar_tensor_tensor(out=r, in0=n, scalar=-TWO_PI_C, in1=r, op0=ALU.mult, op1=ALU.add)
    dve.drain()
    return dve.tensor_scalar(r, r, PI, -PI, ALU.min, ALU.max)


def quarter_turn(dve, r, n, angle):
    dve.tensor_scalar(n, angle, PI / 2, -TWO_PI, ALU.is_gt, ALU.mult)
    dve.tensor_scalar(r, angle, float(np.pi / 2), None, ALU.add)
    dve.drain()
    dve.tensor_tensor(r, r, n, ALU.add)
    dve.drain()
    return dve.tensor_scalar(r, r, PI, -PI, ALU.min, ALU.max)


def stage_modulation(k, rows):
    nc, d = k.nc, k.dram
    with ExitStack() as ctx:
        csil = k.sb("csil", [P, KD], ctx=ctx)
        cexp = k.sb("cexp", [P, KD], ctx=ctx)
        crep = k.sb("crep", [P, KD, P], ctx=ctx)
        pos = k.sb("pos", [P, TT], I32, ctx=ctx)
        posf = k.sb("posf", [P, TT], ctx=ctx)
        ang = k.sb("ang", [P, TT, 32], ctx=ctx)
        red = k.sb("red", [P, TT, 32], ctx=ctx)
        redc = k.sb("redc", [P, TT, 32], ctx=ctx)
        turns = k.sb("turns", [P, TT, 32], ctx=ctx)
        mem = k.sb("mem", [P, TT, D], ctx=ctx)
        xn = k.sb("xn0", [P, TT, D], ctx=ctx)
        memn = k.sb("memn", [P, TT, D], ctx=ctx)
        norm_m = NormT(k, "mem_norm", mem, ctx, memn)
        norm_x = NormT(k, "norm1", k.x, ctx, xn)
        small_in, rows_in, x_in, mem_in, pos_in = (k.sem(s) for s in ("small_in", "rows_in", "x_in", "mem_in", "pos_in"))
        cexp_ready, csil_ready, row_out, angles_ready, tables_ready, cols_done = (
            k.sem(s) for s in ("cexp_ready", "csil_ready", "gate_rows_out", "angles_ready", "tables_ready", "cols_done"))
        mod_ps, row_ps = k.ps[:, 6, :], k.ps[:, 4:6, :]

        with nc.Block() as block:
            @block.sync
            def _(sp):
                sp.dma_start(k.cols[:], d["cols"]).then_inc(small_in, 16)
                sp.dma_start(k.const[:], d["consts"]).then_inc(small_in, 16)
                for n in range(RING):
                    sp.dma_start(k.ring[:, n, :], d["weights"][n]).then_inc(k.landed[n], 16)
                sp.dma_start(pos[:], d["positions"]).then_inc(pos_in, 16)
                sp.dma_start(mem[:], d["mem"]).then_inc(mem_in, 16)
                sp.dma_start(k.x[:], d["x"]).then_inc(x_in, 16)
                sp.dma_start(*rows).then_inc(rows_in, 16)
                stream(k, sp, T_ADA, T_ADA + N_ADA)

            @block.scalar
            def _(act):
                act.wait_ge(small_in, 32)
                act.activation(cexp[:], k.col("c", 0, KD), ACT.Exp, scale=-1.0).then_inc(cexp_ready, 1)
                act.wait_ge(mem_in, 16)
                norm_m.act(act)
                act.wait_ge(x_in, 16)
                norm_x.act(act)
                act.wait_ge(angles_ready, 2)
                act.activation(k.sin[:], red[:], ACT.Sin).then_inc(tables_ready, 1)
                act.activation(k.cos[:], redc[:], ACT.Sin).then_inc(tables_ready, 1)

            @block.gpsimd
            def _(pool):
                norm_m.pool(pool)
                norm_x.pool(pool)

            @block.vector
            def _(dve):
                dve.wait_ge(cexp_ready, 1)
                dve.tensor_scalar(cexp[:], cexp[:], 1.0, None, ALU.add)
                dve.drain()
                dve.reciprocal(cexp[:], cexp[:])
                dve.drain()
                dve.tensor_tensor(csil[:], cexp[:], k.col("c", 0, KD), ALU.mult)
                dve.drain()
                dve.tensor_copy(crep[:], bc(csil[:], 2, P)).then_inc(csil_ready, 1)
                dve.sem_inc(row_out, 1)
                dve.wait_ge(pos_in, 16)
                dve.tensor_copy(posf[:], pos[:])
                dve.drain()
                for t in range(TT):
                    dve.tensor_scalar(ang[:, t, :], k.c("inv_freq"), posf[:, t:t + 1], None, ALU.mult)
                dve.drain()
                range_reduce(dve, red[:], turns[:], ang[:]).then_inc(angles_ready, 1)
                dve.drain()
                quarter_turn(dve, redc[:], turns[:], red[:]).then_inc(angles_ready, 1)
                norm_m.dve_scale(dve)
                norm_x.dve_scale(dve)
                dve.wait_ge(rows_in, 16)
                for half, gate in enumerate(("b_g1", "b_g2")):
                    for j in range(2):
                        dve.wait_ge(k.tile_done, 6 * half + 5 + j)
                        g = k.row(gate)[:, j * 512:(j + 1) * 512]
                        last = dve.tensor_tensor(g, row_ps[:, j, :], g, ALU.add)
                    last.then_inc(row_out, 1)
                dve.tensor_tensor(k.mod[:], mod_ps[:, 0:32], k.col("b_ada", 0, 32), ALU.add)
                dve.drain()
                for i, g in ((8, "norm1_g"), (24, "norm2_g")):
                    dve.scalar_tensor_tensor(out=k.mod[:, i:i + 8], in0=k.mod[:, i:i + 8], scalar=1.0,
                                             in1=k.col(g, 0, 8), op0=ALU.add, op1=ALU.mult)
                dve.drain()
                norm_m.dve_out(dve, k.memT, k.col("mem_norm_w", 0, KD))
                norm_x.dve_out(dve, k.hT, k.mod[:, 8:16], k.mod[:, 0:8])

            @block.tensor
            def _(pe):
                pe.wait_ge(csil_ready, 1)
                with pe.Fori(0, 2) as half:
                    for j in range(6):
                        slot = j % RING
                        pe.wait_ge(k.landed[slot], half * 32 + 16 * (j // RING + 1))
                        w = k.ring[:, slot, :].rearrange("p (k n) -> p k n", k=KD)
                        if j == 4:
                            pe.wait_ge(row_out, half + 1)
                        if j < 4:
                            for f in range(4):
                                for kk in range(KD):
                                    last = pe.matmul(mod_ps[:, bass.ds(half * 16 + (4 * j + f), 1)],
                                                     w[:, kk, f * P:(f + 1) * P], csil[:, kk:kk + 1],
                                                     start=(kk == 0), stop=(kk == KD - 1))
                        else:
                            for kk in range(KD):
                                last = pe.matmul(row_ps[:, j - 4, :], crep[:, kk, :], w[:, kk, :],
                                                 start=(kk == 0), stop=(kk == KD - 1))
                        last.then_inc(k.tile_done, 1)
                norm_m.pe(pe)
                pe.wait_ge(norm_m.done, KD)
                norm_x.pe(pe)


def stage_in_projection(k, a):
    nc = k.nc
    evac = k.sem("in_proj_out")
    gates_done = k.sem("gates_done")
    wg_in = k.sem("w_gate_in")
    with nc.Block() as block:
        @block.sync
        def _(sp):
            sp.dma_start(a["w_gate"][:], k.dram["w_gate"]).then_inc(wg_in, 16)
            stream(k, sp, T_IN, T_IN + N_IN)

        @block.tensor
        def _(pe):
            for m in range(N_IN):
                if m >= 3:
                    pe.wait_ge(evac, m - 2)
                if m in (3, 4):
                    fm_tile(k, pe, T_IN + m, k.hT, pair_fm(k, m))
                else:
                    tm_tile(k, pe, T_IN + m, k.hT, pair(k, m))
            pe.wait_ge(wg_in, 16)
            for g in range(2):
                for kk in range(KD):
                    last = pe.matmul(k.ps[0:4, 6 + g, 0:TOK], a["w_gate"][:, kk, 4 * g:4 * g + 4], k.hT[:, kk, :],
                                     start=(kk == 0), stop=(kk == KD - 1))
            last.then_inc(gates_done, 1)

        @block.vector
        def _(dve):
            dve.memset(a["v_aug"][:], 1.0)
            dve.memset(a["qk_mT"][:, :, 0:3], 0.0)
            dve.drain()
            for m in range(N_IN):
                dve.wait_ge(k.tile_done, T_IN + m + 1)
                if m < 3:
                    ins = dve.tensor_copy(a["qkv"][:, :, m * 512:(m + 1) * 512], pair(k, m))
                elif m < 5:
                    ins = dve.tensor_copy(a["qk_mT"][:, 4 * (m - 3):4 * (m - 3) + 4, 3:3 + TOK], pair_fm(k, m))
                elif m == 5:
                    for t in range(TT):
                        ins = dve.tensor_copy(a["v_aug"][:, t, :, 0:128],
                                              pair(k, m)[:, t, :].rearrange("p (h e) -> p h e", h=4))
                else:
                    ins = dve.tensor_copy(a["o_m"][:], pair(k, m))
                ins.then_inc(evac, 1)
            dve.wait_ge(gates_done, 1)
            for g in range(2):
                dve.tensor_scalar(a["gate_rows"][0:4, g, :], k.ps[0:4, 6 + g, 0:TOK], k.col("b_gate", g)[0:4], None, ALU.add)


def stage_attention(k, a):
    nc = k.nc
    with ExitStack() as ctx:
        rot = k.sb("rot", [P, TT, D], ctx=ctx)
        swp = k.sb("swp", [P, 16, 2, 32], ctx=ctx)
        qkT = k.sb("qkT", [P, KD, TOK], ctx=ctx)
        scores = k.sb("scores", [P, 2, 2, TT, TOK], ctx=ctx)
        pT = k.sb("pT", [P, 2, 2, TT, TOK], ctx=ctx)
        mx = k.sb("mx", [P, 4, 4], ctx=ctx)
        rs = k.sb("rs", [P, 4, 4], ctx=ctx)
        rotated, turned, qkT_ready, scored, masked, expd, p_turned, pT_ready, pv_done = (
            k.sem(s) for s in ("qk_rotated", "qk_turned", "qkT_ready", "scored", "masked", "exp_done", "p_turned",
                               "pT_ready", "pv_done"))
        spair = [k.ps[:, 0:2, :], k.ps[:, 2:4, :]]
        tps = k.ps[:, 4:6, :].rearrange("p h (kt q) -> p h kt q", kt=2)
        ops = k.ps[:, 6:8, :].rearrange("p b (g t e) -> p (b g) t e", t=TT, e=64)
        with nc.Block() as block:
            @block.vector
            def _(dve):
                for t in range(TT):
                    src = a["qkv"][:, t, 0:1024].rearrange("p (h g e) -> p h g e", g=2, e=32)
                    dst = rot[:, t, :].rearrange("p (h g e) -> p h g e", g=2, e=32)
                    cos, sin = k.cos[:, t, :], k.sin[:, t, :]
                    for g in range(2):
                        dve.tensor_tensor(dst[:, :, g, :], src[:, :, g, :], bc(cos, 1, 16), ALU.mult)
                        dve.tensor_tensor(swp[:, :, g, :], src[:, :, 1 - g, :], bc(sin, 1, 16), ALU.mult)
                    dve.drain()
                    dve.tensor_tensor(dst[:, :, 0, :], dst[:, :, 0, :], swp[:, :, 0, :], ALU.subtract)
                    dve.tensor_tensor(dst[:, :, 1, :], dst[:, :, 1, :], swp[:, :, 1, :], ALU.add).then_inc(rotated, 1)
                    dve.drain()
                dve.wait_ge(turned, KD)
                dve.tensor_copy(qkT[:, :, :], k.ps[:, 0:4, :].rearrange("p b (f t) -> p (b f) t", f=2)).then_inc(qkT_ready, 1)

                def mask(hp):
                    dve.wait_ge(scored, hp + 1)
                    for h in range(2):
                        dve.scalar_tensor_tensor(out=scores[:, hp % 2, h], scalar=0.125, op0=ALU.mult, op1=ALU.add,
                                                 in0=spair[hp % 2][:, h, :].rearrange("p (t q) -> p t q", t=TT),
                                                 in1=k.c("causal").rearrange("p (t q) -> p t q", t=TT))
                    dve.drain()
                    dve.tensor_reduce(mx[:, hp, :], scores[:, hp % 2].rearrange("p h t q -> p (h t) q"), AX, ALU.max)
                    dve.drain()
                    dve.tensor_scalar(mx[:, hp, :], mx[:, hp, :], -1.0, None, ALU.mult).then_inc(masked, 1)

                for hp in range(4):
                    if hp == 0:
                        mask(0)
                    dve.wait_ge(p_turned, hp + 1)
                    if hp >= 2:
                        dve.wait_ge(pv_done, hp - 1)
                    dve.tensor_copy(pT[:, hp % 2], tps[:]).then_inc(pT_ready, 1)
                    if hp < 3:
                        mask(hp + 1)
                dve.reciprocal(rs[:], rs[:])
                dve.drain()
                dve.wait_ge(pv_done, 4)
                dst = a["mix"][:, :, 0:512].rearrange("p t (h e) -> p h t e", e=64)
                r = rs[:].rearrange("p a (h t) -> p (a h) t", h=2)
                for t in range(TT):
                    dve.tensor_tensor(dst[:, :, t, :], ops[:, :, t, :], bc(r[:, :, t], 2, 64), ALU.mult)

            @block.scalar
            def _(act):
                for hp in range(4):
                    act.wait_ge(masked, hp + 1)
                    if hp >= 2:
                        act.wait_ge(p_turned, hp - 1)
                    for h in range(2):
                        for t in range(TT):
                            i = 2 * h + t
                            last = act.activation(scores[:, hp % 2, h, t, :], scores[:, hp % 2, h, t, :], ACT.Exp,
                                                  bias=mx[:, hp, i:i + 1], accum_out=rs[:, hp, i:i + 1])
                    last.then_inc(expd, 1)

            @block.tensor
            def _(pe):
                pe.wait_ge(rotated, TT)
                turn(k, pe, rot, KD, k.ps[:, 0:4, :].rearrange("p b (f t) -> p (b f) t", f=2), turned)
                pe.wait_ge(qkT_ready, 1)

                def score(hp):
                    if hp >= 2:
                        pe.wait_ge(masked, hp - 1)
                    for h in range(2):
                        r = slice(64 * h, 64 * h + 64)
                        for t in range(TT):
                            last = pe.matmul(spair[hp % 2][:, h, t * TOK:(t + 1) * TOK], qkT[r, hp, t * P:(t + 1) * P],
                                             qkT[r, 4 + hp, :], start=True, stop=True)
                    last.then_inc(scored, 1)

                score(0)
                for hp in range(4):
                    if hp < 3:
                        score(hp + 1)
                    pe.wait_ge(expd, hp + 1)
                    if hp >= 1:
                        pe.wait_ge(pT_ready, hp)
                    for h in range(2):
                        for kt in range(2):
                            for t in range(TT):
                                last = pe.transpose(tps[:, h, kt, t * P:(t + 1) * P],
                                                    scores[:, hp % 2, h, t, kt * P:(kt + 1) * P], k.c("ident"))
                    last.then_inc(p_turned, 1)
                    pe.wait_ge(pT_ready, hp + 1)
                    for h in range(2):
                        v = slice(1024 + (2 * hp + h) * 64, 1024 + (2 * hp + h) * 64 + 64)
                        for t in range(TT):
                            for kt in range(t + 1):
                                last = pe.matmul(ops[:, 2 * hp + h, t, :], pT[:, hp % 2, h, kt, t * P:(t + 1) * P],
                                                 a["qkv"][:, kt, v], start=(kt == 0), stop=(kt == t))
                    last.then_inc(pv_done, 1)


def stage_conv(k, a):
    nc = k.nc
    with ExitStack() as ctx:
        acc = k.sb("conv_acc", [P, KD, TOK], ctx=ctx)
        ex = k.sb("conv_exp", [P, KD, TOK], ctx=ctx)
        t4 = k.sb("gate_tmp", [4, 8, TOK], ctx=ctx)
        q4 = k.sb("gate_quads", [P, TOK], ctx=ctx)
        sc = k.sb("gate_small", [4, 8], ctx=ctx)
        conv_done, silu_exp, f_ready, f_exp, m_ready, e_ready, quads_ready, cols_ready, arow = (
            k.sem(s) for s in ("conv_done", "silu_exp", "f_ready", "f_exp", "m_ready", "m_exp", "quads_ready",
                               "gate_cols_ready", "a_rows_ready"))
        logf, cum, b, pm, mt, tmp, one = (t4[:, i, :] for i in range(7))
        ig = a["gate_rows"][0:4, 0, :]
        fg = a["gate_rows"][0:4, 1, :]
        with nc.Block() as block:
            @block.gpsimd
            def _(pool):
                pool.memset(q4[:], 0.0).then_inc(arow, 1)

            @block.scalar
            def _(act):
                act.wait_ge(f_ready, 1)
                act.activation(tmp, tmp, ACT.Exp, scale=-1.0)
                act.drain()
                act.activation(tmp, tmp, ACT.Ln, bias=1.0).then_inc(f_exp, 1)
                for f in range(KD):
                    act.wait_ge(conv_done, f + 1)
                    act.activation(ex[:, f, :], acc[:, f, :], ACT.Exp, scale=-1.0).then_inc(silu_exp, 1)
                act.wait_ge(m_ready, 1)
                act.wait_ge(arow, 1)
                act.activation(q4[32:36, :], one, ACT.Exp)
                act.activation(q4[64:68, :], mt, ACT.Exp, scale=-1.0)
                act.activation(q4[96:100, 0:P], b[:, 0:P], ACT.Exp, bias=sc[:, 2:3]).then_inc(e_ready, 1)

            @block.vector
            def _(dve):
                dve.scalar_tensor_tensor(out=tmp, in0=fg, scalar=-1.0, in1=fg, op0=ALU.mult, op1=ALU.max).then_inc(f_ready, 1)
                for f in range(KD):
                    w = [k.col("conv_w", 4 * f + i) for i in range(4)]
                    dve.tensor_scalar(acc[:, f, :], a["qk_mT"][:, f, 0:TOK], w[0], k.col("conv_b", f), ALU.mult, ALU.add)
                    dve.drain()
                    for i in range(1, 4):
                        ins = dve.scalar_tensor_tensor(out=acc[:, f, :], in0=a["qk_mT"][:, f, i:i + TOK], scalar=w[i],
                                                       in1=acc[:, f, :], op0=ALU.mult, op1=ALU.add)
                        if i == 3:
                            ins.then_inc(conv_done, 1)
                        else:
                            dve.drain()
                dve.wait_ge(f_exp, 1)
                dve.tensor_scalar(logf, fg, 0.0, None, ALU.min)
                dve.memset(one, 1.0)
                dve.drain()
                dve.tensor_tensor(logf, logf, tmp, ALU.subtract)
                dve.drain()
                for c in range(2):
                    s = slice(c * P, (c + 1) * P)
                    dve.tensor_tensor_scan(cum[:, s], one[:, s], logf[:, s], 0.0, ALU.mult, ALU.add)
                dve.drain()
                dve.tensor_tensor(b, ig, cum, ALU.subtract)
                dve.drain()
                for c in range(2):
                    s = slice(c * P, (c + 1) * P)
                    dve.tensor_tensor_scan(pm[:, s], one[:, s], b[:, s], -3e38, ALU.mult, ALU.max)
                dve.drain()
                total = cum[:, P - 1:P]
                dve.tensor_tensor(sc[:, 1:2], total, pm[:, P - 1:P], ALU.add)
                dve.drain()
                dve.tensor_tensor(sc[:, 0:1], sc[:, 1:2], total, ALU.max)
                dve.drain()
                dve.tensor_tensor(sc[:, 2:3], total, sc[:, 0:1], ALU.subtract)
                dve.tensor_copy(tmp[:, 0:P], cum[:, 0:P])
                dve.tensor_scalar(tmp[:, P:], cum[:, P:], sc[:, 0:1], None, ALU.add)
                dve.tensor_tensor(mt, cum, pm, ALU.add)
                dve.drain()
                dve.tensor_tensor(mt, mt, tmp, ALU.max)
                dve.drain()
                dve.tensor_tensor(one, tmp, mt, ALU.subtract)
                dve.tensor_tensor(a["a_rows"][:], cum, mt, ALU.subtract)
                dve.drain()
                dve.wait_ge(arow, 1)
                dve.tensor_copy(q4[0:4, :], b).then_inc(m_ready, 1)
                dve.wait_ge(silu_exp, KD)
                dve.tensor_scalar(ex[:], ex[:], 1.0, None, ALU.add)
                dve.drain()
                dve.reciprocal(ex[:], ex[:])
                dve.drain()
                dve.tensor_tensor(a["qk_mT"][:, :, 3:3 + TOK], acc[:], ex[:], ALU.mult)
                dve.wait_ge(quads_ready, 1)
                for t in range(TT):
                    dve.tensor_copy(a["gcol"][:, t, :], k.ps[:, t, 0:P])
                dve.drain()
                dve.tensor_scalar(a["gcol"][:, 0, 96:100], a["gcol"][:, 0, 96:100], 128 ** -0.5, None, ALU.mult)

            @block.tensor
            def _(pe):
                pe.wait_ge(m_ready, 1)
                pe.wait_ge(e_ready, 1)
                for t in range(TT):
                    last = pe.transpose(k.ps[:, t, 0:P], q4[:, t * P:(t + 1) * P], k.c("ident"))
                last.then_inc(quads_ready, 1)


def stage_mlstm(k, a):
    nc = k.nc
    with ExitStack() as ctx:
        dm = k.sb("dmat", [P, 4, TOK], ctx=ctx)
        st = k.sb("s_t", [P, 4, TOK], ctx=ctx)
        kw = k.sb("k_weighted", [P, 4, P], ctx=ctx)
        cst = k.sb("c_state", [P, 4, 129], ctx=ctx)
        num = k.sb("num", [P, TT, 4, 129], ctx=ctx)
        den = k.sb("den", [P, TT, 4, 1], ctx=ctx)
        a_bc, masked, d_exp, s_raw, s_ready, kt, kw_ready, c_done, c_out, num0, num1, inter = (
            k.sem(s) for s in ("a_bc", "d_masked", "d_exp", "s_raw", "s_ready", "k_turned", "kw_ready", "c_done", "c_out",
                               "num0_done", "num1_done", "inter_done"))
        abc = k.ps[:, 0:2, :].rearrange("p b (h t) -> p (b h) t", h=2)
        sps = k.ps[:, 2:4, :].rearrange("p b (h t) -> p (b h) t", h=2)
        qT = lambda h, t: a["qk_mT"][:, h, 3 + t * P:3 + (t + 1) * P]
        kT = lambda h, t: a["qk_mT"][:, 4 + h, 3 + t * P:3 + (t + 1) * P]
        b_col = lambda h, t: a["gcol"][:, t, h:h + 1]
        acc = lambda i, h: k.ps[:, i + h // 2, 256 * (h % 2):256 * (h % 2) + 129]
        with nc.Block() as block:
            @block.tensor
            def _(pe):
                for h in range(4):
                    last = pe.matmul(abc[:, h, :], k.c("one_hot4")[0:4, h * P:(h + 1) * P], a["a_rows"][:],
                                     start=True, stop=True)
                last.then_inc(a_bc, 1)
                for h in range(4):
                    for t in range(TT):
                        last = pe.matmul(sps[:, h, t * P:(t + 1) * P], kT(h, t), qT(h, t), start=True, stop=True)
                last.then_inc(s_raw, 1)
                for h in range(4):
                    last = pe.transpose(k.ps[:, 4, h * P:(h + 1) * P], kT(h, 0), k.c("ident"))
                last.then_inc(kt, 1)
                pe.wait_ge(kw_ready, 1)
                for h in range(4):
                    last = pe.matmul(acc(5, h), kw[:, h, :], a["v_aug"][:, 0, h, :], start=True, stop=True)
                last.then_inc(c_done, 1)
                pe.wait_ge(s_ready, 1)
                for t in range(TT):
                    for h in range(4):
                        last = pe.matmul(acc(2 * t, h), st[:, h, t * P:(t + 1) * P], a["v_aug"][:, t, h, :],
                                         start=True, stop=True)
                last.then_inc(num0, 1)
                pe.wait_ge(c_out, 1)
                for h in range(4):
                    last = pe.matmul(acc(5, h), qT(h, 1), cst[:, h, :], start=True, stop=True)
                last.then_inc(inter, 1)

            @block.scalar
            def _(act):
                act.wait_ge(masked, 1)
                for h in range(4):
                    for t in range(TT):
                        s = slice(t * P, (t + 1) * P)
                        last = act.activation(dm[:, h, s], dm[:, h, s], ACT.Exp, bias=b_col(h, t))
                last.then_inc(d_exp, 1)

            @block.vector
            def _(dve):
                dve.wait_ge(a_bc, 1)
                for t in range(TT):
                    s = slice(t * P, (t + 1) * P)
                    last = dve.tensor_tensor(dm[:, :, s], abc[:, :, s], bc(k.c("causal_t"), 1, 4), ALU.add)
                last.then_inc(masked, 1)
                dve.wait_ge(kt, 1)
                dve.tensor_tensor(kw[:], k.ps[:, 4, :].rearrange("p (h d) -> p h d", h=4),
                                  bc(a["gcol"][:, 0, 96:100], 2, P), ALU.mult).then_inc(kw_ready, 1)
                dve.wait_ge(d_exp, 1)
                dve.wait_ge(s_raw, 1)
                dve.scalar_tensor_tensor(out=st[:], in0=sps[:], scalar=128 ** -0.5, in1=dm[:], op0=ALU.mult,
                                         op1=ALU.mult).then_inc(s_ready, 1)
                dve.wait_ge(c_done, 1)
                for h in range(4):
                    last = dve.tensor_copy(cst[:, h, :], acc(5, h))
                last.then_inc(c_out, 1)
                dve.wait_ge(num0, 1)
                for t in range(TT):
                    for h in range(4):
                        dve.tensor_copy(num[:, t, h, :], acc(2 * t, h))
                dve.drain()
                dve.wait_ge(inter, 1)
                for h in range(4):
                    dve.scalar_tensor_tensor(out=num[:, 1, h, :], in0=acc(5, h), scalar=a["gcol"][:, 1, 32 + h:33 + h],
                                             in1=num[:, 1, h, :], op0=ALU.mult, op1=ALU.add)
                dve.drain()
                dve.scalar_tensor_tensor(out=den[:, :, :, 0], in0=num[:, :, :, 128], scalar=-1.0, in1=num[:, :, :, 128],
                                         op0=ALU.mult, op1=ALU.max)
                dve.drain()
                for t in range(TT):
                    dve.tensor_tensor(den[:, t, :, 0], den[:, t, :, 0], a["gcol"][:, t, 64:68], ALU.max)
                dve.drain()
                dve.reciprocal(den[:], den[:])
                dve.drain()
                for t in range(TT):
                    dve.tensor_tensor(a["mix"][:, t, 512:1024].rearrange("p (h e) -> p h e", h=4), num[:, t, :, 0:128],
                                      den[:, t, :, :].broadcast_to([P, 4, 128]), ALU.mult)


def stage_out_projection(k, a):
    nc = k.nc
    with ExitStack() as ctx:
        sq = k.sb("mix_sq", [P, TT, D], ctx=ctx)
        ss = k.sb("head_ss", [P, TT, 12], ctx=ctx)
        rstd = k.sb("head_rstd", [P, TT, 12], ctx=ctx)
        sig = k.sb("sig", [P, TT, 512], ctx=ctx)
        mixT = k.sb("mixT", [P, KD, TOK], ctx=ctx)
        xn = k.sb("xn1", [P, TT, D], ctx=ctx)
        w_router = k.sb("w_router", [P, KD, 36], ctx=ctx)
        norm = NormT(k, "norm2", k.x, ctx, xn)
        squares, rstd_ready, sig_exp, mix_ready, mix_turned, mixT_ready, x_ready, logits, router_in = (
            k.sem(s) for s in ("mix_squares", "head_rstd_ready", "sig_exp", "mix_ready", "mix_turned", "mixT_ready",
                               "x_ready", "logits_done", "router_in"))
        tps = k.ps[:, 0:4, :].rearrange("p b (f t) -> p (b f) t", f=2)
        groups = ((0, 512, 64, 0, 8, "attn_out_g"), (512, 1024, 128, 8, 12, "mlstm_out_g"))
        with nc.Block() as block:
            @block.sync
            def _(sp):
                sp.dma_start(w_router[:], k.dram["w_router"]).then_inc(router_in, 16)
                for j in range(RING):
                    sp.wait_ge(k.tile_done, T_GLA - RING + j + 1)
                    sp.dma_start(k.ring[:, j, :], k.dram["experts"][j]).then_inc(a["expert_landed"][j], 16)

            @block.scalar
            def _(act):
                act.activation(sig[:], a["o_m"][:], ACT.Exp, scale=-1.0).then_inc(sig_exp, 1)
                act.wait_ge(x_ready, 1)
                norm.act(act)

            @block.gpsimd
            def _(pool):
                pool.wait_ge(squares, 1)
                pool.tensor_scalar(rstd[:, :, 0:8], ss[:, :, 0:8], 1.0 / 64, EPS, ALU.mult, ALU.add)
                pool.tensor_scalar(rstd[:, :, 8:12], ss[:, :, 8:12], 1.0 / 128, EPS, ALU.mult, ALU.add)
                pool.drain()
                for t in range(TT):
                    last = pool.tensor_tensor(out=rstd[:, t, :], in0=rstd[:, t, :], in1=k.c("minus_half")[:, 0:12],
                                              op=ALU.pow)
                last.then_inc(rstd_ready, 1)
                norm.pool(pool)

            @block.vector
            def _(dve):
                dve.tensor_tensor(sq[:], a["mix"][:], a["mix"][:], ALU.mult)
                dve.drain()
                for c0, c1, w, s0, s1, _g in groups:
                    for t in range(TT):
                        last = dve.tensor_reduce(ss[:, t, s0:s1], sq[:, t, c0:c1].rearrange("p (h e) -> p h e", e=w),
                                                 AX, ALU.add)
                last.then_inc(squares, 1)
                dve.wait_ge(sig_exp, 1)
                dve.tensor_scalar(sig[:], sig[:], 1.0, None, ALU.add)
                dve.drain()
                dve.reciprocal(sig[:], sig[:])
                dve.drain()
                dve.tensor_tensor(sig[:], sig[:], bc(k.row("mlstm_out_g"), 1, TT), ALU.mult)
                dve.wait_ge(rstd_ready, 1)
                for c0, c1, w, s0, s1, _g in groups:
                    for t in range(TT):
                        v = a["mix"][:, t, c0:c1].rearrange("p (h e) -> p h e", e=w)
                        dve.tensor_tensor(v, v, bc(rstd[:, t, s0:s1], 2, w), ALU.mult)
                dve.drain()
                dve.tensor_tensor(a["mix"][:, :, 0:512], a["mix"][:, :, 0:512], bc(k.row("attn_out_g"), 1, TT), ALU.mult)
                dve.tensor_tensor(a["mix"][:, :, 512:1024], a["mix"][:, :, 512:1024], sig[:], ALU.mult).then_inc(mix_ready, 1)
                dve.wait_ge(mix_turned, KD)
                dve.tensor_copy(mixT[:], tps[:]).then_inc(mixT_ready, 1)
                for n in range(N_OUT):
                    dve.wait_ge(k.tile_done, T_OUT + n + 1)
                    s = slice(n * 512, (n + 1) * 512)
                    dve.tensor_tensor(sq[:, :, s], k.ps[:, 4 + 2 * n:6 + 2 * n, :], bc(k.row("b_g1")[:, s], 1, TT), ALU.mult)
                dve.drain()
                dve.tensor_tensor(k.x[:], k.x[:], sq[:], ALU.add).then_inc(x_ready, 1)
                norm.dve_scale(dve)
                norm.dve_out(dve, k.hT, k.mod[:, 24:32], k.mod[:, 16:24])
                dve.wait_ge(logits, 1)
                dve.tensor_tensor(a["logits"][:], k.ps[:, 4:6, 0:36], bc(k.row("b_router"), 1, TT), ALU.add)

            @block.tensor
            def _(pe):
                pe.wait_ge(mix_ready, 1)
                turn(k, pe, a["mix"], KD, tps, mix_turned)
                pe.wait_ge(mixT_ready, 1)
                for n in range(N_OUT):
                    tm_tile(k, pe, T_OUT + n, mixT, k.ps[:, 4 + 2 * n:6 + 2 * n, :])
                norm.pe(pe)
                pe.wait_ge(norm.done, KD)
                pe.wait_ge(router_in, 16)
                for t in range(TT):
                    for kk in range(KD):
                        last = pe.matmul(k.ps[:, 4 + t, 0:36], k.hT[:, kk, t * P:(t + 1) * P], w_router[:, kk, :],
                                         start=(kk == 0), stop=(kk == KD - 1))
                last.then_inc(logits, 1)


def stage_route(k, a):
    with ExitStack() as ctx:
        sb = lambda name, s, dt=F32: k.sb(name, s, dt, ctx=ctx)
        g8, gm, gi, gf = sb("g8", [P, TT, 8]), sb("g_top", [P, TT, 8]), sb("g_idx", [P, TT, 8], U32), sb("g_idx_f", [P, TT, 8])
        ge, gs, gmask = sb("g_exp", [P, TT, 4]), sb("g_sum", [P, TT]), sb("g_mask", [P, TT, 4])
        em, et = sb("e_masked", [P, TT, 32]), sb("e_top", [P, TT, 8])
        ei, ef = sb("e_idx", [P, TT, 8], U32), sb("e_idx_f", [P, TT, 8])
        dl, w1, w2 = sb("e_gap", [P, TT]), sb("w_first", [P, TT]), sb("w_second", [P, TT])
        is1, is2, chosen = sb("is_first", [P, TT, 32]), sb("is_second", [P, TT, 32]), sb("chosen", [P, TT, 32])
        over, most = sb("over", [P, 3]), sb("most", [P, 1])
        gap_ready, exp_done, chosen_ready, ranked, h_turned = (
            k.sem(s) for s in ("gap_ready", "route_exp_done", "chosen_ready", "ranked", "h_turned_back"))
        with k.nc.Block() as block:
            @block.tensor
            def _(pe):
                for t in range(TT):
                    for f in range(KD):
                        last = pe.transpose(k.ps[:, 2 * t + f // 4, (f % 4) * P:(f % 4 + 1) * P],
                                            k.hT[:, f, t * P:(t + 1) * P], k.c("ident"))
                last.then_inc(h_turned, 1)
                pe.wait_ge(chosen_ready, 1)
                pe.matmul(k.ps[:, 4, 0:32], k.c("before"), chosen[:, 0, :], start=True, stop=True)
                pe.matmul(k.ps[:, 4, 32:64], k.c("before"), chosen[:, 1, :], start=True, stop=False)
                pe.matmul(k.ps[:, 4, 32:64], k.c("ones"), chosen[:, 0, :], start=False, stop=True)
                pe.matmul(k.ps[:, 5, 0:32], k.c("ones"), chosen[:, 0, :], start=True, stop=False)
                pe.matmul(k.ps[:, 5, 0:32], k.c("ones"), chosen[:, 1, :], start=False, stop=True).then_inc(ranked, 1)

            @block.vector
            def _(dve):
                dve.memset(g8[:], -3e38)
                dve.drain()
                dve.tensor_copy(g8[:, :, 0:4], a["logits"][:, :, 0:4])
                dve.drain()
                for t in range(TT):
                    dve.max(gm[:, t, :], g8[:, t, :])
                dve.drain()
                for t in range(TT):
                    dve.max_index(gi[:, t, :], gm[:, t, :], g8[:, t, :])
                    dve.tensor_scalar(ge[:, t, :], a["logits"][:, t, 0:4], gm[:, t, 0:1], None, ALU.subtract)
                dve.drain()
                dve.tensor_copy(gf[:], gi[:])
                dve.drain()
                for t in range(TT):
                    dve.tensor_scalar(gmask[:, t, :], k.c("iota64")[:, 0:4], gf[:, t, 0:1], None, ALU.is_equal)
                dve.drain()
                for t in range(TT):
                    dve.tensor_tensor(em[:, t, :].rearrange("p (g e) -> p g e", g=4),
                                      a["logits"][:, t, 4:36].rearrange("p (g e) -> p g e", g=4),
                                      bc(gmask[:, t, :], 2, 8), ALU.mult)
                dve.drain()
                dve.tensor_scalar(gmask[:], gmask[:], -NEG, NEG, ALU.mult, ALU.add)
                dve.drain()
                for t in range(TT):
                    v = em[:, t, :].rearrange("p (g e) -> p g e", g=4)
                    dve.tensor_tensor(v, v, bc(gmask[:, t, :], 2, 8), ALU.add)
                dve.drain()
                for t in range(TT):
                    dve.max(et[:, t, :], em[:, t, :])
                dve.drain()
                for t in range(TT):
                    dve.max_index(ei[:, t, :], et[:, t, :], em[:, t, :])
                dve.tensor_tensor(dl[:], et[:, :, 1], et[:, :, 0], ALU.subtract).then_inc(gap_ready, 1)
                dve.drain()
                dve.tensor_copy(ef[:], ei[:])
                dve.drain()
                for t in range(TT):
                    dve.tensor_scalar(is1[:, t, :], k.c("iota64")[:, 0:32], ef[:, t, 0:1], None, ALU.is_equal)
                    dve.tensor_scalar(is2[:, t, :], k.c("iota64")[:, 0:32], ef[:, t, 1:2], None, ALU.is_equal)
                dve.drain()
                dve.tensor_tensor(chosen[:], is1[:], is2[:], ALU.add).then_inc(chosen_ready, 1)
                dve.wait_ge(exp_done, 1)
                dve.tensor_reduce(gs[:], ge[:], AX, ALU.add)
                dve.tensor_scalar(w1[:], dl[:], 1.0, None, ALU.add)
                dve.drain()
                dve.tensor_tensor(w1[:], w1[:], gs[:], ALU.mult)
                dve.drain()
                dve.reciprocal(w1[:], w1[:])
                dve.drain()
                dve.tensor_tensor(w2[:], w1[:], dl[:], ALU.mult)
                dve.drain()
                for t in range(TT):
                    dve.tensor_scalar(is1[:, t, :], is1[:, t, :], w1[:, t:t + 1], None, ALU.mult)
                    dve.tensor_scalar(is2[:, t, :], is2[:, t, :], w2[:, t:t + 1], None, ALU.mult)
                dve.drain()
                dve.tensor_tensor(a["comb"][:, :, 0:N_EXP], is1[:], is2[:], ALU.add)
                dve.wait_ge(ranked, 1)
                r = a["rank"][:, :, 0:N_EXP]
                dve.scalar_tensor_tensor(out=r, in0=k.ps[:, 4, 0:64].rearrange("p (t e) -> p t e", t=TT), scalar=1.0,
                                         in1=chosen[:], op0=ALU.add, op1=ALU.mult)
                dve.tensor_reduce(most[:], k.ps[:, 5, 0:32], AX, ALU.max)
                dve.drain()
                dve.tensor_scalar(r, r, -1.0, None, ALU.add)
                dve.tensor_tensor(over[:], most[:].broadcast_to([P, 3]), k.c("slot_limits"), ALU.is_gt)
                dve.drain()
                dve.tensor_scalar(a["rank"][:, :, N_EXP:N_EXP + 1], a["rank"][:, :, 0:1], -float(SLOTS), None, ALU.add)
                dve.tensor_copy(a["comb"][:, :, N_EXP:N_EXP + 1], a["comb"][:, :, 0:1])
                dve.tensor_reduce(most[:], over[:], AX, ALU.add)
                dve.drain()
                dve.tensor_scalar(a["passes"][:], most[:], 1.0, None, ALU.add)

            @block.scalar
            def _(act):
                act.wait_ge(gap_ready, 1)
                act.activation(ge[:], ge[:], ACT.Exp)
                act.activation(dl[:], dl[:], ACT.Exp).then_inc(exp_done, 1)
                act.wait_ge(h_turned, 1)
                act.copy(a["h2"][:], k.ps[:, 0:4, :].rearrange("p (t b) c -> p t (b c)", t=TT))


def stage_experts(k, a):
    with ExitStack() as ctx:
        sb = lambda name, s: k.sb(name, s, ctx=ctx)
        sel, selw = sb("sel", [P, TT, SLOTS]), sb("sel_weighted", [P, TT, P])
        selT = sb("selT", [SLOTS, 2, TOK])
        xg = sb("x_gathered", [P, KD, SLOTS])
        gate, act_t = sb("gate", [P, 4, SLOTS]), sb("act_t", [P, 4, SLOTS])
        y = sb("y_slots", [SLOTS, D])
        names = ("sel_ready", "xg_done", "xg_ready", "silu_done", "act_ready", "selT_done", "selT_ready", "scattered",
                 "y_ready", "moe_zeroed", "moe_summed")
        sel_ready, xg_done, xg_ready, silu_done, act_ready, selT_done, selT_ready, scattered, y_ready, zeroed, summed = (
            k.sem(n) for n in names)
        done, landed = a["expert_tile_done"], a["expert_landed"]
        acc = k.ps[:, 0:4, :].rearrange("p (t n) c -> p t n c", t=TT)
        xg_ps = k.ps[:, 4, :].rearrange("p (f s) -> p f s", f=KD)
        h1, h3 = (k.ps[:, 5, 256 * i:256 * i + 256].rearrange("p (f s) -> p f s", f=4) for i in range(2))
        selT_ps = k.ps[:, 5, 0:TOK]
        y_ps = k.ps[0:SLOTS, 6:8, :]

        def passes(eng):
            return eng.value_load(a["passes"][0:1, 0:1], min_val=1, max_val=TOK // SLOTS)

        with k.nc.Block() as block:
            @block.sync
            def _(sp):
                n_pass = passes(sp)

                def load(step, e):
                    for j in range(RING):
                        sp.wait_ge(done, step * 3 + j)
                        sp.dma_start(k.ring[:, j, :],
                                     k.dram["experts"][bass.ds(e * 3 + j, 1)].rearrange("a p n -> (a p) n")
                                     ).then_inc(landed[j], 16)

                with sp.Fori(0, n_pass) as p:
                    with sp.Fori(1, N_EXP) as e:
                        load(p * N_EXP + e, e)
                    with sp.If(p < n_pass - 1):
                        for j in range(RING):
                            sp.wait_ge(done, p * (3 * N_EXP) + (3 * N_EXP + j))
                            sp.dma_start(k.ring[:, j, :], k.dram["experts"][j]).then_inc(landed[j], 16)
                for j in range(RING):
                    sp.wait_ge(done, n_pass * (3 * N_EXP) + j)
                    sp.dma_start(k.ring[:, j, :], k.dram["weights"][T_GLA + j]).then_inc(k.landed[j], 16)

            @block.tensor
            def _(pe):
                n_pass = passes(pe)

                def gather():
                    for f in range(KD):
                        for t in range(TT):
                            last = pe.matmul(xg_ps[:, f, :], a["h2"][:, t, f * P:(f + 1) * P], sel[:, t, :],
                                             start=(t == 0), stop=(t == TT - 1))
                    last.then_inc(xg_done, 1)

                def turn_selection():
                    for t in range(TT):
                        last = pe.transpose(selT_ps[:, t * P:(t + 1) * P], selw[:, t, :], k.c("ident"))
                    last.then_inc(selT_done, 1)

                def scatter(b, start=False, stop=False):
                    for t in range(TT):
                        for n in range(2):
                            last = pe.matmul(acc[:, t, n, :], selT[:, b, t * P:(t + 1) * P], y[:, n * 512:(n + 1) * 512],
                                             start=start, stop=stop, skip_group_check=True)
                    return last

                pe.wait_ge(zeroed, 1)
                pe.sem_inc(done, 2)
                scatter(1, start=True)
                pe.wait_ge(sel_ready, 1)
                gather()
                turn_selection()
                with pe.Fori(0, n_pass) as p:
                    with pe.Fori(0, N_EXP // 2) as i:
                        for b in range(2):
                            s = p * N_EXP + i * 2 + b
                            pe.wait_ge(xg_ready, s + 1)
                            pe.wait_ge(selT_ready, s + 1)
                            for j, out in ((0, h1), (1, h3)):
                                pe.wait_ge(landed[j], s * 16 + 16)
                                w = k.ring[:, j, :].rearrange("p (k n) -> p k n", k=KD)
                                for f in range(4):
                                    for kk in range(KD):
                                        last = pe.matmul(out[:, f, :], w[:, kk, f * P:(f + 1) * P], xg[:, kk, :],
                                                         start=(kk == 0), stop=(kk == KD - 1))
                                last.then_inc(done, 1)
                            pe.wait_ge(sel_ready, s + 2)
                            gather()
                            pe.wait_ge(y_ready, s + 1)
                            scatter(1 - b).then_inc(scattered, 1)
                            pe.wait_ge(act_ready, s + 2)
                            turn_selection()
                            pe.wait_ge(landed[2], s * 16 + 16)
                            w = k.ring[:, 2, :].rearrange("p (k n) -> p k n", k=4)
                            for n in range(2):
                                for f in range(4):
                                    last = pe.matmul(y_ps[:, n, :], act_t[:, f, :], w[:, f, n * 512:(n + 1) * 512],
                                                     start=(f == 0), stop=(f == 3))
                            last.then_inc(done, 1)
                pe.wait_ge(y_ready, n_pass * N_EXP + 1)
                scatter(1, stop=True).then_inc(summed, 1)

            @block.scalar
            def _(act):
                n_pass = passes(act)
                act.wait_ge(zeroed, 1)
                act.wait_ge(selT_done, 1)
                act.copy(selT[:, 0, :], selT_ps[0:SLOTS, :]).then_inc(selT_ready, 1)
                with act.Fori(0, n_pass) as p:
                    with act.Fori(0, N_EXP // 2) as i:
                        for b in range(2):
                            s = p * N_EXP + i * 2 + b
                            act.wait_ge(done, s * 3 + 4)
                            act.wait_ge(act_ready, s + 1)
                            act.activation(gate[:], h1, ACT.Silu).then_inc(silu_done, 1)
                            act.wait_ge(scattered, s + 1)
                            act.wait_ge(selT_done, s + 2)
                            act.copy(selT[:, 1 - b, :], selT_ps[0:SLOTS, :]).then_inc(selT_ready, 1)
                            act.wait_ge(done, s * 3 + 5)
                            act.copy(y[:].rearrange("p (n c) -> p n c", n=2), y_ps[:]).then_inc(y_ready, 1)

            @block.vector
            def _(dve):
                n_pass = passes(dve)

                def select(e):
                    for t in range(TT):
                        r = a["rank"][:, t, e]
                        dve.tensor_scalar(sel[:, t, :], k.c("iota64"), r, None, ALU.is_equal)
                        last = dve.tensor_scalar(selw[:, t, 0:SLOTS], k.c("iota64"), r, a["comb"][:, t, e], ALU.is_equal, ALU.mult)
                    return last

                dve.memset(y[:], 0.0)
                dve.memset(selT[:], 0.0)
                dve.memset(selw[:], 0.0)
                dve.drain()
                dve.sem_inc(zeroed, 1)
                dve.sem_inc(y_ready, 1)
                dve.sem_inc(act_ready, 1)
                select(slice(0, 1)).then_inc(sel_ready, 1)
                dve.wait_ge(xg_done, 1)
                dve.tensor_copy(xg[:], xg_ps[:]).then_inc(xg_ready, 1)
                with dve.Fori(0, n_pass) as p:
                    with dve.Fori(0, N_EXP // 2) as i:
                        for b in range(2):
                            s = p * N_EXP + i * 2 + b
                            dve.wait_ge(xg_done, s + 1)
                            dve.wait_ge(selT_done, s + 1)
                            select(bass.ds(i * 2 + (b + 1), 1)).then_inc(sel_ready, 1)
                            dve.wait_ge(silu_done, s + 1)
                            dve.wait_ge(done, s * 3 + 4)
                            dve.tensor_tensor(act_t[:], gate[:], h3, ALU.mult).then_inc(act_ready, 1)
                            dve.wait_ge(xg_done, s + 2)
                            dve.tensor_copy(xg[:], xg_ps[:]).then_inc(xg_ready, 1)
                    dve.drain()
                    dve.tensor_scalar(a["rank"][:], a["rank"][:], -float(SLOTS), None, ALU.add)
                    dve.drain()
                dve.wait_ge(summed, 1)
                dve.tensor_copy(a["moe"][:].rearrange("p t (n c) -> p t n c", n=2), acc[:])


def stage_first_end(k, a):
    nc = k.nc
    with ExitStack() as ctx:
        xn = k.sb("xn2", [P, TT, D], ctx=ctx)
        f = NormT(k, "norm_f", k.x, ctx, xn)
        g = NormT(k, "gla_norm", k.x, ctx, xn)
        x_ready, x_normed = k.sem("moe_added"), k.sem("x_normed")
        with nc.Block() as block:
            @block.vector
            def _(dve):
                dve.tensor_tensor(a["moe"][:], a["moe"][:], bc(k.row("b_g2"), 1, TT), ALU.mult)
                dve.drain()
                dve.tensor_tensor(k.x[:], k.x[:], a["moe"][:], ALU.add).then_inc(x_ready, 1)
                dve.wait_ge(f.rstd_ready, 1)
                for t in range(TT):
                    last = dve.scalar_tensor_tensor(out=k.x[:, t, :], in0=k.x[:, t, :], scalar=f.rstd[:, t:t + 1],
                                                    in1=k.row("norm_f_g"), op0=ALU.mult, op1=ALU.mult)
                last.then_inc(x_normed, 1)
                dve.drain()
                g.dve_scale(dve)
                g.dve_out(dve, k.hT, k.col("norm_w_2", 0, KD))

            @block.scalar
            def _(act):
                act.wait_ge(x_ready, 1)
                f.act(act)
                act.wait_ge(x_normed, 1)
                g.act(act)

            @block.gpsimd
            def _(pool):
                f.pool(pool)
                g.pool(pool)

            @block.tensor
            def _(pe):
                g.pe(pe)


def first_block(k):
    with ExitStack() as ctx:
        stage_modulation(k, k.hold_rows(("b_g1", "b_router"), ctx))
        a = {
            "w_gate": k.sb("w_gate", [P, KD, 8], ctx=ctx),
            "qkv": k.sb("qkv", [P, TT, 1536], ctx=ctx),
            "qk_mT": k.sb("qk_mT", [P, KD, 3 + TOK], ctx=ctx),
            "v_aug": k.sb("v_aug", [P, TT, 4, 129], ctx=ctx),
            "o_m": k.sb("o_m", [P, TT, 512], ctx=ctx),
            "gate_rows": k.sb("gate_rows", [4, 2, TOK], ctx=ctx),
            "a_rows": k.sb("a_rows", [4, TOK], ctx=ctx),
            "gcol": k.sb("gcol", [P, TT, P], ctx=ctx),
            "mix": k.sb("mix", [P, TT, D], ctx=ctx),
            "logits": k.sb("logits", [P, TT, 36], ctx=ctx),
        }
        a["expert_landed"] = [k.sem(f"expert_landed_{j}") for j in range(RING)]
        a["expert_tile_done"] = k.sem("expert_tile_done")
        stage_in_projection(k, a)
        stage_attention(k, a)
        stage_conv(k, a)
        stage_mlstm(k, a)
        stage_out_projection(k, a)
        a["comb"] = k.sb("comb", [P, TT, N_EXP + 1], ctx=ctx)
        a["rank"] = k.sb("rank", [P, TT, N_EXP + 1], ctx=ctx)
        a["passes"] = k.sb("passes", [P, 1], I32, ctx=ctx)
        a["h2"] = k.sb("h2", [P, TT, D], ctx=ctx)
        a["moe"] = k.sb("moe", [P, TT, D], ctx=ctx)
        stage_route(k, a)
        stage_experts(k, a)
        stage_first_end(k, a)


def stage_tiles(k, name, first, specs, sp_extra=None, act_extra=None):
    outs = {e: k.sem(f"{name}_out_{e}") for e in ("dve", "act")}
    nth = [sum(s[3] == spec[3] for s in specs[:m + 1]) for m, spec in enumerate(specs)]
    with k.nc.Block() as block:
        @block.sync
        def _(sp):
            if sp_extra:
                sp_extra(sp)
            stream(k, sp, first, first + len(specs))

        @block.tensor
        def _(pe):
            for m, (kind, src, k0, _engine, _write) in enumerate(specs):
                if m >= 3:
                    pe.wait_ge(outs[specs[m - 3][3]], nth[m - 3])
                if kind == "tm":
                    tm_tile(k, pe, first + m, src, pair(k, m), k0)
                else:
                    fm_tile(k, pe, first + m, src, pair_fm(k, m), k0)

        def write_out(engine, which):
            for m, (kind, _src, _k0, owner, write) in enumerate(specs):
                if owner == which:
                    engine.wait_ge(k.tile_done, first + m + 1)
                    write(engine, pair(k, m) if kind == "tm" else pair_fm(k, m)).then_inc(outs[which], 1)

        @block.vector
        def _(dve):
            write_out(dve, "dve")

        @block.scalar
        def _(act):
            if act_extra:
                act_extra(act)
            write_out(act, "act")


def copy_to(dst):
    return lambda dve, src: dve.tensor_copy(dst, src)


def silu_to(dst):
    return lambda act, src: act.activation(dst, src, ACT.Silu)


def add_after(dst):
    def write(dve, src):
        dve.drain()
        return dve.tensor_tensor(dst, dst, src, ALU.add)
    return write


def stage_gla_gate(k, a):
    with ExitStack() as ctx:
        rT = k.sb("rT", [16, TOK], ctx=ctx)
        g = k.sb("g_log", [P, TT, 512], ctx=ctx)
        lg = k.sb("g_tmp", [P, TT, 512], ctx=ctx)
        eq, ek = (k.sb(n, [P, TT, 512], ctx=ctx) for n in ("exp_q", "exp_k"))
        ee = lg
        r_done, rT_ready, g_pre, abs_ready, log_ready, g_ready, cum_done, exp_done, dec_ready, turned = (
            k.sem(s) for s in ("r_done", "rT_ready", "g_pre", "g_abs_ready", "g_log_ready", "g_ready", "cum_done",
                               "decay_exp_done", "decayed", "gla_turned"))
        q, key = a["qk"][:, :, 0:512], a["qk"][:, :, 512:1024]
        with k.nc.Block() as block:
            @block.tensor
            def _(pe):
                for kk in range(KD):
                    last = pe.matmul(k.ps[0:16, 7, 0:TOK], a["w_rank"][:, kk, :], k.hT[:, kk, :],
                                     start=(kk == 0), stop=(kk == KD - 1))
                last.then_inc(r_done, 1)
                pe.wait_ge(rT_ready, 1)
                for t in range(TT):
                    last = pe.matmul(k.ps[:, t, :], rT[:, t * P:(t + 1) * P], a["w_up"][:], start=True, stop=True)
                last.then_inc(g_pre, 1)
                pe.wait_ge(g_ready, 1)
                for t in range(TT):
                    pe.matmul(k.ps[:, 2 + t, :], k.c("chunk_tri"), g[:, t, :], start=True, stop=True)
                    pe.matmul(k.ps[:, 4 + t, :], k.c("chunk_suffix"), g[:, t, :], start=True, stop=True)
                    for h in range(4):
                        i = 2 * (4 * t + h)
                        last = pe.matmul(k.ps[:, 6, i:i + 2], g[:, t, h * P:(h + 1) * P], k.c("chunk_ind"),
                                         start=True, stop=True)
                last.then_inc(cum_done, 1)
                pe.wait_ge(dec_ready, 1)
                turn(k, pe, q, 4, k.ps[:, 0:2, :].rearrange("p b (f t) -> p (b f) t", f=2), turned)
                turn(k, pe, a["k_inv"], 4, k.ps[:, 2:4, :].rearrange("p b (f t) -> p (b f) t", f=2), turned)

            @block.scalar
            def _(act):
                act.wait_ge(abs_ready, 1)
                act.activation(lg[:], lg[:], ACT.Exp, scale=-1.0)
                act.drain()
                act.activation(lg[:], lg[:], ACT.Ln, bias=1.0).then_inc(log_ready, 1)
                act.wait_ge(cum_done, 1)
                act.activation(eq[:], k.ps[:, 2:4, :], ACT.Exp)
                act.activation(ek[:], k.ps[:, 2:4, :], ACT.Exp, scale=-1.0)
                act.activation(ee[:], k.ps[:, 4:6, :], ACT.Exp)
                act.activation(a["decay"][:], k.ps[:, 6, 0:16], ACT.Exp).then_inc(exp_done, 1)

            @block.vector
            def _(dve):
                dve.memset(a["att"][:], 0.0)
                dve.wait_ge(r_done, 1)
                dve.tensor_copy(rT[:], k.ps[0:16, 7, 0:TOK]).then_inc(rT_ready, 1)
                dve.wait_ge(g_pre, 1)
                dve.tensor_tensor(g[:], k.ps[:, 0:2, :], bc(k.row("gla_bias"), 1, TT), ALU.add)
                dve.drain()
                dve.scalar_tensor_tensor(out=lg[:], in0=g[:], scalar=-1.0, in1=g[:], op0=ALU.mult,
                                         op1=ALU.max).then_inc(abs_ready, 1)
                dve.wait_ge(log_ready, 1)
                dve.scalar_tensor_tensor(out=g[:], in0=g[:], scalar=0.0, in1=lg[:], op0=ALU.min, op1=ALU.subtract)
                dve.drain()
                dve.tensor_scalar(g[:], g[:], 1.0 / 16.0, None, ALU.mult).then_inc(g_ready, 1)
                dve.wait_ge(exp_done, 1)
                dve.scalar_tensor_tensor(out=q, in0=q, scalar=128 ** -0.5, in1=eq[:], op0=ALU.mult, op1=ALU.mult)
                dve.tensor_tensor(a["k_inv"][:], key, ek[:], ALU.mult)
                dve.drain()
                dve.tensor_tensor(key, key, ee[:], ALU.mult).then_inc(dec_ready, 1)
                dve.wait_ge(turned, 8)
                dve.tensor_copy(a["qT"][:], k.ps[:, 0:2, :].rearrange("p b (f t) -> p (b f) t", f=2))
                dve.tensor_copy(a["kT"][:], k.ps[:, 2:4, :].rearrange("p b (f t) -> p (b f) t", f=2))


def stage_gla(k, a):
    HT = TOK // 2
    with ExitStack() as ctx:
        junk = k.sb("o_sq", [P, 512], ctx=ctx)
        ss = k.sb("o_ss", [P, 8], ctx=ctx)
        rstd = k.sb("o_rstd", [P, 8], ctx=ctx)
        att_done, att_ready, upd_done, state_ready, tile_out, o_ready, o_copied, summed, rstd_ready, o_normed, turned, gated = (
            k.sem(s) for s in ("att_done", "att_ready", "state_update_done", "state_ready", "o_tile_out", "o_ready",
                               "o_copied", "o_summed", "o_rstd_ready", "o_normed", "o_turned", "o_gated"))
        state, v, key = a["state"], a["v"], a["qk"][:, :, 512:1024]
        half = lambda c: slice(64 * c, 64 * c + 64)
        ups = lambda h: k.ps[:, 4 + h, :]
        with k.nc.Block() as block:
            @block.tensor
            def _(pe):
                for h in range(4):
                    for t in range(TT):
                        s = slice(t * P, (t + 1) * P)
                        last = pe.matmul(k.ps[:, 4 + h // 2, 256 * (h % 2) + t * P:256 * (h % 2) + (t + 1) * P],
                                         a["kT"][:, h, s], a["qT"][:, h, s], start=True, stop=True)
                last.then_inc(att_done, 1)
                pe.wait_ge(att_ready, 1)

                def inter(t, c, stop):
                    for h in range(4):
                        pe.wait_ge(state_ready, 4 * (2 * t + c - 1) + h + 1)
                        last = pe.matmul(k.ps[half(c), h, :], a["qT"][:, h, t * P + 64 * c:t * P + 64 * c + 64],
                                         state[:, h, :], start=False, stop=stop, skip_group_check=True)
                    return last

                def update(t, c):
                    for h in range(4):
                        if 2 * t + c:
                            pe.wait_ge(state_ready, 4 * (2 * t + c - 1) + h + 1)
                        last = pe.matmul(ups(h), key[half(c), t, h * P:(h + 1) * P], v[half(c), t, h * 512:(h + 1) * 512],
                                         start=True, stop=True)
                        last.then_inc(upd_done, 1)

                for t in range(TT):
                    if t:
                        pe.wait_ge(tile_out, 1)
                    for h in range(4):
                        last = pe.matmul(k.ps[:, h, :], a["att"][:, 2 * h + t, :], v[:, t, h * 512:(h + 1) * 512],
                                         start=True, stop=False, skip_group_check=True)
                    if t:
                        inter(t, 0, False)
                    update(t, 0)
                    last = inter(t, 1, True)
                    if t == 0:
                        update(t, 1)
                    last.then_inc(o_ready, 1) if t else pe.sem_inc(o_ready, 1)
                for r in range(2):
                    pe.wait_ge(o_normed, 1)
                    turn(k, pe, v[:, :, r * 1024:(r + 1) * 1024], KD,
                         k.ps[:, 4 * r:4 * r + 4, :].rearrange("p b (f t) -> p (b f) t", f=2), turned)

            @block.vector
            def _(dve):
                dve.wait_ge(att_done, 1)
                dve.copy_predicated(a["att"][:], bc(k.c("chunk_tri"), 1, 8).bitcast(U32),
                                    k.ps[:, 4:6, :].rearrange("p b (i t) -> p (b i) t", i=4)).then_inc(att_ready, 1)
                for t, c in ((0, 0), (0, 1), (1, 0)):
                    for h in range(4):
                        i = 2 * t + c
                        dve.wait_ge(upd_done, 4 * i + h + 1)
                        if i == 0:
                            ins = dve.tensor_copy(state[:, h, :], ups(h))
                        else:
                            j = 2 * (4 * t + h) + c
                            ins = dve.scalar_tensor_tensor(out=state[:, h, :], in0=state[:, h, :],
                                                           scalar=a["decay"][:, j:j + 1], in1=ups(h),
                                                           op0=ALU.mult, op1=ALU.add)
                        ins.then_inc(state_ready, 1)
                    dve.drain()
                    if (t, c) == (0, 1):
                        dve.wait_ge(o_ready, 1)
                        dve.tensor_copy(v[:, 0, :].rearrange("p (h e) -> p h e", h=4), k.ps[:, 0:4, :]).then_inc(tile_out, 1)
                dve.wait_ge(o_ready, 2)
                dve.tensor_copy(v[:, 1, :].rearrange("p (h e) -> p h e", h=4), k.ps[:, 0:4, :]).then_inc(o_copied, 1)
                dve.wait_ge(rstd_ready, 1)
                for t in range(TT):
                    for h in range(4):
                        o = v[:, t, h * 512:(h + 1) * 512]
                        i = 4 * t + h
                        last = dve.scalar_tensor_tensor(out=o, in0=o, scalar=rstd[:, i:i + 1], in1=k.row("gla_out_g"),
                                                        op0=ALU.mult, op1=ALU.mult)
                last.then_inc(o_normed, 1)
                for r in range(2):
                    dve.wait_ge(turned, KD * (r + 1))
                    z = a["zT"][:, 8 * r:8 * r + 8, :]
                    dve.tensor_tensor(z, z, k.ps[:, 4 * r:4 * r + 4, :].rearrange("p b (f t) -> p (b f) t", f=2), ALU.mult)

            @block.scalar
            def _(act):
                act.wait_ge(tile_out, 1)
                act.wait_ge(o_copied, 1)
                for t in range(TT):
                    for h in range(4):
                        i = 4 * t + h
                        act.activation(junk[:], v[:, t, h * 512:(h + 1) * 512], ACT.Square,
                                       accum_out=ss[:, i:i + 1]).then_inc(summed, 1)
                        act.drain()

            @block.gpsimd
            def _(pool):
                pool.wait_ge(summed, 8)
                rsqrt_mean(k, pool, rstd[:], ss[:], 512).then_inc(rstd_ready, 1)


def stage_memory_attention(k, a, name):
    with ExitStack() as ctx:
        p = k.sb(f"{name}_p", [P, 8, TOK], ctx=ctx)
        pT = k.sb(f"{name}_pT", [P, 4, 2, TOK], ctx=ctx)
        mx = k.sb(f"{name}_mx", [P, 8], ctx=ctx)
        rs = k.sb(f"{name}_rs", [P, 8], ctx=ctx)
        scored, max_ready, exp_done, p_ready, turned, pT_ready, out_done = (
            k.sem(f"{name}_{s}") for s in ("scored", "max_ready", "exp_done", "p_ready", "p_turned", "pT_ready", "out_done"))
        s_ps = k.ps[:, 0:4, :].rearrange("p h (t m) -> p (h t) m", t=2)
        t_ps = k.ps[:, 4:8, :].rearrange("p h (m t) -> p h m t", m=2)
        o_ps = k.ps[:, 0:4, :].rearrange("p b (f t) -> p (b f) t", f=2)
        with k.nc.Block() as block:
            @block.tensor
            def _(pe):
                for h in range(4):
                    for t in range(TT):
                        for c in range(2):
                            last = pe.matmul(s_ps[:, 2 * h + t, :], a["xqT"][:, 2 * h + c, t * P:(t + 1) * P],
                                             a["kmT"][:, 2 * h + c, :], start=(c == 0), stop=(c == 1))
                last.then_inc(scored, 1)
                pe.wait_ge(p_ready, 1)
                for h in range(4):
                    for m in range(2):
                        for t in range(TT):
                            last = pe.transpose(t_ps[:, h, m, t * P:(t + 1) * P], p[:, 2 * h + t, m * P:(m + 1) * P],
                                                k.c("ident"))
                last.then_inc(turned, 1)
                pe.wait_ge(pT_ready, 1)
                for f in range(8):
                    for m in range(2):
                        last = pe.matmul(o_ps[:, f, :], a["vm"][:, m, f * P:(f + 1) * P], pT[:, f // 2, m, :],
                                         start=(m == 0), stop=(m == 1))
                last.then_inc(out_done, 1)

            @block.scalar
            def _(act):
                act.wait_ge(max_ready, 1)
                for i in range(8):
                    last = act.activation(p[:, i, :], s_ps[:, i, :], ACT.Exp, bias=mx[:, i:i + 1], scale=1.0 / 16.0,
                                          accum_out=rs[:, i:i + 1])
                last.then_inc(exp_done, 1)

            @block.vector
            def _(dve):
                dve.wait_ge(scored, 1)
                dve.tensor_reduce(mx[:], s_ps[:], AX, ALU.max)
                dve.drain()
                dve.tensor_scalar(mx[:], mx[:], -1.0 / 16.0, None, ALU.mult).then_inc(max_ready, 1)
                dve.wait_ge(exp_done, 1)
                dve.reciprocal(rs[:], rs[:])
                dve.drain()
                for i in range(8):
                    last = dve.tensor_scalar(p[:, i, :], p[:, i, :], rs[:, i:i + 1], None, ALU.mult)
                last.then_inc(p_ready, 1)
                dve.wait_ge(turned, 1)
                dve.tensor_copy(pT[:], t_ps[:]).then_inc(pT_ready, 1)
                dve.wait_ge(out_done, 1)
                z = a["zT"][:, 16:24, :]
                dve.tensor_tensor(z, z, o_ps[:], ALU.mult)


def out_specs(k, zT):
    return [("tm", zT, 8 * kb, "dve", add_after(k.x[:, :, n * 512:(n + 1) * 512])) for n in range(2) for kb in range(3)]


def gla_layer(k):
    with ExitStack() as ctx:
        sb = lambda n, s: k.sb(n, s, ctx=ctx)
        a = {"zT": sb("gla_zT", [P, 24, TOK])}
        with ExitStack() as mid:
            sm = lambda n, s: k.sb(n, s, ctx=mid)
            a |= {"xqT": sm("gla_xqT", [P, 8, TOK]), "kmT": sm("gla_kmT", [P, 8, TOK]), "vm": sm("gla_vm", [P, TT, 1024])}
            with ExitStack() as inner:
                si = lambda n, s: k.sb(n, s, ctx=inner)
                a |= {"w_rank": si("w_rank", [P, KD, 16]), "w_up": si("w_up", [16, 512]),
                      "qk": si("gla_qk", [P, TT, 1024]), "v": si("gla_v", [P, TT, 2048])}
                low_in = k.sem("low_rank_in")
                rows = k.hold_rows(("gla_bias", "gla_out_g"), inner)

                def load(sp):
                    sp.dma_start(a["w_rank"][:], k.dram["w_rank"]).then_inc(low_in, 16)
                    sp.dma_start(a["w_up"][:], k.dram["w_up"]).then_inc(low_in, 16)
                    sp.dma_start(*rows).then_inc(low_in, 16)
                    sp.wait_ge(low_in, 48)

                zf = lambda m: a["zT"][:, 4 * m:4 * m + 4, :]
                specs = [("tm", k.hT, 0, "dve", copy_to(a["qk"][:, :, m * 512:(m + 1) * 512])) for m in range(2)]
                specs += [("tm", k.hT, 0, "dve", copy_to(a["v"][:, :, m * 512:(m + 1) * 512])) for m in range(4)]
                specs += [("fm", k.hT, 0, "act", silu_to(zf(m))) for m in range(6)]
                specs += [("fm", k.hT, 0, "dve", copy_to(a["xqT"][:, 4 * m:4 * m + 4, :])) for m in range(2)]
                specs += [("fm", k.memT, 0, "dve", copy_to(a["kmT"][:, 4 * m:4 * m + 4, :])) for m in range(2)]
                specs += [("tm", k.memT, 0, "dve", copy_to(a["vm"][:, :, m * 512:(m + 1) * 512])) for m in range(2)]
                stage_tiles(k, "gla_in", T_GLA, specs, sp_extra=load)
                with ExitStack() as rec:
                    sr = lambda n, s: k.sb(n, s, ctx=rec)
                    a |= {"k_inv": sr("k_inv", [P, TT, 512]), "decay": sr("decay", [P, 16]),
                          "state": None, "qT": k.hT[:, 0:4, :], "kT": k.hT[:, 4:8, :], "att": sr("att", [P, 8, P])}
                    stage_gla_gate(k, a)
                    a["state"] = sr("state", [P, 4, 512])
                    stage_gla(k, a)
            stage_memory_attention(k, a, "xa0")
        stage_tiles(k, "gla_out", T_GLA_OUT, out_specs(k, a["zT"]))
        xn = k.sb("xn3", [P, TT, D], ctx=ctx)
        norm_stage(k, NormT(k, "s5_norm", k.x, ctx, xn), k.col("norm_w_2", 8, KD))


def norm_stage(k, norm, gain):
    with k.nc.Block() as block:
        @block.scalar
        def _(act):
            norm.act(act)

        @block.gpsimd
        def _(pool):
            norm.pool(pool)

        @block.vector
        def _(dve):
            norm.dve_scale(dve)
            norm.dve_out(dve, k.hT, gain)

        @block.tensor
        def _(pe):
            norm.pe(pe)


def stage_s5_input(k, a):
    n = 1024
    with ExitStack() as ctx:
        sb = lambda name, w: k.sb(name, [P, w], ctx=ctx)
        lr, li, ls, dt = sb("lam_re", n), sb("lam_im", n), sb("log_step", 16), sb("dt", 16)
        mag, th, s, c, t1, t2 = (sb(f"s5_{x}", n) for x in ("mag", "th", "sin", "cos", "t1", "t2"))
        lrs, lis, lss = sb("lam_re_s", 64), sb("lam_im_s", 64), sb("log_step_s", 64)
        ts, red = sb("theta_s", 64), sb("theta_red", 64)
        lam_in, dt_ready, args_ready, trig_ready, u_out = (
            k.sem(x) for x in ("lam_in", "dt_ready", "s5_args_ready", "s5_trig_ready", "u_out"))
        by_tile = lambda x: x[:].rearrange("p (f s) -> p f s", f=16)
        with k.nc.Block() as block:
            @block.sync
            def _(sp):
                for dst, name in ((lr, "lam_re_f"), (li, "lam_im_f"), (ls, "log_step_f"), (lrs, "lam_re_s"),
                                  (lis, "lam_im_s"), (lss, "log_step_s")):
                    sp.dma_start(dst[:], k.dram[name]).then_inc(lam_in, 16)
                stream(k, sp, T_S5, T_S5 + 4)

            @block.tensor
            def _(pe):
                for m in range(4):
                    if m == 3:
                        pe.wait_ge(u_out, 1)
                    fm_tile(k, pe, T_S5 + m, k.hT, pair_fm(k, m))

            @block.scalar
            def _(act):
                act.wait_ge(lam_in, 96)
                act.activation(dt[:], ls[:], ACT.Exp)
                act.activation(lss[:], lss[:], ACT.Exp).then_inc(dt_ready, 1)

                def u_tile(m):
                    act.wait_ge(k.tile_done, T_S5 + m + 1)
                    act.copy(a["uT"][:, 4 * m:4 * m + 4, :], pair_fm(k, m)).then_inc(u_out, 1)

                u_tile(0)
                act.wait_ge(args_ready, 1)
                act.activation(mag[:], mag[:], ACT.Exp)
                act.activation(a["decay"][:], a["decay"][:], ACT.Exp)
                act.activation(s[:], th[:], ACT.Sin)
                act.activation(c[:], c[:], ACT.Sin).then_inc(trig_ready, 1)
                for m in range(1, 4):
                    u_tile(m)

            @block.vector
            def _(dve):
                dve.memset(a["half_pi"][:], float(np.pi / 2))
                dve.wait_ge(dt_ready, 1)
                dtb = bc(dt[:], 2, 64)
                dve.tensor_tensor(by_tile(mag), by_tile(lr), dtb, ALU.mult)
                dve.tensor_tensor(by_tile(t1), by_tile(li), dtb, ALU.mult)
                dve.tensor_tensor(a["decay"][:], lrs[:], lss[:], ALU.mult)
                dve.tensor_tensor(ts[:], lis[:], lss[:], ALU.mult)
                dve.drain()
                range_reduce(dve, th[:], t2[:], t1[:])
                dve.drain()
                quarter_turn(dve, c[:], t2[:], th[:])
                dve.drain()
                range_reduce(dve, red[:], lss[:], ts[:])
                dve.drain()
                dve.tensor_scalar(a["turns"][:], red[:], 1.0 / TWO_PI, None, ALU.mult).then_inc(args_ready, 1)
                dve.wait_ge(trig_ready, 1)
                dve.tensor_tensor(c[:], c[:], mag[:], ALU.mult)
                dve.tensor_tensor(s[:], s[:], mag[:], ALU.mult)
                dve.tensor_tensor(t1[:], lr[:], lr[:], ALU.mult)
                dve.tensor_tensor(t2[:], li[:], li[:], ALU.mult)
                dve.drain()
                dve.tensor_scalar(c[:], c[:], -1.0, None, ALU.add)
                dve.tensor_tensor(t1[:], t1[:], t2[:], ALU.add)
                dve.drain()
                dve.reciprocal(t1[:], t1[:])
                dve.tensor_tensor(mag[:], c[:], lr[:], ALU.mult)
                dve.tensor_tensor(th[:], s[:], li[:], ALU.mult)
                dve.drain()
                dve.tensor_tensor(mag[:], mag[:], th[:], ALU.add)
                dve.tensor_tensor(s[:], s[:], lr[:], ALU.mult)
                dve.tensor_tensor(c[:], c[:], li[:], ALU.mult)
                dve.drain()
                dve.tensor_tensor(a["coef_re"][:], mag[:], t1[:], ALU.mult)
                dve.tensor_tensor(s[:], s[:], c[:], ALU.subtract)
                dve.drain()
                dve.tensor_tensor(a["coef_im"][:], s[:], t1[:], ALU.mult)


S5_STEPS = 8


def stage_s5_scan(k, a):
    with ExitStack() as ctx:
        sb = lambda name, s: k.sb(name, s, ctx=ctx)
        braw, bb, bt = sb("b_raw", [P, 2, 2, P]), sb("b_bar", [P, 2, 2, P]), sb("b_tmp", [P, P])
        craw, u_stage = sb("c_raw", [P, 2, 4, 2, 32]), sb("u_stage", [P, 2, TOK])
        frac = sb("s5_frac", [P, 4, TOK])
        sin, cos = ([sb(f"s5_{x}{i}", [P, 4, TOK]) for i in range(2)] for x in ("sin", "cos"))
        pa, pb, pc, pd = (sb(f"s5_{x}", [P, 4, TOK]) for x in ("pa", "pb", "pc", "pd"))
        x_re, x_im, t_re, t_im = (sb(f"s5_{x}", [P, 4, TOK]) for x in ("x_re", "x_im", "t_re", "t_im"))
        b_in = [k.sem(f"s5_b_in_{i}") for i in range(2)]
        c_in = [k.sem(f"s5_c_in_{i}") for i in range(2)]
        names = ("b_bar_ready", "bu_done", "u_staged", "phi_ready", "turn_ready", "frac_ready", "rotated_out", "x_ready",
                 "y_done", "y_out", "tile_out", "table_used")
        (bb_ready, bu_done, u_staged, phi_ready, turn_ready, frac_ready, rotated, x_ready, y_done, y_out, tile_out,
         table_used) = (k.sem(f"s5_{x}") for x in names)
        dense = k.ps[:, 6:8, :].rearrange("p b (f t) -> p (b f) t", f=2)
        first = T_S5 + 4
        N = S5_STEPS
        after_step = {1: 0, 3: 1, 5: 2}
        iota = k.c("iota256")
        bur, bui = (k.ps[:, 0:4, c * TOK:(c + 1) * TOK] for c in range(2))
        with k.nc.Block() as block:
            @block.sync
            def _(sp):
                with sp.Fori(0, 2) as r:
                    for q in range(N):
                        sp.wait_ge(y_out, r * N + (q + 1))
                        f = bass.ds(r * N + q, 1)
                        sp.dma_start(braw[:, q % 2], k.dram["s5_b"][f].rearrange("a p c s -> (a p) c s")).then_inc(b_in[q % 2], 16)
                        sp.dma_start(craw[:, q % 2], k.dram["s5_c"][f].rearrange("a p q c h -> (a p) q c h")).then_inc(c_in[q % 2], 16)
                        if q - 2 in after_step:
                            j = after_step[q - 2]
                            slot = (first + j) % RING
                            sp.wait_ge(k.tile_done, r * 3 + (first + j + 1))
                            sp.dma_start(k.ring[:, slot, :], k.dram["weights"][bass.ds(r * 3 + (first + j + RING), 1)]
                                         .rearrange("a p n -> (a p) n")).then_inc(k.landed[slot], 16)

            @block.gpsimd
            def _(pool):
                with pool.Fori(0, 2) as r:
                    for q in range(N + 1):
                        if q < N:
                            b, s = q % 2, r * N + q
                            pool.wait_ge(b_in[b], r * (8 * N) + 16 * (q // 2 + 1))
                            pool.wait_ge(y_out, s + 1)
                            cr, ci = (bc(a[x][:, bass.ds(r * (64 * N) + 64 * q, 64)], 1, 2) for x in ("coef_re", "coef_im"))
                            b_re, b_im = (braw[:, b, x].rearrange("p (g s) -> p g s", g=2) for x in range(2))
                            o_re, o_im = (bb[:, b, x].rearrange("p (g s) -> p g s", g=2) for x in range(2))
                            tmp = bt[:].rearrange("p (g s) -> p g s", g=2)
                            pool.tensor_tensor(o_re, b_re, cr, ALU.mult)
                            pool.tensor_tensor(tmp, b_im, ci, ALU.mult)
                            pool.tensor_tensor(o_im, b_im, cr, ALU.mult)
                            pool.drain()
                            pool.tensor_tensor(o_re, o_re, tmp, ALU.subtract)
                            pool.drain()
                            pool.tensor_tensor(tmp, b_re, ci, ALU.mult)
                            pool.drain()
                            pool.tensor_tensor(o_im, o_im, tmp, ALU.add).then_inc(bb_ready, 1)
                            pool.drain()
                        if q:
                            pool.wait_ge(rotated, r * N + q)
                            pool.tensor_tensor(x_re[:], x_re[:], t_re[:], ALU.add)
                            pool.tensor_tensor(x_im[:], x_im[:], t_im[:], ALU.subtract)
                            pool.drain()
                            pool.sem_inc(x_ready, 1)

            @block.tensor
            def _(pe):
                with pe.Fori(0, 2) as r:
                    def bu(q):
                        pe.wait_ge(bb_ready, r * N + (q + 1))
                        pe.wait_ge(u_staged, r * N + (q + 1))
                        for j in range(4):
                            rows = slice(32 * j, 32 * j + 32)
                            for c in range(2):
                                last = pe.matmul(k.ps[:, j, c * TOK:(c + 1) * TOK], bb[rows, q % 2, c, :],
                                                 u_stage[rows, q % 2, :], start=True, stop=True)
                        last.then_inc(bu_done, 1)

                    bu(0)
                    for q in range(N):
                        if q < N - 1:
                            bu(q + 1)
                        if q in after_step:
                            j = after_step[q]
                            slot, full = (first + j) % RING, 16 * ((first + j) // RING + 1)
                            pe.wait_ge(tile_out, r * 3 + (j + 1))
                            pe.wait_ge(k.landed[slot], r * 16 + full)
                            w = k.ring[:, slot, :].rearrange("p (k n) -> p k n", k=KD)
                            for f in range(4):
                                for kk in range(KD):
                                    last = pe.matmul(dense[:, f, :], w[:, kk, f * P:(f + 1) * P], k.hT[:, kk, :],
                                                     start=(kk == 0), stop=(kk == KD - 1))
                            last.then_inc(k.tile_done, 1)
                        pe.wait_ge(x_ready, r * N + (q + 1))
                        pe.wait_ge(c_in[q % 2], r * (8 * N) + 16 * (q // 2 + 1))
                        for j in range(4):
                            o = k.ps[32 * j:32 * j + 32, 4 + q % 2, 0:TOK]
                            pe.matmul(o, craw[:, q % 2, j, 0, :], x_re[:, j, :], start=True, stop=False)
                            last = pe.matmul(o, craw[:, q % 2, j, 1, :], x_im[:, j, :], start=False, stop=True)
                        last.then_inc(y_done, 1)

            @block.scalar
            def _(act):
                with act.Fori(0, 2) as r:
                    def tables(q):
                        b = q % 2
                        act.wait_ge(table_used, r * N + (q + 1))
                        for j in range(4):
                            last = act.activation(sin[b][:, j, :], iota, ACT.Copy,
                                                  scale=a["turns"][:, bass.ds(r * (4 * N) + (4 * q + j), 1)])
                        last.then_inc(phi_ready, 1)
                        act.wait_ge(frac_ready, r * N + (q + 1))
                        act.activation(sin[b][:], frac[:], ACT.Sin, scale=6.2831845)
                        act.activation(cos[b][:], frac[:], ACT.Abs)
                        act.drain()
                        act.activation(cos[b][:], cos[b][:], ACT.Sin, scale=-6.2831845,
                                       bias=a["half_pi"][:]).then_inc(turn_ready, 1)

                    tables(0)
                    for q in range(N):
                        if q < N - 1:
                            tables(q + 1)
                        if q in after_step:
                            j = after_step[q]
                            act.wait_ge(k.tile_done, r * 3 + (first + j + 1))
                            act.activation(a["zT"][:, bass.ds(r * 12 + 4 * j, 4), :], dense[:], ACT.Copy).then_inc(tile_out, 1)

            @block.vector
            def _(dve):
                dve.sem_inc(y_out, 2)
                dve.sem_inc(table_used, 2)
                dve.sem_inc(tile_out, 1)
                with dve.Fori(0, 2) as r:
                    def feature(q):
                        return a["uT"][:, bass.ds(r * N + q, 1), :].rearrange("p a t -> p (a t)")

                    def stage_u(q):
                        dve.tensor_copy(u_stage[:, q % 2, :], feature(q)).then_inc(u_staged, 1)

                    def fraction(q):
                        b = q % 2
                        dve.wait_ge(phi_ready, r * N + (q + 1))
                        dve.tensor_scalar(frac[:], sin[b][:], ROUND, -ROUND, ALU.add, ALU.add)
                        dve.drain()
                        dve.tensor_tensor(frac[:], sin[b][:], frac[:], ALU.subtract).then_inc(frac_ready, 1)

                    def take_y(q):
                        dve.wait_ge(y_done, r * N + (q + 1))
                        dve.scalar_tensor_tensor(out=feature(q), in0=feature(q), in1=k.ps[:, 4 + q % 2, 0:TOK],
                                                 scalar=k.cols[:, bass.ds(r * N + (COLS["s5_d"][0] + q), 1)],
                                                 op0=ALU.mult, op1=ALU.add).then_inc(y_out, 1)

                    stage_u(0)
                    fraction(0)
                    for q in range(N):
                        b = q % 2
                        dve.wait_ge(turn_ready, r * N + (q + 1))
                        dve.wait_ge(bu_done, r * N + (q + 1))
                        dve.tensor_tensor(pa[:], bur, cos[b][:], ALU.mult)
                        dve.tensor_tensor(pb[:], bui, sin[b][:], ALU.mult)
                        dve.tensor_tensor(pc[:], bur, sin[b][:], ALU.mult)
                        dve.tensor_tensor(pd[:], bui, cos[b][:], ALU.mult)
                        dve.drain()
                        if q < N - 1:
                            stage_u(q + 1)
                        dve.tensor_tensor(pa[:], pa[:], pb[:], ALU.add)
                        dve.tensor_tensor(pc[:], pc[:], pd[:], ALU.subtract)
                        if q < N - 1:
                            fraction(q + 1)
                        dve.drain()
                        for j in range(4):
                            d = a["decay"][:, bass.ds(r * (4 * N) + (4 * q + j), 1)].broadcast_to([P, TOK])
                            dve.tensor_tensor_scan(pb[:, j, :], d, pa[:, j, :], 0.0, ALU.mult, ALU.add)
                            dve.tensor_tensor_scan(pd[:, j, :], d, pc[:, j, :], 0.0, ALU.mult, ALU.add)
                        dve.drain()
                        if q:
                            take_y(q - 1)
                        dve.tensor_tensor(x_re[:], pb[:], cos[b][:], ALU.mult)
                        dve.tensor_tensor(t_re[:], pd[:], sin[b][:], ALU.mult)
                        dve.tensor_tensor(x_im[:], pd[:], cos[b][:], ALU.mult)
                        dve.tensor_tensor(t_im[:], pb[:], sin[b][:], ALU.mult).then_inc(rotated, 1)
                        dve.drain()
                        dve.sem_inc(table_used, 1)
                    take_y(N - 1)


def stage_glu_gate(k, a):
    sig_ready, gated = k.sem("sig_ready"), k.sem("y_gated")
    with k.nc.Block() as block:
        @block.scalar
        def _(act):
            for f in range(16):
                act.activation(a["glu"][:, f, :], a["glu"][:, f, :], ACT.Sigmoid, bias=k.col("s5_b_glu", f)).then_inc(sig_ready, 1)

        @block.vector
        def _(dve):
            z = a["zT"][:, 0:16, :]
            dve.tensor_tensor(z, z, a["uT"][:], ALU.mult)
            dve.wait_ge(sig_ready, 16)
            dve.drain()
            dve.tensor_tensor(z, z, a["glu"][:], ALU.mult)


def s5_layer(k):
    with ExitStack() as ctx:
        uT = k.sb("uT", [P, 16, TOK], ctx=ctx)
        a = {"uT": uT}
        a["zT"] = k.sb("s5_zT", [P, 24, TOK], ctx=ctx)
        with ExitStack() as rec:
            for n in ("coef_re", "coef_im"):
                a[n] = k.sb(n, [P, 1024], ctx=rec)
            a["decay"], a["turns"] = k.sb("s5_decay", [P, 64], ctx=rec), k.sb("s5_turns", [P, 64], ctx=rec)
            a["half_pi"] = k.sb("half_pi", [P, 1], ctx=rec)
            stage_s5_input(k, a)
            stage_s5_scan(k, a)
        with ExitStack() as mid:
            sm = lambda n, s: k.sb(n, s, ctx=mid)
            a |= {"xqT": sm("s5_xqT", [P, 8, TOK]), "kmT": sm("s5_kmT", [P, 8, TOK]), "vm": sm("s5_vm", [P, TT, 1024])}
            specs = [("fm", k.hT, 0, "dve", copy_to(a["xqT"][:, 4 * m:4 * m + 4, :])) for m in range(2)]
            specs += [("fm", k.memT, 0, "dve", copy_to(a["kmT"][:, 4 * m:4 * m + 4, :])) for m in range(2)]
            specs += [("tm", k.memT, 0, "dve", copy_to(a["vm"][:, :, m * 512:(m + 1) * 512])) for m in range(2)]

            def activate(act):
                act.activation(uT[:], uT[:], ACT.Gelu_apprx_tanh)
                act.activation(a["zT"][:], a["zT"][:], ACT.Silu)

            stage_tiles(k, "s5_in", T_S5 + 10, specs, act_extra=activate)
            stage_memory_attention(k, a, "xa1")
        a["glu"] = k.sb("glu", [P, 16, TOK], ctx=ctx)
        specs = []
        for n in range(4):
            g = a["glu"][:, 4 * n:4 * n + 4, :]
            specs += [("fm", uT, 0, "dve", copy_to(g)), ("fm", uT, 8, "dve", add_after(g))]
        stage_tiles(k, "glu", T_GLU, specs)
        stage_glu_gate(k, a)
        stage_tiles(k, "s5_out", T_S5_OUT, out_specs(k, a["zT"]))


def final_norm(k):
    with ExitStack() as ctx:
        xn = k.sb("xn4", [P, TT, D], ctx=ctx)
        norm = NormT(k, "final", k.x, ctx, xn)
        rows, rows_in = k.hold_rows(("final_norm",), ctx), k.sem("final_row_in")
        with k.nc.Block() as block:
            @block.sync
            def _(sp):
                sp.dma_start(*rows).then_inc(rows_in, 16)

            @block.scalar
            def _(act):
                norm.act(act)

            @block.gpsimd
            def _(pool):
                norm.pool(pool)

            @block.vector
            def _(dve):
                dve.wait_ge(rows_in, 16)
                dve.wait_ge(norm.rstd_ready, 1)
                for t in range(TT):
                    dve.scalar_tensor_tensor(out=k.x[:, t, :], in0=k.x[:, t, :], scalar=norm.rstd[:, t:t + 1],
                                             in1=k.row("final_norm"), op0=ALU.mult, op1=ALU.mult)


def build(nc, dram, out):
    with ExitStack() as ctx:
        k = Core(nc, ctx, dram)
        first_block(k)
        k.clear_stage_sems()
        gla_layer(k)
        k.clear_stage_sems()
        s5_layer(k)
        final_norm(k)
        store(k, out)


def store(k, out):
    stored = k.sem("stored")
    with k.nc.Block() as block:
        @block.sync
        def _(sp):
            sp.dma_start(out.rearrange("a (t p) d -> p (a t) d", p=P), k.x[:]).then_inc(stored, 16)
            sp.wait_ge(stored, 16)



def constants():
    c = np.zeros((P, N_CONST), np.float32)
    p = np.arange(P)

    def put(name, value):
        a, b = CONSTS[name]
        c[:, a:b] = np.asarray(value, np.float32).reshape(P, -1)

    put("ident", np.eye(P))
    q = p[:, None, None] + P * np.arange(TT)[None, :, None]
    put("causal", np.where(np.arange(TOK)[None, None, :] <= q, 0.0, NEG))
    put("causal_t", np.where(p[:, None] <= p[None, :], 0.0, NEG))
    put("inv_freq", np.tile(np.float32(10000.0) ** (-np.arange(32, dtype=np.float32) / np.float32(32)), (P, 1)))
    put("iota64", np.tile(np.arange(64), (P, 1)))
    hot = np.zeros((P, 4, P))
    for h in range(4):
        hot[h, h] = 1.0
    put("one_hot4", hot)
    same = p[:, None] // 64 == p[None, :] // 64
    put("chunk_tri", same & (p[:, None] <= p[None, :]))
    put("chunk_suffix", same & (p[:, None] > p[None, :]))
    put("chunk_ind", p[:, None] // 64 == np.arange(2)[None, :])
    put("iota256", np.tile(np.arange(TOK), (P, 1)))
    put("minus_half", np.full((P, 16), -0.5))
    put("before", p[:, None] < p[None, :])
    put("ones", np.ones((P, P)))
    put("slot_limits", np.tile(SLOTS * np.arange(1, 4), (P, 1)))
    return c


def s5_arrays(g):
    lam_re, lam_im, step = g["s5_lam_re_2"][0], g["s5_lam_im_2"][0], g["s5_log_step_2"][0]

    def feature(v):
        v = v.reshape(16, 8, 1, -1)
        return np.broadcast_to(v, (16, 8, 16, v.shape[-1])).transpose(1, 2, 0, 3).reshape(P, -1)

    def state(v):
        return v.reshape(64, 2, 64).transpose(1, 2, 0).reshape(P, 64)

    b = np.zeros((16, 4, 2, 16, 2, 2, 64), np.float32)
    c = np.zeros((16, 2, 64, 4, 2, 2, 16), np.float32)
    for part, (bv, cv) in enumerate(((g["s5_b_re_2"][0], g["s5_c_re_2"][0]), (g["s5_b_im_2"][0], g["s5_c_im_2"][0]))):
        bv = bv.reshape(16, 4, 2, 64, 16)
        cv = cv.reshape(16, 4, 2, 16, 64)
        for q in range(2):
            b[:, :, q, :, part, q, :] = bv[:, :, q].transpose(0, 1, 3, 2)
            c[:, q, :, :, part, q, :] = cv[:, :, q].transpose(0, 3, 1, 2)
    return {
        "lam_re_f": feature(lam_re), "lam_im_f": feature(lam_im), "log_step_f": feature(step[:, None]),
        "lam_re_s": state(lam_re), "lam_im_s": state(lam_im),
        "log_step_s": state(np.broadcast_to(step[:, None], (P, 64))),
        "s5_b": b.reshape(16, P, 2, P), "s5_c": c.reshape(16, P, 4, 2, 32),
    }


def kernel(**inputs):
    import concourse.bacc as bacc
    from concourse.bass_utils import run_bass_kernel_spmd

    g = {n: np.asarray(v) for n, v in inputs.items()}

    def wide(w, rows=1024, width=512):
        kt, nt = w.shape[0] // rows, w.shape[1] // width
        w = w.reshape(kt, rows // P, P, nt, width).transpose(3, 0, 2, 1, 4)
        return w.reshape(nt * kt, P, TILE)

    w_in = g["w_in"][0]
    gla = g["gla_w_in_2"][0]
    ada = wide(g["w_ada"][0])
    kv = [wide(g["xa_w_kv_2"][i]) for i in range(2)]
    groups = [
        ada, wide(w_in[:, :3584]), wide(g["w_out"][0]),
        np.stack([g["w1"][0].reshape(N_EXP, KD, P, 512).transpose(0, 2, 1, 3).reshape(N_EXP, P, TILE),
                  g["w3"][0].reshape(N_EXP, KD, P, 512).transpose(0, 2, 1, 3).reshape(N_EXP, P, TILE),
                  g["w2"][0].reshape(N_EXP, 4, P, 1024).transpose(0, 2, 1, 3).reshape(N_EXP, P, TILE)],
                 axis=1).reshape(3 * N_EXP, P, TILE),
        wide(gla[:, :3072]), wide(gla[:, 3088:]), kv[0], wide(g["w_out_2"][0]),
        wide(g["s5_w_in_2"][0]), kv[1], wide(g["s5_w_glu_2"][0]), wide(g["w_out_2"][1]),
    ]
    experts = groups.pop(3)
    weights = np.concatenate(groups, axis=0)
    assert weights.shape[0] == T_END

    def by_feature(v, n):
        return v.reshape(n, P).T

    cols = np.zeros((P, N_COLS), np.float32)

    def put_col(name, value):
        a, b = COLS[name]
        cols[:value.shape[0], a:b] = value

    put_col("c", by_feature(g["c"][0], 8))
    b_ada = g["b_ada"][0].reshape(6, 1024)
    put_col("b_ada", by_feature(np.concatenate([b_ada[0], b_ada[1], b_ada[3], b_ada[4]]), 32))
    put_col("norm1_g", by_feature(g["norm1_g"][0], 8))
    put_col("norm2_g", by_feature(g["norm2_g"][0], 8))
    put_col("conv_w", g["conv_w"][0].reshape(4, 8, P).transpose(2, 1, 0).reshape(P, 32))
    put_col("conv_b", by_feature(g["conv_b"][0], 8))
    put_col("norm_w_2", by_feature(g["norm_w_2"], 16))
    put_col("mem_norm_w", by_feature(g["mem_norm_w_2"], 8))
    put_col("s5_d", by_feature(g["s5_d_2"][0], 16))
    put_col("s5_b_glu", by_feature(g["s5_b_glu_2"][0], 16))
    put_col("b_gate", g["b_gate"][0].reshape(2, 4).T)

    rows = np.concatenate([b_ada[2], b_ada[5], g["attn_out_g"][0], g["mlstm_out_g"][0], g["norm_f_g"], g["b_rg"][0],
                           g["b_re"][0], g["gla_gate_bias_2"][0], g["gla_out_norm_w_2"][0], g["final_norm_w_2"]])
    arrays = {
        "weights": weights, "experts": experts, "cols": cols, "rows": rows, "consts": constants(),
        "positions": g["positions"].reshape(TT, P).T,
        "x": g["x"].reshape(TT, P, D).transpose(1, 0, 2), "mem": g["mem_2"].reshape(TT, P, D).transpose(1, 0, 2),
        "w_gate": w_in[:, 3584:].reshape(KD, P, 8).transpose(1, 0, 2),
        "w_router": np.concatenate([g["w_rg"][0], g["w_re"][0]], axis=1).reshape(KD, P, 36).transpose(1, 0, 2),
        "w_rank": gla[:, 3072:3088].reshape(KD, P, 16).transpose(1, 0, 2), "w_up": g["gla_w_gate_up_2"][0],
        **s5_arrays(g),
    }
    nc = bacc.Bacc("TRN2", target_bir_lowering=False, num_devices=1)
    fed, dram = {}, {}
    for name, value in arrays.items():
        fed[f"in_{name}"] = np.ascontiguousarray(value)
        dram[name] = nc.dram_tensor(f"in_{name}", value.shape, mybir.dt.from_np(value.dtype), kind="ExternalInput").ap()
    out = nc.dram_tensor("out_0", (1, TOK, D), F32, kind="ExternalOutput").ap()
    build(nc, dram, out)
    return run_bass_kernel_spmd(nc, [fed], core_ids=[0]).results[0]["out_0"]
```

```python
from contextlib import ExitStack

import numpy as np
import concourse.bass as bass
from concourse import mybir

F32 = mybir.dt.float32
F32R = mybir.dt.float32r
BF16 = mybir.dt.bfloat16
I32 = mybir.dt.int32
U32 = mybir.dt.uint32
ALU = mybir.AluOpType
ACT = mybir.ActivationFunctionType
AX = mybir.AxisListType.X

P = 128
TOK = 256
TT = TOK // P
D = 1024
KD = D // P
EPS = 1e-6
NEG = -1e30
SLOTS = 64
RING = 3
TILE = 4096
PI = 3.1415925
TWO_PI = 2.0 * np.pi
TWO_PI_A = 6.28125
TWO_PI_B = float(np.float32(int((TWO_PI - TWO_PI_A) * 2 ** 21) / 2 ** 21))
TWO_PI_C = float(np.float32(TWO_PI - TWO_PI_A - TWO_PI_B))
ROUND = 12582912.0

N_ADA, N_IN, N_OUT, N_EXP = 12, 7, 2, 32
T_ADA = 0
T_IN = T_ADA + N_ADA
T_OUT = T_IN + N_IN
T_GLA = T_OUT + N_OUT
T_GLA_OUT = T_GLA + 18
T_S5 = T_GLA_OUT + 6
T_GLU = T_S5 + 16
T_S5_OUT = T_GLU + 8
T_END = T_S5_OUT + 6

CONSTS = {}
_at = 0
for _name, _n in (("ident", 128), ("fold", SLOTS), ("causal", 512), ("causal_t", 128), ("inv_freq", 32), ("iota64", 2 * SLOTS),
                  ("one_hot4", 512), ("chunk_tri", 128), ("chunk_suffix", 128), ("chunk_ind", 2),
                  ("iota256", 256), ("minus_half", 16),
                  ("before", 128), ("ones", 128), ("slot_limits", 3)):
    CONSTS[_name] = (_at, _at + _n)
    _at += _n
N_CONST = _at

COLS = {}
_at = 0
for _name, _n in (("c", 8), ("b_ada", 32), ("norm1_g", 8), ("norm2_g", 8), ("conv_w", 32), ("conv_b", 8),
                  ("norm_w_2", 16), ("mem_norm_w", 8), ("s5_d", 16), ("s5_b_glu", 16), ("b_gate", 2)):
    COLS[_name] = (_at, _at + _n)
    _at += _n
N_COLS = _at

ROWS = {}
_at = 0
for _name, _n in (("b_g1", 1024), ("b_g2", 1024), ("attn_out_g", 512), ("mlstm_out_g", 512), ("norm_f_g", 1024),
                  ("b_router", 36), ("gla_bias", 512), ("gla_out_g", 512), ("final_norm", 1024)):
    ROWS[_name] = (_at, _at + _n)
    _at += _n
N_ROWS = _at


class Core:

    def __init__(self, nc, ctx, dram):
        self.nc, self.ctx, self.dram = nc, ctx, dram
        self.ring = self.sb("ring", [P, RING, TILE])
        self.const = self.sb("const", [P, N_CONST])
        self.cols = self.sb("cols", [P, N_COLS])
        self.x = self.sb("x", [P, TT, D])
        self.hT = self.sb("hT", [P, KD, TOK])
        self.memT = self.sb("memT", [P, KD, TOK])
        self.small = self.sb("small", [P, 64])
        self.sin = self.sb("sin", [P, TT, 32])
        self.cos = self.sb("cos", [P, TT, 32])
        self.mod = self.sb("mod", [P, 32])
        self.ps = ctx.enter_context(nc.psum_tensor("ps", [P, 8, 512], F32))
        self.stage_sems = None
        self.landed = [self.sem(f"weights_landed_{j}") for j in range(RING)]
        self.tile_done = self.sem("tile_done")
        self.stage_sems = []

    def sb(self, name, shape, dt=F32, ctx=None):
        return (ctx or self.ctx).enter_context(self.nc.sbuf_tensor(name, shape, dt))

    def sem(self, name):
        if self.stage_sems is None:
            return self.ctx.enter_context(self.nc.semaphore(name))
        self.stage_sems.append(self.nc.alloc_semaphore(name))
        return self.stage_sems[-1]

    def clear_stage_sems(self):
        self.nc.clear_and_free_semaphores(self.stage_sems)
        self.nc.all_engine_barrier()
        self.stage_sems = []

    def c(self, name):
        a, b = CONSTS[name]
        return self.const[:, a:b]

    def col(self, name, i=0, n=1):
        a = COLS[name][0] + i
        return self.cols[:, a:a + n]

    def hold_rows(self, names, ctx):
        self.row_base, end = ROWS[names[0]][0], ROWS[names[-1]][1]
        self.rows = self.sb(f"rows_{names[0]}", [P, end - self.row_base], ctx=ctx)
        return self.rows[:], self.dram["rows"][self.row_base:end].partition_broadcast(P)

    def row(self, name):
        a, b = ROWS[name]
        return self.rows[:, a - self.row_base:b - self.row_base]

    def slot(self, n, k=8):
        return self.ring[:, n % RING, :].rearrange("p (k n) -> p k n", k=k)

    def wait_tile(self, pe, n):
        pe.wait_ge(self.landed[n % RING], 16 * (n // RING + 1))


def bc(ap, axis, n):
    ap = ap.unsqueeze(axis)
    shape = list(ap.shape)
    shape[axis] = n
    return ap.broadcast_to(shape)


def stream(k, sp, used_from, used_to):
    n0, n1 = used_from + RING, min(used_to + RING, T_END)
    if used_to < T_GLA:
        n1 = min(n1, T_GLA)

    def load(n, j):
        sp.wait_ge(k.tile_done, n - (RING - 1))
        sp.dma_start(k.ring[:, j, :], k.dram["weights"][n]).then_inc(k.landed[j], 16)

    body = (n1 - n0) // RING
    if body > 1:
        with sp.Fori(0, body) as i:
            for j in range(RING):
                sp.wait_ge(k.tile_done, i * RING + (n0 + j - (RING - 1)))
                sp.dma_start(k.ring[:, (n0 + j) % RING, :],
                             k.dram["weights"][bass.ds(i * RING + (n0 + j), 1)].rearrange("a p n -> (a p) n")
                             ).then_inc(k.landed[(n0 + j) % RING], 16)
        n0 += body * RING
    for n in range(n0, n1):
        load(n, n % RING)


def tm_tile(k, pe, n, lhs, out, k0=0):
    k.wait_tile(pe, n)
    w = k.slot(n)
    for t in range(TT):
        for kk in range(KD):
            last = pe.matmul(out[:, t, :], lhs[:, k0 + kk, t * P:(t + 1) * P], w[:, kk, :],
                             start=(kk == 0), stop=(kk == KD - 1))
    last.then_inc(k.tile_done, 1)


def fm_tile(k, pe, n, rhs, out, k0=0):
    k.wait_tile(pe, n)
    w = k.slot(n)
    for f in range(4):
        for kk in range(KD):
            last = pe.matmul(out[:, f, :], w[:, kk, f * P:(f + 1) * P], rhs[:, k0 + kk, :],
                             start=(kk == 0), stop=(kk == KD - 1))
    last.then_inc(k.tile_done, 1)


def pair(k, m):
    j = m % 3
    return k.ps[:, 2 * j:2 * j + 2, :]


def pair_fm(k, m):
    return pair(k, m).rearrange("p b (f t) -> p (b f) t", f=2)


class NormT:

    def __init__(self, k, name, x, ctx, xn):
        self.k, self.x, self.xn = k, x, xn
        self.ss = k.sb(f"{name}_ss", [P, TT], ctx=ctx)
        self.rstd = k.sb(f"{name}_rstd", [P, TT], ctx=ctx)
        self.summed = k.sem(f"{name}_squares_summed")
        self.rstd_ready = k.sem(f"{name}_rstd_ready")
        self.scaled = k.sem(f"{name}_scaled")
        self.turned = k.sem(f"{name}_turned")
        self.done = k.sem(f"{name}_done")

    def act(self, act):
        for t in range(TT):
            act.activation(self.xn[:, t, :], self.x[:, t, :], ACT.Square,
                           accum_out=self.ss[:, t:t + 1]).then_inc(self.summed, 1)

    def pool(self, pool):
        pool.wait_ge(self.summed, TT)
        rsqrt_mean(self.k, pool, self.rstd[:], self.ss[:], D).then_inc(self.rstd_ready, 1)

    def dve_scale(self, dve):
        dve.wait_ge(self.rstd_ready, 1)
        for t in range(TT):
            dve.tensor_scalar(self.xn[:, t, :], self.x[:, t, :], self.rstd[:, t:t + 1], None,
                              ALU.mult).then_inc(self.scaled, 1)

    def pe(self, pe):
        pe.wait_ge(self.scaled, TT)
        turn(self.k, pe, self.xn, KD, self.k.ps[:, 0:4, :].rearrange("p b (f t) -> p (b f) t", f=2), self.turned)

    def dve_out(self, dve, out, scale, shift=None):
        dve.wait_ge(self.turned, KD)
        src = self.k.ps[:, 0:4, :].rearrange("p b (f t) -> p (b f) t", f=2)
        for f in range(KD):
            dve.tensor_scalar(out[:, f, :], src[:, f, :], scale[:, f:f + 1],
                              None if shift is None else shift[:, f:f + 1], ALU.mult,
                              *(() if shift is None else (ALU.add,))).then_inc(self.done, 1)


def rsqrt_mean(k, pool, out, ss, width, eps=EPS):
    pool.tensor_scalar(out, ss, 1.0 / width, eps, ALU.mult, ALU.add)
    pool.drain()
    n = out.shape[-1]
    return pool.tensor_tensor(out=out, in0=out, in1=k.c("minus_half")[:, 0:n], op=ALU.pow)


def turn(k, pe, src, nf, dst, turned):
    for f in range(nf):
        for t in range(TT):
            last = pe.transpose(dst[:, f, t * P:(t + 1) * P], src[:, t, f * P:(f + 1) * P], k.c("ident"))
        last.then_inc(turned, 1)


def range_reduce(dve, r, n, ang):
    dve.tensor_scalar(n, ang, 1.0 / TWO_PI, ROUND, ALU.mult, ALU.add)
    dve.drain()
    dve.tensor_scalar(n, n, -ROUND, None, ALU.add)
    dve.drain()
    dve.scalar_tensor_tensor(out=r, in0=n, scalar=-TWO_PI_A, in1=ang, op0=ALU.mult, op1=ALU.add)
    dve.drain()
    dve.scalar_tensor_tensor(out=r, in0=n, scalar=-TWO_PI_B, in1=r, op0=ALU.mult, op1=ALU.add)
    dve.drain()
    dve.scalar_tensor_tensor(out=r, in0=n, scalar=-TWO_PI_C, in1=r, op0=ALU.mult, op1=ALU.add)
    dve.drain()
    return dve.tensor_scalar(r, r, PI, -PI, ALU.min, ALU.max)


def quarter_turn(dve, r, n, angle):
    dve.tensor_scalar(n, angle, PI / 2, -TWO_PI, ALU.is_gt, ALU.mult)
    dve.tensor_scalar(r, angle, float(np.pi / 2), None, ALU.add)
    dve.drain()
    dve.tensor_tensor(r, r, n, ALU.add)
    dve.drain()
    return dve.tensor_scalar(r, r, PI, -PI, ALU.min, ALU.max)


def stage_modulation(k, rows):
    nc, d = k.nc, k.dram
    with ExitStack() as ctx:
        csil = k.sb("csil", [P, KD], ctx=ctx)
        cexp = k.sb("cexp", [P, KD], ctx=ctx)
        crep = k.sb("crep", [P, KD, P], ctx=ctx)
        pos = k.sb("pos", [P, TT], I32, ctx=ctx)
        posf = k.sb("posf", [P, TT], ctx=ctx)
        ang = k.sb("ang", [P, TT, 32], ctx=ctx)
        red = k.sb("red", [P, TT, 32], ctx=ctx)
        redc = k.sb("redc", [P, TT, 32], ctx=ctx)
        turns = k.sb("turns", [P, TT, 32], ctx=ctx)
        mem = k.sb("mem", [P, TT, D], ctx=ctx)
        xn = k.sb("xn0", [P, TT, D], ctx=ctx)
        memn = k.sb("memn", [P, TT, D], ctx=ctx)
        norm_m = NormT(k, "mem_norm", mem, ctx, memn)
        norm_x = NormT(k, "norm1", k.x, ctx, xn)
        small_in, rows_in, x_in, mem_in, pos_in = (k.sem(s) for s in ("small_in", "rows_in", "x_in", "mem_in", "pos_in"))
        cexp_ready, csil_ready, row_out, angles_ready, tables_ready, cols_done = (
            k.sem(s) for s in ("cexp_ready", "csil_ready", "gate_rows_out", "angles_ready", "tables_ready", "cols_done"))
        mod_row = k.sb("mod_row", [1, 4, 512], ctx=ctx)
        row_copied = k.sem("mod_row_copied")
        mod_ps, row_ps = k.ps[:, 6, :], k.ps[:, 4:6, :]
        NBUF = 4

        with nc.Block() as block:
            @block.sync
            def _(sp):
                sp.dma_start(k.cols[:], d["cols"]).then_inc(small_in, 16)
                sp.dma_start(k.const[:], d["consts"]).then_inc(small_in, 16)
                for n in range(RING):
                    sp.dma_start(k.ring[:, n, :], d["weights"][n]).then_inc(k.landed[n], 16)
                sp.dma_start(pos[:], d["positions"]).then_inc(pos_in, 16)
                sp.dma_start(*rows).then_inc(rows_in, 16)
                stream(k, sp, T_ADA, T_ADA + N_ADA)

            @block.scalar
            def _(act):
                act.wait_ge(small_in, 32)
                act.activation(cexp[:], k.col("c", 0, KD), ACT.Exp, scale=-1.0).then_inc(cexp_ready, 1)
                act.sem_inc(row_copied, NBUF)

                def copy_rows(tiles):
                    for n in tiles:
                        half, j = n // NBUF, n % NBUF
                        act.wait_ge(k.tile_done, 6 * half + j + 1)
                        act.copy(mod_row[:, j, :], k.ps[0:1, j, :]).then_inc(row_copied, 1)

                copy_rows((0,))
                act.dma_start(mem[:], d["mem"]).then_inc(mem_in, 16)
                act.dma_start(k.x[:], d["x"]).then_inc(x_in, 16)
                copy_rows((1, 2, 3))
                act.wait_ge(mem_in, 16)
                norm_m.act(act)
                act.wait_ge(x_in, 16)
                norm_x.act(act)
                copy_rows((4, 5, 6, 7))
                act.wait_ge(angles_ready, 2)
                act.activation(k.sin[:], red[:], ACT.Sin).then_inc(tables_ready, 1)
                act.activation(k.cos[:], redc[:], ACT.Sin).then_inc(tables_ready, 1)

            @block.gpsimd
            def _(pool):
                norm_m.pool(pool)
                norm_x.pool(pool)

            @block.vector
            def _(dve):
                dve.wait_ge(cexp_ready, 1)
                dve.tensor_scalar(cexp[:], cexp[:], 1.0, None, ALU.add)
                dve.drain()
                dve.reciprocal(cexp[:], cexp[:])
                dve.drain()
                dve.tensor_tensor(csil[:], cexp[:], k.col("c", 0, KD), ALU.mult)
                dve.drain()
                dve.tensor_copy(crep[:], bc(csil[:], 2, P)).then_inc(csil_ready, 1)
                dve.sem_inc(row_out, 1)
                dve.wait_ge(pos_in, 16)
                dve.tensor_copy(posf[:], pos[:])
                dve.drain()
                for t in range(TT):
                    dve.tensor_scalar(ang[:, t, :], k.c("inv_freq"), posf[:, t:t + 1], None, ALU.mult)
                dve.drain()
                range_reduce(dve, red[:], turns[:], ang[:]).then_inc(angles_ready, 1)
                dve.drain()
                quarter_turn(dve, redc[:], turns[:], red[:]).then_inc(angles_ready, 1)
                norm_m.dve_scale(dve)
                norm_x.dve_scale(dve)
                dve.wait_ge(rows_in, 16)
                for half, gate in enumerate(("b_g1", "b_g2")):
                    for j in range(2):
                        dve.wait_ge(k.tile_done, 6 * half + 5 + j)
                        g = k.row(gate)[:, j * 512:(j + 1) * 512]
                        last = dve.tensor_tensor(g, row_ps[:, j, :], g, ALU.add)
                    last.then_inc(row_out, 1)
                dve.wait_ge(cols_done, 2)
                dve.tensor_tensor(k.mod[:], mod_ps[:, 0:32], k.col("b_ada", 0, 32), ALU.add)
                dve.drain()
                for i, g in ((8, "norm1_g"), (24, "norm2_g")):
                    dve.scalar_tensor_tensor(out=k.mod[:, i:i + 8], in0=k.mod[:, i:i + 8], scalar=1.0,
                                             in1=k.col(g, 0, 8), op0=ALU.add, op1=ALU.mult)
                dve.drain()
                norm_m.dve_out(dve, k.memT, k.col("mem_norm_w", 0, KD))
                norm_x.dve_out(dve, k.hT, k.mod[:, 8:16], k.mod[:, 0:8])

            @block.tensor
            def _(pe):
                pe.wait_ge(csil_ready, 1)
                with pe.Fori(0, 2) as half:
                    for j in range(6):
                        slot = j % RING
                        pe.wait_ge(k.landed[slot], half * 32 + 16 * (j // RING + 1))
                        w = k.ring[:, slot, :].rearrange("p (k n) -> p k n", k=KD)
                        if j == 4:
                            pe.wait_ge(row_out, half + 1)
                        if j < NBUF:
                            pe.wait_ge(row_copied, half * NBUF + (j + 1))
                        out = k.ps[:, j, :] if j < NBUF else row_ps[:, j - NBUF, :]
                        for kk in range(KD):
                            last = pe.matmul(out, crep[:, kk, :], w[:, kk, :], start=(kk == 0), stop=(kk == KD - 1))
                        last.then_inc(k.tile_done, 1)
                        if 1 <= j <= NBUF:
                            pe.wait_ge(row_copied, half * NBUF + (j + NBUF))
                            for f in range(4):
                                last = pe.matmul(mod_ps[:, bass.ds(half * 16 + (4 * (j - 1) + f), 1)],
                                                 mod_row[:, j - 1, f * P:(f + 1) * P], k.c("ones")[0:1, 0:1],
                                                 start=True, stop=True)
                            if j == NBUF:
                                last.then_inc(cols_done, 1)
                norm_m.pe(pe)
                pe.wait_ge(norm_m.done, KD)
                norm_x.pe(pe)


def stage_in_projection(k, a):
    nc = k.nc
    evac = k.sem("in_proj_out")
    gates_done = k.sem("gates_done")
    wg_in = k.sem("w_gate_in")
    with nc.Block() as block:
        @block.sync
        def _(sp):
            sp.dma_start(a["w_gate"][:], k.dram["w_gate"]).then_inc(wg_in, 16)
            stream(k, sp, T_IN, T_IN + N_IN)

        @block.tensor
        def _(pe):
            for m in range(N_IN):
                if m >= 3:
                    pe.wait_ge(evac, m - 2)
                if m in (3, 4):
                    fm_tile(k, pe, T_IN + m, k.hT, pair_fm(k, m))
                else:
                    tm_tile(k, pe, T_IN + m, k.hT, pair(k, m))
            pe.wait_ge(wg_in, 16)
            for g in range(2):
                for kk in range(KD):
                    last = pe.matmul(k.ps[0:4, 6 + g, 0:TOK], a["w_gate"][:, kk, 4 * g:4 * g + 4], k.hT[:, kk, :],
                                     start=(kk == 0), stop=(kk == KD - 1))
            last.then_inc(gates_done, 1)

        @block.vector
        def _(dve):
            dve.memset(a["v_aug"][:], 1.0)
            dve.memset(a["qk_mT"][:, :, 0:3], 0.0)
            dve.drain()
            for m in range(N_IN):
                dve.wait_ge(k.tile_done, T_IN + m + 1)
                if m < 3:
                    ins = dve.tensor_copy(a["qkv"][:, :, m * 512:(m + 1) * 512], pair(k, m))
                elif m < 5:
                    ins = dve.tensor_copy(a["qk_mT"][:, 4 * (m - 3):4 * (m - 3) + 4, 3:3 + TOK], pair_fm(k, m))
                elif m == 5:
                    for t in range(TT):
                        ins = dve.tensor_copy(a["v_aug"][:, t, :, 0:128],
                                              pair(k, m)[:, t, :].rearrange("p (h e) -> p h e", h=4))
                else:
                    ins = dve.tensor_copy(a["o_m"][:], pair(k, m))
                ins.then_inc(evac, 1)
            dve.wait_ge(gates_done, 1)
            for g in range(2):
                dve.tensor_scalar(a["gate_rows"][0:4, g, :], k.ps[0:4, 6 + g, 0:TOK], k.col("b_gate", g)[0:4], None, ALU.add)


def stage_attention(k, a):
    nc = k.nc
    with ExitStack() as ctx:
        rot = k.sb("rot", [P, TT, D], ctx=ctx)
        swp = k.sb("swp", [P, 16, 2, 32], ctx=ctx)
        qkT = k.sb("qkT", [P, KD, TOK], ctx=ctx)
        scores = k.sb("scores", [P, 2, 2, TT, TOK], ctx=ctx)
        pT = k.sb("pT", [P, 2, 2, TT, TOK], ctx=ctx)
        mx = k.sb("mx", [P, 4, 4], ctx=ctx)
        rs = k.sb("rs", [P, 4, 4], ctx=ctx)
        rotated, turned, qkT_ready, scored, masked, expd, p_turned, pT_ready, pv_done = (
            k.sem(s) for s in ("qk_rotated", "qk_turned", "qkT_ready", "scored", "masked", "exp_done", "p_turned",
                               "pT_ready", "pv_done"))
        spair = [k.ps[:, 0:2, :], k.ps[:, 2:4, :]]
        tps = k.ps[:, 4:6, :].rearrange("p h (kt q) -> p h kt q", kt=2)
        ops = k.ps[:, 6:8, :].rearrange("p b (g t e) -> p (b g) t e", t=TT, e=64)
        with nc.Block() as block:
            @block.vector
            def _(dve):
                for t in range(TT):
                    src = a["qkv"][:, t, 0:1024].rearrange("p (h g e) -> p h g e", g=2, e=32)
                    dst = rot[:, t, :].rearrange("p (h g e) -> p h g e", g=2, e=32)
                    cos, sin = k.cos[:, t, :], k.sin[:, t, :]
                    for g in range(2):
                        dve.tensor_tensor(dst[:, :, g, :], src[:, :, g, :], bc(cos, 1, 16), ALU.mult)
                        dve.tensor_tensor(swp[:, :, g, :], src[:, :, 1 - g, :], bc(sin, 1, 16), ALU.mult)
                    dve.drain()
                    dve.tensor_tensor(dst[:, :, 0, :], dst[:, :, 0, :], swp[:, :, 0, :], ALU.subtract)
                    dve.tensor_tensor(dst[:, :, 1, :], dst[:, :, 1, :], swp[:, :, 1, :], ALU.add).then_inc(rotated, 1)
                    dve.drain()
                dve.wait_ge(turned, KD)
                dve.tensor_copy(qkT[:, :, :], k.ps[:, 0:4, :].rearrange("p b (f t) -> p (b f) t", f=2)).then_inc(qkT_ready, 1)

                def mask(hp):
                    dve.wait_ge(scored, hp + 1)
                    for h in range(2):
                        dve.scalar_tensor_tensor(out=scores[:, hp % 2, h], scalar=0.125, op0=ALU.mult, op1=ALU.add,
                                                 in0=spair[hp % 2][:, h, :].rearrange("p (t q) -> p t q", t=TT),
                                                 in1=k.c("causal").rearrange("p (t q) -> p t q", t=TT))
                    dve.drain()
                    dve.tensor_reduce(mx[:, hp, :], scores[:, hp % 2].rearrange("p h t q -> p (h t) q"), AX, ALU.max)
                    dve.drain()
                    dve.tensor_scalar(mx[:, hp, :], mx[:, hp, :], -1.0, None, ALU.mult).then_inc(masked, 1)

                for hp in range(4):
                    if hp == 0:
                        mask(0)
                    dve.wait_ge(p_turned, hp + 1)
                    if hp >= 2:
                        dve.wait_ge(pv_done, hp - 1)
                    dve.tensor_copy(pT[:, hp % 2], tps[:]).then_inc(pT_ready, 1)
                    if hp < 3:
                        mask(hp + 1)
                dve.reciprocal(rs[:], rs[:])
                dve.drain()
                dve.wait_ge(pv_done, 4)
                dst = a["mix"][:, :, 0:512].rearrange("p t (h e) -> p h t e", e=64)
                r = rs[:].rearrange("p a (h t) -> p (a h) t", h=2)
                for t in range(TT):
                    dve.tensor_tensor(dst[:, :, t, :], ops[:, :, t, :], bc(r[:, :, t], 2, 64), ALU.mult)

            @block.scalar
            def _(act):
                for hp in range(4):
                    act.wait_ge(masked, hp + 1)
                    if hp >= 2:
                        act.wait_ge(p_turned, hp - 1)
                    for h in range(2):
                        for t in range(TT):
                            i = 2 * h + t
                            last = act.activation(scores[:, hp % 2, h, t, :], scores[:, hp % 2, h, t, :], ACT.Exp,
                                                  bias=mx[:, hp, i:i + 1], accum_out=rs[:, hp, i:i + 1])
                    last.then_inc(expd, 1)

            @block.tensor
            def _(pe):
                pe.wait_ge(rotated, TT)
                turn(k, pe, rot, KD, k.ps[:, 0:4, :].rearrange("p b (f t) -> p (b f) t", f=2), turned)
                pe.wait_ge(qkT_ready, 1)

                def score(hp):
                    if hp >= 2:
                        pe.wait_ge(masked, hp - 1)
                    for h in range(2):
                        r = slice(64 * h, 64 * h + 64)
                        for t in range(TT):
                            last = pe.matmul(spair[hp % 2][:, h, t * TOK:(t + 1) * TOK], qkT[r, hp, t * P:(t + 1) * P],
                                             qkT[r, 4 + hp, :], start=True, stop=True)
                    last.then_inc(scored, 1)

                score(0)
                for hp in range(4):
                    if hp < 3:
                        score(hp + 1)
                    pe.wait_ge(expd, hp + 1)
                    if hp >= 1:
                        pe.wait_ge(pT_ready, hp)
                    for h in range(2):
                        for kt in range(2):
                            for t in range(TT):
                                last = pe.transpose(tps[:, h, kt, t * P:(t + 1) * P],
                                                    scores[:, hp % 2, h, t, kt * P:(kt + 1) * P], k.c("ident"))
                    last.then_inc(p_turned, 1)
                    pe.wait_ge(pT_ready, hp + 1)
                    for h in range(2):
                        v = slice(1024 + (2 * hp + h) * 64, 1024 + (2 * hp + h) * 64 + 64)
                        for t in range(TT):
                            for kt in range(t + 1):
                                last = pe.matmul(ops[:, 2 * hp + h, t, :], pT[:, hp % 2, h, kt, t * P:(t + 1) * P],
                                                 a["qkv"][:, kt, v], start=(kt == 0), stop=(kt == t))
                    last.then_inc(pv_done, 1)


def stage_conv(k, a):
    nc = k.nc
    with ExitStack() as ctx:
        acc = k.sb("conv_acc", [P, KD, TOK], ctx=ctx)
        t4 = k.sb("gate_tmp", [4, 8, TOK], ctx=ctx)
        q4 = k.sb("gate_quads", [P, TOK], ctx=ctx)
        sc = k.sb("gate_small", [4, 8], ctx=ctx)
        conv_done, f_ready, f_exp, m_ready, e_ready, quads_ready, cols_ready, arow = (
            k.sem(s) for s in ("conv_done", "f_ready", "f_exp", "m_ready", "m_exp", "quads_ready",
                               "gate_cols_ready", "a_rows_ready"))
        logf, cum, b, pm, mt, tmp, one = (t4[:, i, :] for i in range(7))
        ig = a["gate_rows"][0:4, 0, :]
        fg = a["gate_rows"][0:4, 1, :]
        with nc.Block() as block:
            @block.gpsimd
            def _(pool):
                pool.memset(q4[:], 0.0).then_inc(arow, 1)

            @block.scalar
            def _(act):
                act.wait_ge(f_ready, 1)
                act.activation(tmp, tmp, ACT.Exp, scale=-1.0)
                act.drain()
                act.activation(tmp, tmp, ACT.Ln, bias=1.0).then_inc(f_exp, 1)
                act.wait_ge(m_ready, 1)
                act.wait_ge(arow, 1)
                act.activation(q4[32:36, :], one, ACT.Exp)
                act.activation(q4[64:68, :], mt, ACT.Exp, scale=-1.0)
                act.activation(q4[96:100, 0:P], b[:, 0:P], ACT.Exp, bias=sc[:, 2:3]).then_inc(e_ready, 1)
                act.wait_ge(conv_done, 1)
                act.activation(a["qk_mT"][:, :, 3:3 + TOK], acc[:], ACT.Silu)

            @block.vector
            def _(dve):
                dve.scalar_tensor_tensor(out=tmp, in0=fg, scalar=-1.0, in1=fg, op0=ALU.mult, op1=ALU.max).then_inc(f_ready, 1)
                dve.wait_ge(f_exp, 1)
                dve.tensor_scalar(logf, fg, 0.0, None, ALU.min)
                dve.memset(one, 1.0)
                dve.drain()
                dve.tensor_tensor(logf, logf, tmp, ALU.subtract)
                dve.drain()
                for c in range(2):
                    s = slice(c * P, (c + 1) * P)
                    dve.tensor_tensor_scan(cum[:, s], one[:, s], logf[:, s], 0.0, ALU.mult, ALU.add)
                dve.drain()
                dve.tensor_tensor(b, ig, cum, ALU.subtract)
                dve.drain()
                for c in range(2):
                    s = slice(c * P, (c + 1) * P)
                    dve.tensor_tensor_scan(pm[:, s], one[:, s], b[:, s], -3e38, ALU.mult, ALU.max)
                dve.drain()
                total = cum[:, P - 1:P]
                dve.tensor_tensor(sc[:, 1:2], total, pm[:, P - 1:P], ALU.add)
                dve.drain()
                dve.tensor_tensor(sc[:, 0:1], sc[:, 1:2], total, ALU.max)
                dve.drain()
                dve.tensor_tensor(sc[:, 2:3], total, sc[:, 0:1], ALU.subtract)
                dve.tensor_copy(tmp[:, 0:P], cum[:, 0:P])
                dve.tensor_scalar(tmp[:, P:], cum[:, P:], sc[:, 0:1], None, ALU.add)
                dve.tensor_tensor(mt, cum, pm, ALU.add)
                dve.drain()
                dve.tensor_tensor(mt, mt, tmp, ALU.max)
                dve.drain()
                dve.tensor_tensor(one, tmp, mt, ALU.subtract)
                dve.tensor_tensor(a["a_rows"][:], cum, mt, ALU.subtract)
                dve.drain()
                dve.wait_ge(arow, 1)
                dve.tensor_copy(q4[0:4, :], b).then_inc(m_ready, 1)
                for i in range(4):
                    for f in range(KD):
                        w, src = k.col("conv_w", 4 * f + i), a["qk_mT"][:, f, i:i + TOK]
                        if i == 0:
                            dve.tensor_scalar(acc[:, f, :], src, w, k.col("conv_b", f), ALU.mult, ALU.add)
                        else:
                            last = dve.scalar_tensor_tensor(out=acc[:, f, :], in0=src, scalar=w, in1=acc[:, f, :],
                                                            op0=ALU.mult, op1=ALU.add)
                    if i < 3:
                        dve.drain()
                last.then_inc(conv_done, 1)
                dve.wait_ge(quads_ready, 1)
                for t in range(TT):
                    dve.tensor_copy(a["gcol"][:, t, :], k.ps[:, t, 0:P])
                dve.drain()
                dve.tensor_scalar(a["gcol"][:, 0, 96:100], a["gcol"][:, 0, 96:100], 128 ** -0.5, None, ALU.mult)

            @block.tensor
            def _(pe):
                pe.wait_ge(m_ready, 1)
                pe.wait_ge(e_ready, 1)
                for t in range(TT):
                    last = pe.transpose(k.ps[:, t, 0:P], q4[:, t * P:(t + 1) * P], k.c("ident"))
                last.then_inc(quads_ready, 1)


def stage_mlstm(k, a):
    nc = k.nc
    with ExitStack() as ctx:
        dm = k.sb("dmat", [P, 4, TOK], ctx=ctx)
        st = k.sb("s_t", [P, 4, TOK], ctx=ctx)
        kw = k.sb("k_weighted", [P, 4, P], ctx=ctx)
        cst = k.sb("c_state", [P, 4, 129], ctx=ctx)
        num = k.sb("num", [P, TT, 4, 129], ctx=ctx)
        den = k.sb("den", [P, TT, 4, 1], ctx=ctx)
        a_bc, masked, d_exp, s_raw, s_ready, kt, kw_ready, c_done, c_out, num0, num1, inter = (
            k.sem(s) for s in ("a_bc", "d_masked", "d_exp", "s_raw", "s_ready", "k_turned", "kw_ready", "c_done", "c_out",
                               "num0_done", "num1_done", "inter_done"))
        abc = k.ps[:, 0:2, :].rearrange("p b (h t) -> p (b h) t", h=2)
        sps = k.ps[:, 2:4, :].rearrange("p b (h t) -> p (b h) t", h=2)
        qT = lambda h, t: a["qk_mT"][:, h, 3 + t * P:3 + (t + 1) * P]
        kT = lambda h, t: a["qk_mT"][:, 4 + h, 3 + t * P:3 + (t + 1) * P]
        b_col = lambda h, t: a["gcol"][:, t, h:h + 1]
        acc = lambda i, h: k.ps[:, i + h // 2, 256 * (h % 2):256 * (h % 2) + 129]
        with nc.Block() as block:
            @block.tensor
            def _(pe):
                for h in range(4):
                    last = pe.matmul(abc[:, h, :], k.c("one_hot4")[0:4, h * P:(h + 1) * P], a["a_rows"][:],
                                     start=True, stop=True)
                last.then_inc(a_bc, 1)
                for h in range(4):
                    for t in range(TT):
                        last = pe.matmul(sps[:, h, t * P:(t + 1) * P], kT(h, t), qT(h, t), start=True, stop=True)
                last.then_inc(s_raw, 1)
                for h in range(4):
                    last = pe.transpose(k.ps[:, 4, h * P:(h + 1) * P], kT(h, 0), k.c("ident"))
                last.then_inc(kt, 1)
                pe.wait_ge(kw_ready, 1)
                for h in range(4):
                    last = pe.matmul(acc(5, h), kw[:, h, :], a["v_aug"][:, 0, h, :], start=True, stop=True)
                last.then_inc(c_done, 1)
                pe.wait_ge(s_ready, 1)
                for t in range(TT):
                    for h in range(4):
                        last = pe.matmul(acc(2 * t, h), st[:, h, t * P:(t + 1) * P], a["v_aug"][:, t, h, :],
                                         start=True, stop=True)
                last.then_inc(num0, 1)
                pe.wait_ge(c_out, 1)
                for h in range(4):
                    last = pe.matmul(acc(5, h), qT(h, 1), cst[:, h, :], start=True, stop=True)
                last.then_inc(inter, 1)

            @block.scalar
            def _(act):
                act.wait_ge(masked, 1)
                for h in range(4):
                    for t in range(TT):
                        s = slice(t * P, (t + 1) * P)
                        last = act.activation(dm[:, h, s], dm[:, h, s], ACT.Exp, bias=b_col(h, t))
                last.then_inc(d_exp, 1)

            @block.vector
            def _(dve):
                dve.wait_ge(a_bc, 1)
                for t in range(TT):
                    s = slice(t * P, (t + 1) * P)
                    last = dve.tensor_tensor(dm[:, :, s], abc[:, :, s], bc(k.c("causal_t"), 1, 4), ALU.add)
                last.then_inc(masked, 1)
                dve.wait_ge(kt, 1)
                dve.tensor_tensor(kw[:], k.ps[:, 4, :].rearrange("p (h d) -> p h d", h=4),
                                  bc(a["gcol"][:, 0, 96:100], 2, P), ALU.mult).then_inc(kw_ready, 1)
                dve.wait_ge(d_exp, 1)
                dve.wait_ge(s_raw, 1)
                dve.scalar_tensor_tensor(out=st[:], in0=sps[:], scalar=128 ** -0.5, in1=dm[:], op0=ALU.mult,
                                         op1=ALU.mult).then_inc(s_ready, 1)
                dve.wait_ge(c_done, 1)
                for h in range(4):
                    last = dve.tensor_copy(cst[:, h, :], acc(5, h))
                last.then_inc(c_out, 1)
                dve.wait_ge(num0, 1)
                for t in range(TT):
                    for h in range(4):
                        dve.tensor_copy(num[:, t, h, :], acc(2 * t, h))
                dve.drain()
                dve.wait_ge(inter, 1)
                for h in range(4):
                    dve.scalar_tensor_tensor(out=num[:, 1, h, :], in0=acc(5, h), scalar=a["gcol"][:, 1, 32 + h:33 + h],
                                             in1=num[:, 1, h, :], op0=ALU.mult, op1=ALU.add)
                dve.drain()
                dve.scalar_tensor_tensor(out=den[:, :, :, 0], in0=num[:, :, :, 128], scalar=-1.0, in1=num[:, :, :, 128],
                                         op0=ALU.mult, op1=ALU.max)
                dve.drain()
                for t in range(TT):
                    dve.tensor_tensor(den[:, t, :, 0], den[:, t, :, 0], a["gcol"][:, t, 64:68], ALU.max)
                dve.drain()
                dve.reciprocal(den[:], den[:])
                dve.drain()
                for t in range(TT):
                    dve.tensor_tensor(a["mix"][:, t, 512:1024].rearrange("p (h e) -> p h e", h=4), num[:, t, :, 0:128],
                                      den[:, t, :, :].broadcast_to([P, 4, 128]), ALU.mult)


def stage_out_projection(k, a):
    nc = k.nc
    with ExitStack() as ctx:
        sq = k.sb("mix_sq", [P, TT, D], ctx=ctx)
        ss = k.sb("head_ss", [P, TT, 12], ctx=ctx)
        rstd = k.sb("head_rstd", [P, TT, 12], ctx=ctx)
        sig = k.sb("sig", [P, TT, 512], ctx=ctx)
        mixT = k.sb("mixT", [P, KD, TOK], ctx=ctx)
        xn = k.sb("xn1", [P, TT, D], ctx=ctx)
        w_router = k.sb("w_router", [P, KD, 36], ctx=ctx)
        norm = NormT(k, "norm2", k.x, ctx, xn)
        squares, rstd_ready, sig_ready, mix_ready, mix_turned, mixT_ready, x_ready, logits, router_in = (
            k.sem(s) for s in ("mix_squares", "head_rstd_ready", "out_gate_ready", "mix_ready", "mix_turned", "mixT_ready",
                               "x_ready", "logits_done", "router_in"))
        tps = k.ps[:, 0:4, :].rearrange("p b (f t) -> p (b f) t", f=2)
        groups = ((0, 512, 64, 0, 8, "attn_out_g"), (512, 1024, 128, 8, 12, "mlstm_out_g"))
        with nc.Block() as block:
            @block.sync
            def _(sp):
                sp.dma_start(w_router[:], k.dram["w_router"]).then_inc(router_in, 16)
                for j in range(RING):
                    sp.wait_ge(k.tile_done, T_GLA - RING + j + 1)
                    for h in range(2):
                        at = slice(h * TILE // 2, (h + 1) * TILE // 2)
                        sp.dma_start(k.ring[:, j, at], k.dram["experts"][j][:, at]).then_inc(a["expert_landed"][j][h], 16)

            @block.scalar
            def _(act):
                act.activation(sig[:], a["o_m"][:], ACT.Sigmoid).then_inc(sig_ready, 1)
                act.wait_ge(x_ready, 1)
                norm.act(act)

            @block.gpsimd
            def _(pool):
                pool.wait_ge(squares, 1)
                pool.tensor_scalar(rstd[:, :, 0:8], ss[:, :, 0:8], 1.0 / 64, EPS, ALU.mult, ALU.add)
                pool.tensor_scalar(rstd[:, :, 8:12], ss[:, :, 8:12], 1.0 / 128, EPS, ALU.mult, ALU.add)
                pool.drain()
                for t in range(TT):
                    last = pool.tensor_tensor(out=rstd[:, t, :], in0=rstd[:, t, :], in1=k.c("minus_half")[:, 0:12],
                                              op=ALU.pow)
                last.then_inc(rstd_ready, 1)
                norm.pool(pool)

            @block.vector
            def _(dve):
                dve.tensor_tensor(sq[:], a["mix"][:], a["mix"][:], ALU.mult)
                dve.drain()
                for c0, c1, w, s0, s1, _g in groups:
                    for t in range(TT):
                        last = dve.tensor_reduce(ss[:, t, s0:s1], sq[:, t, c0:c1].rearrange("p (h e) -> p h e", e=w),
                                                 AX, ALU.add)
                last.then_inc(squares, 1)
                dve.wait_ge(sig_ready, 1)
                dve.tensor_tensor(sig[:], sig[:], bc(k.row("mlstm_out_g"), 1, TT), ALU.mult)
                dve.wait_ge(rstd_ready, 1)
                for c0, c1, w, s0, s1, _g in groups:
                    for t in range(TT):
                        v = a["mix"][:, t, c0:c1].rearrange("p (h e) -> p h e", e=w)
                        dve.tensor_tensor(v, v, bc(rstd[:, t, s0:s1], 2, w), ALU.mult)
                dve.drain()
                dve.tensor_tensor(a["mix"][:, :, 0:512], a["mix"][:, :, 0:512], bc(k.row("attn_out_g"), 1, TT), ALU.mult)
                dve.tensor_tensor(a["mix"][:, :, 512:1024], a["mix"][:, :, 512:1024], sig[:], ALU.mult).then_inc(mix_ready, 1)
                dve.wait_ge(mix_turned, KD)
                dve.tensor_copy(mixT[:], tps[:]).then_inc(mixT_ready, 1)
                for n in range(N_OUT):
                    dve.wait_ge(k.tile_done, T_OUT + n + 1)
                    s = slice(n * 512, (n + 1) * 512)
                    dve.tensor_tensor(sq[:, :, s], k.ps[:, 4 + 2 * n:6 + 2 * n, :], bc(k.row("b_g1")[:, s], 1, TT), ALU.mult)
                dve.drain()
                dve.tensor_tensor(k.x[:], k.x[:], sq[:], ALU.add).then_inc(x_ready, 1)
                norm.dve_scale(dve)
                norm.dve_out(dve, k.hT, k.mod[:, 24:32], k.mod[:, 16:24])
                dve.wait_ge(logits, 1)
                dve.tensor_tensor(a["logits"][:], k.ps[:, 4:6, 0:36], bc(k.row("b_router"), 1, TT), ALU.add)

            @block.tensor
            def _(pe):
                pe.wait_ge(mix_ready, 1)
                turn(k, pe, a["mix"], KD, tps, mix_turned)
                pe.wait_ge(mixT_ready, 1)
                for n in range(N_OUT):
                    tm_tile(k, pe, T_OUT + n, mixT, k.ps[:, 4 + 2 * n:6 + 2 * n, :])
                norm.pe(pe)
                pe.wait_ge(norm.done, KD)
                pe.wait_ge(router_in, 16)
                for t in range(TT):
                    for kk in range(KD):
                        last = pe.matmul(k.ps[:, 4 + t, 0:36], k.hT[:, kk, t * P:(t + 1) * P], w_router[:, kk, :],
                                         start=(kk == 0), stop=(kk == KD - 1))
                last.then_inc(logits, 1)


def stage_route(k, a):
    with ExitStack() as ctx:
        sb = lambda name, s, dt=F32: k.sb(name, s, dt, ctx=ctx)
        g8, gm, gi, gf = sb("g8", [P, TT, 8]), sb("g_top", [P, TT, 8]), sb("g_idx", [P, TT, 8], U32), sb("g_idx_f", [P, TT, 8])
        ge, gs, gmask = sb("g_exp", [P, TT, 4]), sb("g_sum", [P, TT]), sb("g_mask", [P, TT, 4])
        em, et = sb("e_masked", [P, TT, 32]), sb("e_top", [P, TT, 8])
        ei, ef = sb("e_idx", [P, TT, 8], U32), sb("e_idx_f", [P, TT, 8])
        dl, w1, w2 = sb("e_gap", [P, TT]), sb("w_first", [P, TT]), sb("w_second", [P, TT])
        is1, is2, chosen = sb("is_first", [P, TT, 32]), sb("is_second", [P, TT, 32]), sb("chosen", [P, TT, 32])
        over, most = sb("over", [P, 3]), sb("most", [P, 1])
        rest = sb("h2_rest", [P, TT, D])
        h_tm = k.ps[:, 0:4, :].rearrange("p (t b) c -> p t (b c)", t=TT)
        gap_ready, exp_done, chosen_ready, ranked, h_turned, part_ready, rest_ready = (
            k.sem(s) for s in ("gap_ready", "route_exp_done", "chosen_ready", "ranked", "h_turned_back",
                               "h2_part_ready", "h2_rest_ready"))
        with k.nc.Block() as block:
            @block.tensor
            def _(pe):
                for t in range(TT):
                    for f in range(KD):
                        last = pe.transpose(k.ps[:, 2 * t + f // 4, (f % 4) * P:(f % 4 + 1) * P],
                                            k.hT[:, f, t * P:(t + 1) * P], k.c("ident"))
                last.then_inc(h_turned, 1)
                pe.wait_ge(chosen_ready, 1)
                pe.matmul(k.ps[:, 4, 0:32], k.c("before"), chosen[:, 0, :], start=True, stop=True)
                pe.matmul(k.ps[:, 4, 32:64], k.c("before"), chosen[:, 1, :], start=True, stop=False)
                pe.matmul(k.ps[:, 4, 32:64], k.c("ones"), chosen[:, 0, :], start=False, stop=True)
                pe.matmul(k.ps[:, 5, 0:32], k.c("ones"), chosen[:, 0, :], start=True, stop=False)
                pe.matmul(k.ps[:, 5, 0:32], k.c("ones"), chosen[:, 1, :], start=False, stop=True).then_inc(ranked, 1)

            @block.vector
            def _(dve):
                dve.memset(g8[:], -3e38)
                dve.drain()
                dve.tensor_copy(g8[:, :, 0:4], a["logits"][:, :, 0:4])
                dve.drain()
                for t in range(TT):
                    dve.max(gm[:, t, :], g8[:, t, :])
                dve.drain()
                for t in range(TT):
                    dve.max_index(gi[:, t, :], gm[:, t, :], g8[:, t, :])
                    dve.tensor_scalar(ge[:, t, :], a["logits"][:, t, 0:4], gm[:, t, 0:1], None, ALU.subtract)
                dve.drain()
                dve.tensor_copy(gf[:], gi[:])
                dve.drain()
                for t in range(TT):
                    dve.tensor_scalar(gmask[:, t, :], k.c("iota64")[:, 0:4], gf[:, t, 0:1], None, ALU.is_equal)
                dve.drain()
                for t in range(TT):
                    dve.tensor_tensor(em[:, t, :].rearrange("p (g e) -> p g e", g=4),
                                      a["logits"][:, t, 4:36].rearrange("p (g e) -> p g e", g=4),
                                      bc(gmask[:, t, :], 2, 8), ALU.mult)
                dve.drain()
                dve.tensor_scalar(gmask[:], gmask[:], -NEG, NEG, ALU.mult, ALU.add)
                dve.drain()
                for t in range(TT):
                    v = em[:, t, :].rearrange("p (g e) -> p g e", g=4)
                    dve.tensor_tensor(v, v, bc(gmask[:, t, :], 2, 8), ALU.add)
                dve.drain()
                for t in range(TT):
                    dve.max(et[:, t, :], em[:, t, :])
                dve.drain()
                for t in range(TT):
                    dve.max_index(ei[:, t, :], et[:, t, :], em[:, t, :])
                dve.tensor_tensor(dl[:], et[:, :, 1], et[:, :, 0], ALU.subtract).then_inc(gap_ready, 1)
                dve.drain()
                dve.tensor_copy(ef[:], ei[:])
                dve.drain()
                for t in range(TT):
                    dve.tensor_scalar(is1[:, t, :], k.c("iota64")[:, 0:32], ef[:, t, 0:1], None, ALU.is_equal)
                    dve.tensor_scalar(is2[:, t, :], k.c("iota64")[:, 0:32], ef[:, t, 1:2], None, ALU.is_equal)
                dve.drain()
                dve.tensor_tensor(chosen[:], is1[:], is2[:], ALU.add).then_inc(chosen_ready, 1)
                dve.wait_ge(part_ready, 1)
                dve.tensor_tensor(rest[:], h_tm, a["h2"][:, :, 0, :], ALU.subtract).then_inc(rest_ready, 1)
                dve.wait_ge(exp_done, 1)
                dve.tensor_reduce(gs[:], ge[:], AX, ALU.add)
                dve.tensor_scalar(w1[:], dl[:], 1.0, None, ALU.add)
                dve.drain()
                dve.tensor_tensor(w1[:], w1[:], gs[:], ALU.mult)
                dve.drain()
                dve.reciprocal(w1[:], w1[:])
                dve.drain()
                dve.tensor_tensor(w2[:], w1[:], dl[:], ALU.mult)
                dve.drain()
                for t in range(TT):
                    dve.tensor_scalar(is1[:, t, :], is1[:, t, :], w1[:, t:t + 1], None, ALU.mult)
                    dve.tensor_scalar(is2[:, t, :], is2[:, t, :], w2[:, t:t + 1], None, ALU.mult)
                dve.drain()
                dve.tensor_tensor(a["comb"][:, :, 0:N_EXP], is1[:], is2[:], ALU.add)
                dve.wait_ge(ranked, 1)
                r = a["rank"][:, :, 0:N_EXP]
                dve.scalar_tensor_tensor(out=r, in0=k.ps[:, 4, 0:64].rearrange("p (t e) -> p t e", t=TT), scalar=1.0,
                                         in1=chosen[:], op0=ALU.add, op1=ALU.mult)
                dve.tensor_reduce(most[:], k.ps[:, 5, 0:32], AX, ALU.max)
                dve.drain()
                dve.tensor_scalar(r, r, -1.0, None, ALU.add)
                dve.tensor_tensor(over[:], most[:].broadcast_to([P, 3]), k.c("slot_limits"), ALU.is_gt)
                dve.drain()
                dve.tensor_scalar(a["rank"][:, :, N_EXP:N_EXP + 1], a["rank"][:, :, 0:1], -float(SLOTS), None, ALU.add)
                dve.tensor_copy(a["comb"][:, :, N_EXP:N_EXP + 1], a["comb"][:, :, 0:1])
                dve.tensor_reduce(most[:], over[:], AX, ALU.add)
                dve.drain()
                dve.tensor_scalar(a["passes"][:], most[:], 1.0, None, ALU.add)
                dve.wait_ge(part_ready, 2)
                dve.tensor_tensor(a["h2"][:, :, 2, :], rest[:], a["h2"][:, :, 1, :], ALU.subtract)

            @block.scalar
            def _(act):
                act.wait_ge(gap_ready, 1)
                act.activation(ge[:], ge[:], ACT.Exp)
                act.activation(dl[:], dl[:], ACT.Exp).then_inc(exp_done, 1)
                act.wait_ge(h_turned, 1)
                act.copy(a["h2"][:, :, 0, :], h_tm).then_inc(part_ready, 1)
                act.wait_ge(rest_ready, 1)
                act.copy(a["h2"][:, :, 1, :], rest[:]).then_inc(part_ready, 1)


def stage_experts(k, a):
    S2, HALF = 2 * SLOTS, TILE // 2
    with ExitStack() as ctx:
        sb = lambda name, s, dt=F32: k.sb(name, s, dt, ctx=ctx)
        high, low = sb("w_high", [P, 3, TILE], F32R), sb("w_low", [P, 2, TILE], F32R)
        sel, selw = sb("sel", [P, TT, SLOTS], BF16), sb("sel_weighted", [P, TT, S2])
        selT = sb("selT", [P, 2, TOK])
        xg, act_t = sb("x_gathered", [P, KD, S2], F32R), sb("act_parts", [P, 4, S2], F32R)
        free = k.hT[:].rearrange("p f n -> p (f n)")
        h1, h3, y = free[:, 0:512], free[:, 512:1024], free[:, 1024:2048]
        gate, act_f = sb("gate", [P, 4, SLOTS]), sb("act_full", [P, 4, SLOTS])
        names = ("w_high_ready", "w_low_ready", "expert_tile_done", "sel_ready", "xg_done", "xg_high_ready", "xg_ready",
                 "h1_copied", "h3_copied", "folded", "silu_done", "act_ready", "selT_done", "selT_ready", "scattered",
                 "y0_done", "y0_ready", "y1_ready", "moe_zeroed", "moe_summed")
        (high_ready, low_ready, done, sel_ready, xg_done, xg_high, xg_ready, h1_copied, h3_copied, folded, silu_done,
         act_ready, selT_done, selT_ready, scattered, y0_done, y0_ready, y1_ready, zeroed, summed) = (
            k.sem(n) for n in names)
        landed = a["expert_landed"]
        LOW0, DONE0 = 5, 2
        acc = k.ps[:, 0:4, :].rearrange("p (t n) c -> p t n c", t=TT)
        xg_ps = k.ps[:, 4, :].rearrange("p (f s) -> p f s", f=KD)
        h1T, h3T = (k.ps[:, 5, 256 * i:256 * i + 256].rearrange("p (f s) -> p f s", f=4) for i in range(2))
        selT_ps = k.ps[:, 5, 0:TOK]
        h1_ps, h3_ps = k.ps[:, 6, :], k.ps[:, 7, :]
        y_ps = k.ps[:, 6:8, :]

        def passes(eng):
            return eng.value_load(a["passes"][0:1, 0:1], min_val=1, max_val=TOK // SLOTS)

        with k.nc.Block() as block:
            @block.sync
            def _(sp):
                n_pass = passes(sp)

                def free(step, j, h):
                    sp.wait_ge(low_ready, step * 6 + (LOW0 - 5 + 2 * j + h))

                def load(step, tile):
                    for j in range(3):
                        for h in range(2):
                            free(step, j, h)
                            at = slice(h * HALF, (h + 1) * HALF)
                            sp.dma_start(k.ring[:, j, at], tile(j)[:, at]).then_inc(landed[j][h], 16)

                with sp.Fori(0, n_pass) as p:
                    with sp.Fori(1, N_EXP) as e:
                        load(p * N_EXP + e, lambda j: k.dram["experts"][bass.ds(e * 3 + j, 1)]
                             .rearrange("a p n -> (a p) n"))
                    with sp.If(p < n_pass - 1):
                        load(p * N_EXP + N_EXP, lambda j: k.dram["experts"][j])
                for j in range(2):
                    for h in range(2):
                        free(n_pass * N_EXP, j, h)
                        sp.sem_inc(landed[j][h], 16)
                sp.wait_ge(low_ready, n_pass * (6 * N_EXP) + (LOW0 + 2))
                for j in range(RING):
                    if j == 1:
                        sp.wait_ge(high_ready, n_pass * (6 * N_EXP) + 4)
                    sp.dma_start(k.ring[:, j, :], k.dram["weights"][T_GLA + j]).then_inc(k.landed[j], 16)

            @block.tensor
            def _(pe):
                n_pass = passes(pe)

                def gather():
                    for f in range(KD):
                        for t in range(TT):
                            for part in range(3):
                                last = pe.matmul(xg_ps[:, f, :], a["h2"][:, t, part, f * P:(f + 1) * P], sel[:, t, :],
                                                 start=(t == 0 and part == 0), stop=(t == TT - 1 and part == 2))
                    last.then_inc(xg_done, 1)

                def turn_selection():
                    for t in range(TT):
                        last = pe.transpose(selT_ps[:, t * P:(t + 1) * P], selw[:, t, :], k.c("ident"))
                    last.then_inc(selT_done, 1)

                def scatter(b, start=False, stop=False):
                    for t in range(TT):
                        for n in range(2):
                            last = pe.matmul(acc[:, t, n, :], selT[:, b, t * P:(t + 1) * P], y[:, n * 512:(n + 1) * 512],
                                             start=start, stop=stop, skip_group_check=True)
                    return last

                def halves(j, b, s):
                    for h in range(2):
                        pe.wait_ge(low_ready, s * 6 + (2 * j + h + 1 + LOW0))
                        at = slice(h * HALF, (h + 1) * HALF)
                        yield h, [w[:, i, at].rearrange("p (k n) -> p k n", k=4 if j < 2 else 2)
                                  for w, i in ((high, j), (low, (b + j) % 2))]

                pe.wait_ge(zeroed, 1)
                pe.sem_inc(done, DONE0)
                scatter(1, start=True)
                pe.wait_ge(sel_ready, 1)
                gather()
                turn_selection()
                with pe.Fori(0, n_pass) as p:
                    with pe.Fori(0, N_EXP // 2) as i:
                        for b in range(2):
                            s = p * N_EXP + i * 2 + b
                            pe.wait_ge(xg_ready, s + 1)
                            for j, out, y_read in ((0, h1_ps, y0_ready), (1, h3_ps, y1_ready)):
                                pe.wait_ge(y_read, s + 1)
                                for h, parts in halves(j, b, s):
                                    for kk in range(4):
                                        for part, w in enumerate(parts):
                                            last = pe.matmul(out, xg[:, 4 * h + kk, :], w[:, kk, :],
                                                             start=(h + kk + part == 0),
                                                             stop=(h == 1 and kk == 3 and part == 1))
                                last.then_inc(done, 1)
                            pe.wait_ge(sel_ready, s + 2)
                            gather()
                            pe.wait_ge(selT_ready, s + 1)
                            for out, h_sb, copied in ((h1T, h1, h1_copied), (h3T, h3, h3_copied)):
                                pe.wait_ge(copied, s + 1)
                                for f in range(4):
                                    last = pe.matmul(out[:, f, :], h_sb[:, f * P:(f + 1) * P], k.c("fold"),
                                                     start=True, stop=True)
                            last.then_inc(folded, 1)
                            scatter(1 - b).then_inc(scattered, 1)
                            pe.wait_ge(act_ready, s + 2)
                            turn_selection()
                            pe.wait_ge(low_ready, s * 6 + (6 + LOW0))
                            w2 = [w[:, i, :].rearrange("p (k n) -> p k n", k=4) for w, i in ((high, 2), (low, b % 2))]
                            for n in range(2):
                                for f in range(4):
                                    for part, w in enumerate(w2):
                                        last = pe.matmul(y_ps[:, n, :], act_t[:, f, :], w[:, f, n * 512:(n + 1) * 512],
                                                         start=(f + part == 0), stop=(f == 3 and part == 1))
                                last.then_inc(y0_done if n == 0 else done, 1)
                pe.wait_ge(y0_ready, n_pass * N_EXP + 1)
                pe.wait_ge(y1_ready, n_pass * N_EXP + 1)
                scatter(1, stop=True).then_inc(summed, 1)

            @block.scalar
            def _(act):
                n_pass = passes(act)

                def split_high(j, s, n_landed):
                    act.wait_ge(done, s * 3 + (j - 2 + DONE0))
                    for h in range(2):
                        act.wait_ge(landed[j][h], n_landed)
                        at = slice(h * HALF, (h + 1) * HALF)
                        act.copy(high[:, j, at], k.ring[:, j, at]).then_inc(high_ready, 1)

                act.wait_ge(zeroed, 1)
                for j in range(2):
                    for h in range(2):
                        act.wait_ge(landed[j][h], 16)
                        at = slice(h * HALF, (h + 1) * HALF)
                        act.copy(high[:, j, at], k.ring[:, j, at]).then_inc(high_ready, 1)
                act.wait_ge(xg_done, 1)
                act.copy(xg[:, :, 0:SLOTS], xg_ps).then_inc(xg_high, 1)
                act.wait_ge(selT_done, 1)
                act.copy(selT[:, 0, :], selT_ps).then_inc(selT_ready, 1)
                with act.Fori(0, n_pass) as p:
                    with act.Fori(0, N_EXP // 2) as i:
                        for b in range(2):
                            s = p * N_EXP + i * 2 + b
                            split_high(2, s, s * 16 + 16)
                            act.wait_ge(done, s * 3 + (1 + DONE0))
                            act.copy(h1, h1_ps).then_inc(h1_copied, 1)
                            split_high(0, s + 1, s * 16 + 32)
                            act.wait_ge(xg_done, s + 2)
                            act.copy(xg[:, :, 0:SLOTS], xg_ps).then_inc(xg_high, 1)
                            act.wait_ge(folded, s + 1)
                            act.wait_ge(act_ready, s + 1)
                            act.activation(gate[:], h1T, ACT.Silu).then_inc(silu_done, 1)
                            split_high(1, s + 1, s * 16 + 32)
                            act.wait_ge(scattered, s + 1)
                            act.wait_ge(selT_done, s + 2)
                            act.copy(selT[:, 1 - b, :], selT_ps).then_inc(selT_ready, 1)
                            act.wait_ge(y0_done, s + 1)
                            act.copy(y[:, 0:512], y_ps[:, 0, :]).then_inc(y0_ready, 1)

            @block.vector
            def _(dve):
                n_pass = passes(dve)

                def split_low(j, lo, s, h):
                    dve.wait_ge(high_ready, s * 6 + (2 * j + h + 1))
                    dve.wait_ge(done, s * 3 + (j - 1 + DONE0))
                    at = slice(h * HALF, (h + 1) * HALF)
                    dve.tensor_tensor(low[:, lo, at], k.ring[:, j, at], high[:, j, at], ALU.subtract
                                      ).then_inc(low_ready, 1)

                def select(e):
                    for t in range(TT):
                        r = a["rank"][:, t, e]
                        dve.tensor_scalar(sel[:, t, :], k.c("iota64")[:, 0:SLOTS], r, None, ALU.is_equal)
                        last = dve.tensor_scalar(selw[:, t, :], k.c("iota64"), r, a["comb"][:, t, e],
                                                 ALU.is_equal, ALU.mult)
                    last.then_inc(sel_ready, 1)

                dve.memset(y, 0.0)
                dve.memset(selT[:], 0.0)
                dve.drain()
                dve.sem_inc(zeroed, 1)
                dve.sem_inc(y0_ready, 1)
                dve.sem_inc(y1_ready, 1)
                dve.sem_inc(act_ready, 1)
                dve.sem_inc(low_ready, LOW0)
                select(slice(0, 1))
                for h in range(2):
                    dve.wait_ge(high_ready, h + 1)
                    at = slice(h * HALF, (h + 1) * HALF)
                    dve.tensor_tensor(low[:, 0, at], k.ring[:, 0, at], high[:, 0, at], ALU.subtract
                                      ).then_inc(low_ready, 1)
                dve.wait_ge(xg_high, 1)
                dve.tensor_tensor(xg[:, :, SLOTS:S2], xg_ps, xg[:, :, 0:SLOTS], ALU.subtract).then_inc(xg_ready, 1)
                with dve.Fori(0, n_pass) as p:
                    with dve.Fori(0, N_EXP // 2) as i:
                        for b in range(2):
                            s = p * N_EXP + i * 2 + b
                            split_low(1, 1 - b, s, 0)
                            split_low(1, 1 - b, s, 1)
                            dve.wait_ge(xg_done, s + 1)
                            dve.wait_ge(selT_done, s + 1)
                            select(bass.ds(i * 2 + (b + 1), 1))
                            split_low(2, b, s, 0)
                            dve.wait_ge(done, s * 3 + (2 + DONE0))
                            dve.tensor_copy(h3, h3_ps).then_inc(h3_copied, 1)
                            split_low(2, b, s, 1)
                            dve.wait_ge(xg_high, s + 2)
                            dve.tensor_tensor(xg[:, :, SLOTS:S2], xg_ps, xg[:, :, 0:SLOTS], ALU.subtract
                                              ).then_inc(xg_ready, 1)
                            dve.wait_ge(silu_done, s + 1)
                            dve.tensor_tensor(act_f[:], gate[:], h3T, ALU.mult)
                            dve.tensor_tensor(act_t[:, :, 0:SLOTS], gate[:], h3T, ALU.mult)
                            dve.drain()
                            dve.tensor_tensor(act_t[:, :, SLOTS:S2], act_f[:], act_t[:, :, 0:SLOTS], ALU.subtract
                                              ).then_inc(act_ready, 1)
                            split_low(0, 1 - b, s + 1, 0)
                            split_low(0, 1 - b, s + 1, 1)
                            dve.wait_ge(done, s * 3 + (3 + DONE0))
                            dve.wait_ge(scattered, s + 1)
                            dve.tensor_copy(y[:, 512:1024], y_ps[:, 1, :]).then_inc(y1_ready, 1)
                    dve.drain()
                    dve.tensor_scalar(a["rank"][:], a["rank"][:], -float(SLOTS), None, ALU.add)
                    dve.drain()
                dve.wait_ge(summed, 1)
                dve.tensor_copy(a["moe"].rearrange("p t (n c) -> p t n c", n=2), acc[:])


def stage_first_end(k, a):
    nc = k.nc
    with ExitStack() as ctx:
        xn = k.sb("xn2", [P, TT, D], ctx=ctx)
        f = NormT(k, "norm_f", k.x, ctx, xn)
        g = NormT(k, "gla_norm", k.x, ctx, xn)
        x_ready, x_normed = k.sem("moe_added"), k.sem("x_normed")
        with nc.Block() as block:
            @block.vector
            def _(dve):
                dve.tensor_tensor(a["moe"], a["moe"], bc(k.row("b_g2"), 1, TT), ALU.mult)
                dve.drain()
                dve.tensor_tensor(k.x[:], k.x[:], a["moe"], ALU.add).then_inc(x_ready, 1)
                dve.wait_ge(f.rstd_ready, 1)
                for t in range(TT):
                    last = dve.scalar_tensor_tensor(out=k.x[:, t, :], in0=k.x[:, t, :], scalar=f.rstd[:, t:t + 1],
                                                    in1=k.row("norm_f_g"), op0=ALU.mult, op1=ALU.mult)
                last.then_inc(x_normed, 1)
                dve.drain()
                g.dve_scale(dve)
                g.dve_out(dve, k.hT, k.col("norm_w_2", 0, KD))

            @block.scalar
            def _(act):
                act.wait_ge(x_ready, 1)
                f.act(act)
                act.wait_ge(x_normed, 1)
                g.act(act)

            @block.gpsimd
            def _(pool):
                f.pool(pool)
                g.pool(pool)

            @block.tensor
            def _(pe):
                g.pe(pe)


def first_block(k):
    with ExitStack() as ctx:
        stage_modulation(k, k.hold_rows(("b_g1", "b_router"), ctx))
        a = {
            "logits": k.sb("logits", [P, TT, 36], ctx=ctx),
            "comb": k.sb("comb", [P, TT, N_EXP + 1], ctx=ctx),
            "rank": k.sb("rank", [P, TT, N_EXP + 1], ctx=ctx),
            "passes": k.sb("passes", [P, 1], I32, ctx=ctx),
            "expert_landed": [[k.sem(f"expert_landed_{j}_{h}") for h in range(2)] for j in range(RING)],
        }
        with ExitStack() as mixing:
            a |= {
                "w_gate": k.sb("w_gate", [P, KD, 8], ctx=mixing),
                "qkv": k.sb("qkv", [P, TT, 1536], ctx=mixing),
                "qk_mT": k.sb("qk_mT", [P, KD, 3 + TOK], ctx=mixing),
                "v_aug": k.sb("v_aug", [P, TT, 4, 129], ctx=mixing),
                "o_m": k.sb("o_m", [P, TT, 512], ctx=mixing),
                "gate_rows": k.sb("gate_rows", [4, 2, TOK], ctx=mixing),
                "a_rows": k.sb("a_rows", [4, TOK], ctx=mixing),
                "gcol": k.sb("gcol", [P, TT, P], ctx=mixing),
                "mix": k.sb("mix", [P, TT, D], ctx=mixing),
            }
            stage_in_projection(k, a)
            stage_attention(k, a)
            stage_conv(k, a)
            stage_mlstm(k, a)
            stage_out_projection(k, a)
        a["h2"] = k.sb("h2", [P, TT, 3, D], BF16, ctx=ctx)
        stage_route(k, a)
        a["moe"] = k.hT[:].rearrange("p f n -> p (f n)").rearrange("p (t d) -> p t d", t=TT)
        stage_experts(k, a)
        stage_first_end(k, a)


def stage_tiles(k, name, first, specs, sp_extra=None, act_extra=None):
    outs = {e: k.sem(f"{name}_out_{e}") for e in ("dve", "act")}
    nth = [sum(s[3] == spec[3] for s in specs[:m + 1]) for m, spec in enumerate(specs)]
    with k.nc.Block() as block:
        @block.sync
        def _(sp):
            if sp_extra:
                sp_extra(sp)
            stream(k, sp, first, first + len(specs))

        @block.tensor
        def _(pe):
            for m, (kind, src, k0, _engine, _write) in enumerate(specs):
                if m >= 3:
                    pe.wait_ge(outs[specs[m - 3][3]], nth[m - 3])
                if kind == "tm":
                    tm_tile(k, pe, first + m, src, pair(k, m), k0)
                else:
                    fm_tile(k, pe, first + m, src, pair_fm(k, m), k0)

        def write_out(engine, which):
            for m, (kind, _src, _k0, owner, write) in enumerate(specs):
                if owner == which:
                    engine.wait_ge(k.tile_done, first + m + 1)
                    write(engine, pair(k, m) if kind == "tm" else pair_fm(k, m)).then_inc(outs[which], 1)

        @block.vector
        def _(dve):
            write_out(dve, "dve")

        @block.scalar
        def _(act):
            if act_extra:
                act_extra(act)
            write_out(act, "act")


def copy_to(dst):
    return lambda dve, src: dve.tensor_copy(dst, src)


def silu_to(dst):
    return lambda act, src: act.activation(dst, src, ACT.Silu)


def add_after(dst):
    def write(dve, src):
        dve.drain()
        return dve.tensor_tensor(dst, dst, src, ALU.add)
    return write


def stage_gla_gate(k, a):
    with ExitStack() as ctx:
        rT = k.sb("rT", [16, TOK], ctx=ctx)
        g = k.sb("g_log", [P, TT, 512], ctx=ctx)
        lg = k.sb("g_tmp", [P, TT, 512], ctx=ctx)
        eq, ek = (k.sb(n, [P, TT, 512], ctx=ctx) for n in ("exp_q", "exp_k"))
        ee = lg
        r_done, rT_ready, g_pre, abs_ready, log_ready, g_ready, cum_done, exp_done, dec_ready, turned = (
            k.sem(s) for s in ("r_done", "rT_ready", "g_pre", "g_abs_ready", "g_log_ready", "g_ready", "cum_done",
                               "decay_exp_done", "decayed", "gla_turned"))
        q, key = a["qk"][:, :, 0:512], a["qk"][:, :, 512:1024]
        with k.nc.Block() as block:
            @block.tensor
            def _(pe):
                for kk in range(KD):
                    last = pe.matmul(k.ps[0:16, 7, 0:TOK], a["w_rank"][:, kk, :], k.hT[:, kk, :],
                                     start=(kk == 0), stop=(kk == KD - 1))
                last.then_inc(r_done, 1)
                pe.wait_ge(rT_ready, 1)
                for t in range(TT):
                    last = pe.matmul(k.ps[:, t, :], rT[:, t * P:(t + 1) * P], a["w_up"][:], start=True, stop=True)
                last.then_inc(g_pre, 1)
                pe.wait_ge(g_ready, 1)
                for t in range(TT):
                    pe.matmul(k.ps[:, 2 + t, :], k.c("chunk_tri"), g[:, t, :], start=True, stop=True)
                    pe.matmul(k.ps[:, 4 + t, :], k.c("chunk_suffix"), g[:, t, :], start=True, stop=True)
                    for h in range(4):
                        i = 2 * (4 * t + h)
                        last = pe.matmul(k.ps[:, 6, i:i + 2], g[:, t, h * P:(h + 1) * P], k.c("chunk_ind"),
                                         start=True, stop=True)
                last.then_inc(cum_done, 1)
                pe.wait_ge(dec_ready, 1)
                turn(k, pe, q, 4, k.ps[:, 0:2, :].rearrange("p b (f t) -> p (b f) t", f=2), turned)
                turn(k, pe, a["k_inv"], 4, k.ps[:, 2:4, :].rearrange("p b (f t) -> p (b f) t", f=2), turned)

            @block.scalar
            def _(act):
                act.wait_ge(abs_ready, 1)
                act.activation(lg[:], lg[:], ACT.Exp, scale=-1.0)
                act.drain()
                act.activation(lg[:], lg[:], ACT.Ln, bias=1.0).then_inc(log_ready, 1)
                act.wait_ge(cum_done, 1)
                act.activation(eq[:], k.ps[:, 2:4, :], ACT.Exp)
                act.activation(ek[:], k.ps[:, 2:4, :], ACT.Exp, scale=-1.0)
                act.activation(ee[:], k.ps[:, 4:6, :], ACT.Exp)
                act.activation(a["decay"][:], k.ps[:, 6, 0:16], ACT.Exp).then_inc(exp_done, 1)

            @block.vector
            def _(dve):
                dve.memset(a["att"][:], 0.0)
                dve.wait_ge(r_done, 1)
                dve.tensor_copy(rT[:], k.ps[0:16, 7, 0:TOK]).then_inc(rT_ready, 1)
                dve.wait_ge(g_pre, 1)
                dve.tensor_tensor(g[:], k.ps[:, 0:2, :], bc(k.row("gla_bias"), 1, TT), ALU.add)
                dve.drain()
                dve.scalar_tensor_tensor(out=lg[:], in0=g[:], scalar=-1.0, in1=g[:], op0=ALU.mult,
                                         op1=ALU.max).then_inc(abs_ready, 1)
                dve.wait_ge(log_ready, 1)
                dve.scalar_tensor_tensor(out=g[:], in0=g[:], scalar=0.0, in1=lg[:], op0=ALU.min, op1=ALU.subtract)
                dve.drain()
                dve.tensor_scalar(g[:], g[:], 1.0 / 16.0, None, ALU.mult).then_inc(g_ready, 1)
                dve.wait_ge(exp_done, 1)
                dve.scalar_tensor_tensor(out=q, in0=q, scalar=128 ** -0.5, in1=eq[:], op0=ALU.mult, op1=ALU.mult)
                dve.tensor_tensor(a["k_inv"][:], key, ek[:], ALU.mult)
                dve.drain()
                dve.tensor_tensor(key, key, ee[:], ALU.mult).then_inc(dec_ready, 1)
                dve.wait_ge(turned, 8)
                dve.tensor_copy(a["qT"][:], k.ps[:, 0:2, :].rearrange("p b (f t) -> p (b f) t", f=2))
                dve.tensor_copy(a["kT"][:], k.ps[:, 2:4, :].rearrange("p b (f t) -> p (b f) t", f=2))


def stage_gla(k, a):
    with ExitStack() as ctx:
        junk = k.sb("o_sq", [P, 512], ctx=ctx)
        ss = k.sb("o_ss", [P, 8], ctx=ctx)
        rstd = k.sb("o_rstd", [P, 8], ctx=ctx)
        att_done, att_ready, upd_done, state_ready, tile_out, o_ready, o_copied, summed, rstd_ready, o_normed, turned = (
            k.sem(s) for s in ("att_done", "att_ready", "state_update_done", "state_ready", "o_tile_out", "o_ready",
                               "o_copied", "o_summed", "o_rstd_ready", "o_normed", "o_turned"))
        state, v, key = a["state"], a["v"], a["qk"][:, :, 512:1024]
        half = lambda c: slice(64 * c, 64 * c + 64)
        ups = lambda h: k.ps[:, 4 + h, :]
        with k.nc.Block() as block:
            @block.tensor
            def _(pe):
                for h in range(4):
                    for t in range(TT):
                        s = slice(t * P, (t + 1) * P)
                        last = pe.matmul(k.ps[:, 4 + h // 2, 256 * (h % 2) + t * P:256 * (h % 2) + (t + 1) * P],
                                         a["kT"][:, h, s], a["qT"][:, h, s], start=True, stop=True)
                last.then_inc(att_done, 1)
                pe.wait_ge(att_ready, 1)

                def inter(t, c, stop):
                    for h in range(4):
                        pe.wait_ge(state_ready, 4 * (2 * t + c - 1) + h + 1)
                        last = pe.matmul(k.ps[half(c), h, :], a["qT"][:, h, t * P + 64 * c:t * P + 64 * c + 64],
                                         state[:, h, :], start=False, stop=stop, skip_group_check=True)
                    return last

                def update(t, c):
                    for h in range(4):
                        if 2 * t + c:
                            pe.wait_ge(state_ready, 4 * (2 * t + c - 1) + h + 1)
                        last = pe.matmul(ups(h), key[half(c), t, h * P:(h + 1) * P], v[half(c), t, h * 512:(h + 1) * 512],
                                         start=True, stop=True)
                        last.then_inc(upd_done, 1)

                for t in range(TT):
                    if t:
                        pe.wait_ge(tile_out, 1)
                    for h in range(4):
                        last = pe.matmul(k.ps[:, h, :], a["att"][:, 2 * h + t, :], v[:, t, h * 512:(h + 1) * 512],
                                         start=True, stop=False, skip_group_check=True)
                    if t:
                        inter(t, 0, False)
                    update(t, 0)
                    last = inter(t, 1, True)
                    if t == 0:
                        update(t, 1)
                    last.then_inc(o_ready, 1) if t else pe.sem_inc(o_ready, 1)
                for r in range(2):
                    pe.wait_ge(o_normed, 1)
                    turn(k, pe, v[:, :, r * 1024:(r + 1) * 1024], KD,
                         k.ps[:, 4 * r:4 * r + 4, :].rearrange("p b (f t) -> p (b f) t", f=2), turned)

            @block.vector
            def _(dve):
                dve.wait_ge(att_done, 1)
                dve.copy_predicated(a["att"][:], bc(k.c("chunk_tri"), 1, 8).bitcast(U32),
                                    k.ps[:, 4:6, :].rearrange("p b (i t) -> p (b i) t", i=4)).then_inc(att_ready, 1)
                for t, c in ((0, 0), (0, 1), (1, 0)):
                    for h in range(4):
                        i = 2 * t + c
                        dve.wait_ge(upd_done, 4 * i + h + 1)
                        if i == 0:
                            ins = dve.tensor_copy(state[:, h, :], ups(h))
                        else:
                            j = 2 * (4 * t + h) + c
                            ins = dve.scalar_tensor_tensor(out=state[:, h, :], in0=state[:, h, :],
                                                           scalar=a["decay"][:, j:j + 1], in1=ups(h),
                                                           op0=ALU.mult, op1=ALU.add)
                        ins.then_inc(state_ready, 1)
                    dve.drain()
                    if (t, c) == (0, 1):
                        dve.wait_ge(o_ready, 1)
                        dve.tensor_copy(v[:, 0, :].rearrange("p (h e) -> p h e", h=4), k.ps[:, 0:4, :]).then_inc(tile_out, 1)
                dve.wait_ge(o_ready, 2)
                dve.tensor_copy(v[:, 1, :].rearrange("p (h e) -> p h e", h=4), k.ps[:, 0:4, :]).then_inc(o_copied, 1)
                dve.wait_ge(rstd_ready, 1)
                for t in range(TT):
                    for h in range(4):
                        o = v[:, t, h * 512:(h + 1) * 512]
                        i = 4 * t + h
                        last = dve.scalar_tensor_tensor(out=o, in0=o, scalar=rstd[:, i:i + 1], in1=k.row("gla_out_g"),
                                                        op0=ALU.mult, op1=ALU.mult)
                last.then_inc(o_normed, 1)
                for r in range(2):
                    dve.wait_ge(turned, KD * (r + 1))
                    z = a["zT"][:, 8 * r:8 * r + 8, :]
                    dve.tensor_tensor(z, z, k.ps[:, 4 * r:4 * r + 4, :].rearrange("p b (f t) -> p (b f) t", f=2), ALU.mult)

            @block.scalar
            def _(act):
                act.wait_ge(tile_out, 1)
                act.wait_ge(o_copied, 1)
                for t in range(TT):
                    for h in range(4):
                        i = 4 * t + h
                        act.activation(junk[:], v[:, t, h * 512:(h + 1) * 512], ACT.Square,
                                       accum_out=ss[:, i:i + 1]).then_inc(summed, 1)
                        act.drain()

            @block.gpsimd
            def _(pool):
                pool.wait_ge(summed, 8)
                rsqrt_mean(k, pool, rstd[:], ss[:], 512).then_inc(rstd_ready, 1)


def stage_memory_attention(k, a, name):
    with ExitStack() as ctx:
        p = k.sb(f"{name}_p", [P, 8, TOK], ctx=ctx)
        pT = k.sb(f"{name}_pT", [P, 4, 2, TOK], ctx=ctx)
        mx = k.sb(f"{name}_mx", [P, 8], ctx=ctx)
        rs = k.sb(f"{name}_rs", [P, 8], ctx=ctx)
        scored, max_ready, exp_done, p_ready, turned, pT_ready, out_done = (
            k.sem(f"{name}_{s}") for s in ("scored", "max_ready", "exp_done", "p_ready", "p_turned", "pT_ready", "out_done"))
        s_ps = k.ps[:, 0:4, :].rearrange("p h (t m) -> p (h t) m", t=2)
        t_ps = k.ps[:, 4:8, :].rearrange("p h (m t) -> p h m t", m=2)
        o_ps = k.ps[:, 0:4, :].rearrange("p b (f t) -> p (b f) t", f=2)
        with k.nc.Block() as block:
            @block.tensor
            def _(pe):
                for h in range(4):
                    for t in range(TT):
                        for c in range(2):
                            last = pe.matmul(s_ps[:, 2 * h + t, :], a["xqT"][:, 2 * h + c, t * P:(t + 1) * P],
                                             a["kmT"][:, 2 * h + c, :], start=(c == 0), stop=(c == 1))
                last.then_inc(scored, 1)
                pe.wait_ge(p_ready, 1)
                for h in range(4):
                    for m in range(2):
                        for t in range(TT):
                            last = pe.transpose(t_ps[:, h, m, t * P:(t + 1) * P], p[:, 2 * h + t, m * P:(m + 1) * P],
                                                k.c("ident"))
                last.then_inc(turned, 1)
                pe.wait_ge(pT_ready, 1)
                for f in range(8):
                    for m in range(2):
                        last = pe.matmul(o_ps[:, f, :], a["vm"][:, m, f * P:(f + 1) * P], pT[:, f // 2, m, :],
                                         start=(m == 0), stop=(m == 1))
                last.then_inc(out_done, 1)

            @block.scalar
            def _(act):
                act.wait_ge(max_ready, 1)
                for i in range(8):
                    last = act.activation(p[:, i, :], s_ps[:, i, :], ACT.Exp, bias=mx[:, i:i + 1], scale=1.0 / 16.0,
                                          accum_out=rs[:, i:i + 1])
                last.then_inc(exp_done, 1)

            @block.vector
            def _(dve):
                dve.wait_ge(scored, 1)
                dve.tensor_reduce(mx[:], s_ps[:], AX, ALU.max)
                dve.drain()
                dve.tensor_scalar(mx[:], mx[:], -1.0 / 16.0, None, ALU.mult).then_inc(max_ready, 1)
                dve.wait_ge(exp_done, 1)
                dve.reciprocal(rs[:], rs[:])
                dve.drain()
                for i in range(8):
                    last = dve.tensor_scalar(p[:, i, :], p[:, i, :], rs[:, i:i + 1], None, ALU.mult)
                last.then_inc(p_ready, 1)
                dve.wait_ge(turned, 1)
                dve.tensor_copy(pT[:], t_ps[:]).then_inc(pT_ready, 1)
                dve.wait_ge(out_done, 1)
                z = a["zT"][:, 16:24, :]
                dve.tensor_tensor(z, z, o_ps[:], ALU.mult)


def out_specs(k, zT):
    return [("tm", zT, 8 * kb, "dve", add_after(k.x[:, :, n * 512:(n + 1) * 512])) for n in range(2) for kb in range(3)]


def gla_layer(k):
    with ExitStack() as ctx:
        sb = lambda n, s: k.sb(n, s, ctx=ctx)
        a = {"zT": sb("gla_zT", [P, 24, TOK])}
        with ExitStack() as mid:
            sm = lambda n, s: k.sb(n, s, ctx=mid)
            a |= {"xqT": sm("gla_xqT", [P, 8, TOK]), "kmT": sm("gla_kmT", [P, 8, TOK]), "vm": sm("gla_vm", [P, TT, 1024])}
            with ExitStack() as inner:
                si = lambda n, s: k.sb(n, s, ctx=inner)
                a |= {"w_rank": si("w_rank", [P, KD, 16]), "w_up": si("w_up", [16, 512]),
                      "qk": si("gla_qk", [P, TT, 1024]), "v": si("gla_v", [P, TT, 2048])}
                low_in = k.sem("low_rank_in")
                rows = k.hold_rows(("gla_bias", "gla_out_g"), inner)

                def load(sp):
                    sp.dma_start(a["w_rank"][:], k.dram["w_rank"]).then_inc(low_in, 16)
                    sp.dma_start(a["w_up"][:], k.dram["w_up"]).then_inc(low_in, 16)
                    sp.dma_start(*rows).then_inc(low_in, 16)
                    sp.wait_ge(low_in, 48)

                zf = lambda m: a["zT"][:, 4 * m:4 * m + 4, :]
                specs = [("tm", k.hT, 0, "dve", copy_to(a["qk"][:, :, m * 512:(m + 1) * 512])) for m in range(2)]
                specs += [("tm", k.hT, 0, "dve", copy_to(a["v"][:, :, m * 512:(m + 1) * 512])) for m in range(4)]
                specs += [("fm", k.hT, 0, "act", silu_to(zf(m))) for m in range(6)]
                specs += [("fm", k.hT, 0, "dve", copy_to(a["xqT"][:, 4 * m:4 * m + 4, :])) for m in range(2)]
                specs += [("fm", k.memT, 0, "dve", copy_to(a["kmT"][:, 4 * m:4 * m + 4, :])) for m in range(2)]
                specs += [("tm", k.memT, 0, "dve", copy_to(a["vm"][:, :, m * 512:(m + 1) * 512])) for m in range(2)]
                stage_tiles(k, "gla_in", T_GLA, specs, sp_extra=load)
                with ExitStack() as rec:
                    sr = lambda n, s: k.sb(n, s, ctx=rec)
                    a |= {"k_inv": sr("k_inv", [P, TT, 512]), "decay": sr("decay", [P, 16]),
                          "state": None, "qT": k.hT[:, 0:4, :], "kT": k.hT[:, 4:8, :], "att": sr("att", [P, 8, P])}
                    stage_gla_gate(k, a)
                    a["state"] = sr("state", [P, 4, 512])
                    stage_gla(k, a)
            stage_memory_attention(k, a, "xa0")
        stage_tiles(k, "gla_out", T_GLA_OUT, out_specs(k, a["zT"]))
        xn = k.sb("xn3", [P, TT, D], ctx=ctx)
        norm_stage(k, NormT(k, "s5_norm", k.x, ctx, xn), k.col("norm_w_2", 8, KD))


def norm_stage(k, norm, gain):
    with k.nc.Block() as block:
        @block.scalar
        def _(act):
            norm.act(act)

        @block.gpsimd
        def _(pool):
            norm.pool(pool)

        @block.vector
        def _(dve):
            norm.dve_scale(dve)
            norm.dve_out(dve, k.hT, gain)

        @block.tensor
        def _(pe):
            norm.pe(pe)


def stage_s5_input(k, a):
    n = 1024
    with ExitStack() as ctx:
        sb = lambda name, w: k.sb(name, [P, w], ctx=ctx)
        lr, li, ls, dt = sb("lam_re", n), sb("lam_im", n), sb("log_step", 16), sb("dt", 16)
        mag, th, s, c, t1, t2 = (sb(f"s5_{x}", n) for x in ("mag", "th", "sin", "cos", "t1", "t2"))
        lrs, lis, lss = sb("lam_re_s", 64), sb("lam_im_s", 64), sb("log_step_s", 64)
        ts, red = sb("theta_s", 64), sb("theta_red", 64)
        lam_in, dt_ready, args_ready, trig_ready, u_out = (
            k.sem(x) for x in ("lam_in", "dt_ready", "s5_args_ready", "s5_trig_ready", "u_out"))
        by_tile = lambda x: x[:].rearrange("p (f s) -> p f s", f=16)
        with k.nc.Block() as block:
            @block.sync
            def _(sp):
                for dst, name in ((lr, "lam_re_f"), (li, "lam_im_f"), (ls, "log_step_f"), (lrs, "lam_re_s"),
                                  (lis, "lam_im_s"), (lss, "log_step_s")):
                    sp.dma_start(dst[:], k.dram[name]).then_inc(lam_in, 16)
                stream(k, sp, T_S5, T_S5 + 4)

            @block.tensor
            def _(pe):
                for m in range(4):
                    if m == 3:
                        pe.wait_ge(u_out, 1)
                    fm_tile(k, pe, T_S5 + m, k.hT, pair_fm(k, m))

            @block.scalar
            def _(act):
                act.wait_ge(lam_in, 96)
                act.activation(dt[:], ls[:], ACT.Exp)
                act.activation(lss[:], lss[:], ACT.Exp).then_inc(dt_ready, 1)

                def u_tile(m):
                    act.wait_ge(k.tile_done, T_S5 + m + 1)
                    act.copy(a["uT"][:, 4 * m:4 * m + 4, :], pair_fm(k, m)).then_inc(u_out, 1)

                u_tile(0)
                act.wait_ge(args_ready, 1)
                act.activation(mag[:], mag[:], ACT.Exp)
                act.activation(a["decay"][:], a["decay"][:], ACT.Exp)
                act.activation(s[:], th[:], ACT.Sin)
                act.activation(c[:], c[:], ACT.Sin).then_inc(trig_ready, 1)
                for m in range(1, 4):
                    u_tile(m)

            @block.vector
            def _(dve):
                dve.memset(a["half_pi"][:], float(np.pi / 2))
                dve.wait_ge(dt_ready, 1)
                dtb = bc(dt[:], 2, 64)
                dve.tensor_tensor(by_tile(mag), by_tile(lr), dtb, ALU.mult)
                dve.tensor_tensor(by_tile(t1), by_tile(li), dtb, ALU.mult)
                dve.tensor_tensor(a["decay"][:], lrs[:], lss[:], ALU.mult)
                dve.tensor_tensor(ts[:], lis[:], lss[:], ALU.mult)
                dve.drain()
                range_reduce(dve, th[:], t2[:], t1[:])
                dve.drain()
                quarter_turn(dve, c[:], t2[:], th[:])
                dve.drain()
                range_reduce(dve, red[:], lss[:], ts[:])
                dve.drain()
                dve.tensor_scalar(a["turns"][:], red[:], 1.0 / TWO_PI, None, ALU.mult).then_inc(args_ready, 1)
                dve.wait_ge(trig_ready, 1)
                dve.tensor_tensor(c[:], c[:], mag[:], ALU.mult)
                dve.tensor_tensor(s[:], s[:], mag[:], ALU.mult)
                dve.tensor_tensor(t1[:], lr[:], lr[:], ALU.mult)
                dve.tensor_tensor(t2[:], li[:], li[:], ALU.mult)
                dve.drain()
                dve.tensor_scalar(c[:], c[:], -1.0, None, ALU.add)
                dve.tensor_tensor(t1[:], t1[:], t2[:], ALU.add)
                dve.drain()
                dve.reciprocal(t1[:], t1[:])
                dve.tensor_tensor(mag[:], c[:], lr[:], ALU.mult)
                dve.tensor_tensor(th[:], s[:], li[:], ALU.mult)
                dve.drain()
                dve.tensor_tensor(mag[:], mag[:], th[:], ALU.add)
                dve.tensor_tensor(s[:], s[:], lr[:], ALU.mult)
                dve.tensor_tensor(c[:], c[:], li[:], ALU.mult)
                dve.drain()
                dve.tensor_tensor(a["coef_re"][:], mag[:], t1[:], ALU.mult)
                dve.tensor_tensor(s[:], s[:], c[:], ALU.subtract)
                dve.drain()
                dve.tensor_tensor(a["coef_im"][:], s[:], t1[:], ALU.mult)


S5_STEPS = 8


def stage_s5_scan(k, a):
    with ExitStack() as ctx:
        sb = lambda name, s: k.sb(name, s, ctx=ctx)
        braw, bb, bt = sb("b_raw", [P, 2, 2, P]), sb("b_bar", [P, 2, 2, P]), sb("b_tmp", [P, P])
        craw, u_stage = sb("c_raw", [P, 2, 4, 2, 32]), sb("u_stage", [P, 2, TOK])
        frac = sb("s5_frac", [P, 4, TOK])
        sin, cos = ([sb(f"s5_{x}{i}", [P, 4, TOK]) for i in range(2)] for x in ("sin", "cos"))
        pa, pb, pc, pd = (sb(f"s5_{x}", [P, 4, TOK]) for x in ("pa", "pb", "pc", "pd"))
        x_re, x_im, t_re, t_im = (sb(f"s5_{x}", [P, 4, TOK]) for x in ("x_re", "x_im", "t_re", "t_im"))
        b_in = [k.sem(f"s5_b_in_{i}") for i in range(2)]
        c_in = [k.sem(f"s5_c_in_{i}") for i in range(2)]
        names = ("b_bar_ready", "bu_done", "u_staged", "phi_ready", "turn_ready", "frac_ready", "rotated_out",
                 "y_done", "y_out", "tile_out", "table_used")
        (bb_ready, bu_done, u_staged, phi_ready, turn_ready, frac_ready, rotated, y_done, y_out, tile_out,
         table_used) = (k.sem(f"s5_{x}") for x in names)
        dense = k.ps[:, 6:8, :].rearrange("p b (f t) -> p (b f) t", f=2)
        first = T_S5 + 4
        N = S5_STEPS
        after_step = {1: 0, 3: 1, 5: 2}
        iota = k.c("iota256")
        bur, bui = (k.ps[:, 0:4, c * TOK:(c + 1) * TOK] for c in range(2))
        with k.nc.Block() as block:
            @block.sync
            def _(sp):
                with sp.Fori(0, 2) as r:
                    for q in range(N):
                        sp.wait_ge(bb_ready, r * N + (q + 1))
                        sp.dma_start(braw[:, q % 2], k.dram["s5_b"][bass.ds(r * N + q, 1)].rearrange("a p c s -> (a p) c s")
                                     ).then_inc(b_in[q % 2], 16)
                        if q - 2 in after_step:
                            j = after_step[q - 2]
                            slot = (first + j) % RING
                            sp.wait_ge(k.tile_done, r * 3 + (first + j + 1))
                            sp.dma_start(k.ring[:, slot, :], k.dram["weights"][bass.ds(r * 3 + (first + j + RING), 1)]
                                         .rearrange("a p n -> (a p) n")).then_inc(k.landed[slot], 16)

            @block.gpsimd
            def _(pool):
                pool.sem_inc(bb_ready, 2)
                with pool.Fori(0, 2) as r:
                    for q in range(N):
                        b, s = q % 2, r * N + q
                        pool.wait_ge(b_in[b], r * (8 * N) + 16 * (q // 2 + 1))
                        pool.wait_ge(bu_done, s + 1)
                        cr, ci = (bc(a[x][:, bass.ds(r * (64 * N) + 64 * q, 64)], 1, 2) for x in ("coef_re", "coef_im"))
                        b_re, b_im = (braw[:, b, x].rearrange("p (g s) -> p g s", g=2) for x in range(2))
                        o_re, o_im = (bb[:, b, x].rearrange("p (g s) -> p g s", g=2) for x in range(2))
                        tmp = bt[:].rearrange("p (g s) -> p g s", g=2)
                        pool.tensor_tensor(o_re, b_re, cr, ALU.mult)
                        pool.tensor_tensor(tmp, b_im, ci, ALU.mult)
                        pool.tensor_tensor(o_im, b_im, cr, ALU.mult)
                        pool.drain()
                        pool.tensor_tensor(o_re, o_re, tmp, ALU.subtract)
                        pool.drain()
                        pool.tensor_tensor(tmp, b_re, ci, ALU.mult)
                        pool.drain()
                        pool.tensor_tensor(o_im, o_im, tmp, ALU.add).then_inc(bb_ready, 1)
                        pool.drain()

            @block.tensor
            def _(pe):
                pe.sem_inc(bu_done, 2)
                with pe.Fori(0, 2) as r:
                    def bu(q):
                        pe.wait_ge(bb_ready, r * N + (q + 3))
                        pe.wait_ge(u_staged, r * N + (q + 1))
                        for j in range(4):
                            rows = slice(32 * j, 32 * j + 32)
                            for c in range(2):
                                last = pe.matmul(k.ps[:, j, c * TOK:(c + 1) * TOK], bb[rows, q % 2, c, :],
                                                 u_stage[rows, q % 2, :], start=True, stop=True)
                        last.then_inc(bu_done, 1)

                    bu(0)
                    for q in range(N):
                        if q < N - 1:
                            bu(q + 1)
                        if q in after_step:
                            j = after_step[q]
                            slot, full = (first + j) % RING, 16 * ((first + j) // RING + 1)
                            pe.wait_ge(tile_out, r * 3 + (j + 1))
                            pe.wait_ge(k.landed[slot], r * 16 + full)
                            w = k.ring[:, slot, :].rearrange("p (k n) -> p k n", k=KD)
                            for f in range(4):
                                for kk in range(KD):
                                    last = pe.matmul(dense[:, f, :], w[:, kk, f * P:(f + 1) * P], k.hT[:, kk, :],
                                                     start=(kk == 0), stop=(kk == KD - 1))
                            last.then_inc(k.tile_done, 1)
                        pe.wait_ge(rotated, r * N + (q + 1))
                        pe.wait_ge(c_in[q % 2], r * (8 * N) + 16 * (q // 2 + 1))
                        for j in range(4):
                            o = k.ps[32 * j:32 * j + 32, 4 + q % 2, 0:TOK]
                            for i, (c, x) in enumerate(((0, x_re), (0, t_re), (1, x_im), (1, t_im))):
                                last = pe.matmul(o, craw[:, q % 2, j, c, :], x[:, j, :], start=(i == 0), stop=(i == 3))
                        last.then_inc(y_done, 1)

            @block.scalar
            def _(act):
                with act.Fori(0, 2) as r:
                    def tables(q):
                        b = q % 2
                        act.wait_ge(table_used, r * N + (q + 1))
                        for j in range(4):
                            last = act.activation(sin[b][:, j, :], iota, ACT.Copy,
                                                  scale=a["turns"][:, bass.ds(r * (4 * N) + (4 * q + j), 1)])
                        last.then_inc(phi_ready, 1)
                        act.wait_ge(frac_ready, r * N + (q + 1))
                        act.activation(sin[b][:], frac[:], ACT.Sin, scale=6.2831845)
                        act.activation(cos[b][:], frac[:], ACT.Abs)
                        act.drain()
                        act.activation(cos[b][:], cos[b][:], ACT.Sin, scale=-6.2831845,
                                       bias=a["half_pi"][:]).then_inc(turn_ready, 1)

                    tables(0)
                    for q in range(N):
                        act.wait_ge(y_out, r * N + (q + 1))
                        act.dma_start(craw[:, q % 2], k.dram["s5_c"][bass.ds(r * N + q, 1)]
                                      .rearrange("a p q c h -> (a p) q c h")).then_inc(c_in[q % 2], 16)
                        if q < N - 1:
                            tables(q + 1)
                        if q - 1 in after_step:
                            j = after_step[q - 1]
                            act.wait_ge(k.tile_done, r * 3 + (first + j + 1))
                            act.activation(a["zT"][:, bass.ds(r * 12 + 4 * j, 4), :], dense[:], ACT.Copy).then_inc(tile_out, 1)

            @block.vector
            def _(dve):
                dve.sem_inc(y_out, 2)
                dve.sem_inc(table_used, 2)
                dve.sem_inc(tile_out, 1)
                with dve.Fori(0, 2) as r:
                    def feature(q):
                        return a["uT"][:, bass.ds(r * N + q, 1), :].rearrange("p a t -> p (a t)")

                    def stage_u(q):
                        dve.tensor_copy(u_stage[:, q % 2, :], feature(q)).then_inc(u_staged, 1)

                    def fraction(q):
                        b = q % 2
                        dve.wait_ge(phi_ready, r * N + (q + 1))
                        dve.tensor_scalar(frac[:], sin[b][:], ROUND, -ROUND, ALU.add, ALU.add)
                        dve.drain()
                        dve.tensor_tensor(frac[:], sin[b][:], frac[:], ALU.subtract).then_inc(frac_ready, 1)

                    def take_y(q):
                        dve.wait_ge(y_done, r * N + (q + 1))
                        dve.scalar_tensor_tensor(out=feature(q), in0=feature(q), in1=k.ps[:, 4 + q % 2, 0:TOK],
                                                 scalar=k.cols[:, bass.ds(r * N + (COLS["s5_d"][0] + q), 1)],
                                                 op0=ALU.mult, op1=ALU.add).then_inc(y_out, 1)

                    stage_u(0)
                    fraction(0)
                    for q in range(N):
                        b = q % 2
                        dve.wait_ge(turn_ready, r * N + (q + 1))
                        dve.wait_ge(bu_done, r * N + (q + 3))
                        dve.tensor_tensor(pa[:], bur, cos[b][:], ALU.mult)
                        dve.tensor_tensor(pb[:], bui, sin[b][:], ALU.mult)
                        dve.tensor_tensor(pc[:], bur, sin[b][:], ALU.mult)
                        dve.tensor_tensor(pd[:], bui, cos[b][:], ALU.mult)
                        dve.drain()
                        if q < N - 1:
                            stage_u(q + 1)
                        dve.tensor_tensor(pa[:], pa[:], pb[:], ALU.add)
                        dve.tensor_tensor(pc[:], pc[:], pd[:], ALU.subtract)
                        if q < N - 1:
                            fraction(q + 1)
                        dve.drain()
                        for j in range(4):
                            d = a["decay"][:, bass.ds(r * (4 * N) + (4 * q + j), 1)].broadcast_to([P, TOK])
                            dve.tensor_tensor_scan(pb[:, j, :], d, pa[:, j, :], 0.0, ALU.mult, ALU.add)
                            dve.tensor_tensor_scan(pd[:, j, :], d, pc[:, j, :], 0.0, ALU.mult, ALU.add)
                        dve.drain()
                        if q:
                            take_y(q - 1)
                        dve.tensor_tensor(x_re[:], pb[:], cos[b][:], ALU.mult)
                        dve.tensor_tensor(t_re[:], pd[:], sin[b][:], ALU.mult)
                        dve.tensor_tensor(x_im[:], pd[:], cos[b][:], ALU.mult)
                        dve.scalar_tensor_tensor(out=t_im[:], in0=pb[:], scalar=-1.0, in1=sin[b][:],
                                                 op0=ALU.mult, op1=ALU.mult).then_inc(rotated, 1)
                        dve.drain()
                        dve.sem_inc(table_used, 1)
                    take_y(N - 1)


def stage_glu_gate(k, a):
    sig_ready = k.sem("sig_ready")
    with k.nc.Block() as block:
        @block.scalar
        def _(act):
            for f in range(16):
                act.activation(a["glu"][:, f, :], a["glu"][:, f, :], ACT.Sigmoid, bias=k.col("s5_b_glu", f)).then_inc(sig_ready, 1)

        @block.vector
        def _(dve):
            z = a["zT"][:, 0:16, :]
            dve.tensor_tensor(z, z, a["uT"][:], ALU.mult)
            dve.wait_ge(sig_ready, 16)
            dve.drain()
            dve.tensor_tensor(z, z, a["glu"][:], ALU.mult)


def s5_layer(k):
    with ExitStack() as ctx:
        uT = k.sb("uT", [P, 16, TOK], ctx=ctx)
        a = {"uT": uT}
        a["zT"] = k.sb("s5_zT", [P, 24, TOK], ctx=ctx)
        with ExitStack() as rec:
            for n in ("coef_re", "coef_im"):
                a[n] = k.sb(n, [P, 1024], ctx=rec)
            a["decay"], a["turns"] = k.sb("s5_decay", [P, 64], ctx=rec), k.sb("s5_turns", [P, 64], ctx=rec)
            a["half_pi"] = k.sb("half_pi", [P, 1], ctx=rec)
            stage_s5_input(k, a)
            stage_s5_scan(k, a)
        with ExitStack() as mid:
            sm = lambda n, s: k.sb(n, s, ctx=mid)
            a |= {"xqT": sm("s5_xqT", [P, 8, TOK]), "kmT": sm("s5_kmT", [P, 8, TOK]), "vm": sm("s5_vm", [P, TT, 1024])}
            specs = [("fm", k.hT, 0, "dve", copy_to(a["xqT"][:, 4 * m:4 * m + 4, :])) for m in range(2)]
            specs += [("fm", k.memT, 0, "dve", copy_to(a["kmT"][:, 4 * m:4 * m + 4, :])) for m in range(2)]
            specs += [("tm", k.memT, 0, "dve", copy_to(a["vm"][:, :, m * 512:(m + 1) * 512])) for m in range(2)]

            def activate(act):
                act.activation(uT[:], uT[:], ACT.Gelu_apprx_tanh)
                act.activation(a["zT"][:], a["zT"][:], ACT.Silu)

            stage_tiles(k, "s5_in", T_S5 + 10, specs, act_extra=activate)
            stage_memory_attention(k, a, "xa1")
        a["glu"] = k.sb("glu", [P, 16, TOK], ctx=ctx)
        specs = []
        for n in range(4):
            g = a["glu"][:, 4 * n:4 * n + 4, :]
            specs += [("fm", uT, 0, "dve", copy_to(g)), ("fm", uT, 8, "dve", add_after(g))]
        stage_tiles(k, "glu", T_GLU, specs)
        stage_glu_gate(k, a)
        stage_tiles(k, "s5_out", T_S5_OUT, out_specs(k, a["zT"]))


def final_norm(k):
    with ExitStack() as ctx:
        xn = k.sb("xn4", [P, TT, D], ctx=ctx)
        norm = NormT(k, "final", k.x, ctx, xn)
        rows, rows_in = k.hold_rows(("final_norm",), ctx), k.sem("final_row_in")
        with k.nc.Block() as block:
            @block.sync
            def _(sp):
                sp.dma_start(*rows).then_inc(rows_in, 16)

            @block.scalar
            def _(act):
                norm.act(act)

            @block.gpsimd
            def _(pool):
                norm.pool(pool)

            @block.vector
            def _(dve):
                dve.wait_ge(rows_in, 16)
                dve.wait_ge(norm.rstd_ready, 1)
                for t in range(TT):
                    dve.scalar_tensor_tensor(out=k.x[:, t, :], in0=k.x[:, t, :], scalar=norm.rstd[:, t:t + 1],
                                             in1=k.row("final_norm"), op0=ALU.mult, op1=ALU.mult)


def build(nc, dram, out):
    with ExitStack() as ctx:
        k = Core(nc, ctx, dram)
        first_block(k)
        k.clear_stage_sems()
        gla_layer(k)
        k.clear_stage_sems()
        s5_layer(k)
        final_norm(k)
        store(k, out)


def store(k, out):
    stored = k.sem("stored")
    with k.nc.Block() as block:
        @block.sync
        def _(sp):
            sp.dma_start(out.rearrange("a (t p) d -> p (a t) d", p=P), k.x[:]).then_inc(stored, 16)
            sp.wait_ge(stored, 16)



def constants():
    c = np.zeros((P, N_CONST), np.float32)
    p = np.arange(P)

    def put(name, value):
        a, b = CONSTS[name]
        c[:, a:b] = np.asarray(value, np.float32).reshape(P, -1)

    put("ident", np.eye(P))
    q = p[:, None, None] + P * np.arange(TT)[None, :, None]
    put("causal", np.where(np.arange(TOK)[None, None, :] <= q, 0.0, NEG))
    put("causal_t", np.where(p[:, None] <= p[None, :], 0.0, NEG))
    put("inv_freq", np.tile(np.float32(10000.0) ** (-np.arange(32, dtype=np.float32) / np.float32(32)), (P, 1)))
    put("iota64", np.tile(np.arange(2 * SLOTS) % SLOTS, (P, 1)))
    put("fold", p[:, None] % SLOTS == np.arange(SLOTS)[None, :])
    hot = np.zeros((P, 4, P))
    for h in range(4):
        hot[h, h] = 1.0
    put("one_hot4", hot)
    same = p[:, None] // 64 == p[None, :] // 64
    put("chunk_tri", same & (p[:, None] <= p[None, :]))
    put("chunk_suffix", same & (p[:, None] > p[None, :]))
    put("chunk_ind", p[:, None] // 64 == np.arange(2)[None, :])
    put("iota256", np.tile(np.arange(TOK), (P, 1)))
    put("minus_half", np.full((P, 16), -0.5))
    put("before", p[:, None] < p[None, :])
    put("ones", np.ones((P, P)))
    put("slot_limits", np.tile(SLOTS * np.arange(1, 4), (P, 1)))
    return c


def s5_arrays(g):
    lam_re, lam_im, step = g["s5_lam_re_2"][0], g["s5_lam_im_2"][0], g["s5_log_step_2"][0]

    def feature(v):
        v = v.reshape(16, 8, 1, -1)
        return np.broadcast_to(v, (16, 8, 16, v.shape[-1])).transpose(1, 2, 0, 3).reshape(P, -1)

    def state(v):
        return v.reshape(64, 2, 64).transpose(1, 2, 0).reshape(P, 64)

    b = np.zeros((16, 4, 2, 16, 2, 2, 64), np.float32)
    c = np.zeros((16, 2, 64, 4, 2, 2, 16), np.float32)
    for part, (bv, cv) in enumerate(((g["s5_b_re_2"][0], g["s5_c_re_2"][0]), (g["s5_b_im_2"][0], g["s5_c_im_2"][0]))):
        bv = bv.reshape(16, 4, 2, 64, 16)
        cv = cv.reshape(16, 4, 2, 16, 64)
        for q in range(2):
            b[:, :, q, :, part, q, :] = bv[:, :, q].transpose(0, 1, 3, 2)
            c[:, q, :, :, part, q, :] = cv[:, :, q].transpose(0, 3, 1, 2)
    return {
        "lam_re_f": feature(lam_re), "lam_im_f": feature(lam_im), "log_step_f": feature(step[:, None]),
        "lam_re_s": state(lam_re), "lam_im_s": state(lam_im),
        "log_step_s": state(np.broadcast_to(step[:, None], (P, 64))),
        "s5_b": b.reshape(16, P, 2, P), "s5_c": c.reshape(16, P, 4, 2, 32),
    }


def kernel(**inputs):
    import concourse.bacc as bacc
    from concourse.bass_utils import run_bass_kernel_spmd

    g = {n: np.asarray(v) for n, v in inputs.items()}

    def wide(w, rows=1024, width=512):
        kt, nt = w.shape[0] // rows, w.shape[1] // width
        w = w.reshape(kt, rows // P, P, nt, width).transpose(3, 0, 2, 1, 4)
        return w.reshape(nt * kt, P, TILE)

    w_in = g["w_in"][0]
    gla = g["gla_w_in_2"][0]
    ada = wide(g["w_ada"][0])
    kv = [wide(g["xa_w_kv_2"][i]) for i in range(2)]
    groups = [
        ada, wide(w_in[:, :3584]), wide(g["w_out"][0]),
        np.stack([g["w1"][0].reshape(N_EXP, KD, P, 512).transpose(0, 2, 1, 3).reshape(N_EXP, P, TILE),
                  g["w3"][0].reshape(N_EXP, KD, P, 512).transpose(0, 2, 1, 3).reshape(N_EXP, P, TILE),
                  g["w2"][0].reshape(N_EXP, 4, P, 1024).transpose(0, 2, 1, 3).reshape(N_EXP, P, TILE)],
                 axis=1).reshape(3 * N_EXP, P, TILE),
        wide(gla[:, :3072]), wide(gla[:, 3088:]), kv[0], wide(g["w_out_2"][0]),
        wide(g["s5_w_in_2"][0]), kv[1], wide(g["s5_w_glu_2"][0]), wide(g["w_out_2"][1]),
    ]
    experts = groups.pop(3)
    weights = np.concatenate(groups, axis=0)
    assert weights.shape[0] == T_END

    def by_feature(v, n):
        return v.reshape(n, P).T

    cols = np.zeros((P, N_COLS), np.float32)

    def put_col(name, value):
        a, b = COLS[name]
        cols[:value.shape[0], a:b] = value

    put_col("c", by_feature(g["c"][0], 8))
    b_ada = g["b_ada"][0].reshape(6, 1024)
    put_col("b_ada", by_feature(np.concatenate([b_ada[0], b_ada[1], b_ada[3], b_ada[4]]), 32))
    put_col("norm1_g", by_feature(g["norm1_g"][0], 8))
    put_col("norm2_g", by_feature(g["norm2_g"][0], 8))
    put_col("conv_w", g["conv_w"][0].reshape(4, 8, P).transpose(2, 1, 0).reshape(P, 32))
    put_col("conv_b", by_feature(g["conv_b"][0], 8))
    put_col("norm_w_2", by_feature(g["norm_w_2"], 16))
    put_col("mem_norm_w", by_feature(g["mem_norm_w_2"], 8))
    put_col("s5_d", by_feature(g["s5_d_2"][0], 16))
    put_col("s5_b_glu", by_feature(g["s5_b_glu_2"][0], 16))
    put_col("b_gate", g["b_gate"][0].reshape(2, 4).T)

    rows = np.concatenate([b_ada[2], b_ada[5], g["attn_out_g"][0], g["mlstm_out_g"][0], g["norm_f_g"], g["b_rg"][0],
                           g["b_re"][0], g["gla_gate_bias_2"][0], g["gla_out_norm_w_2"][0], g["final_norm_w_2"]])
    arrays = {
        "weights": weights, "experts": experts, "cols": cols, "rows": rows, "consts": constants(),
        "positions": g["positions"].reshape(TT, P).T,
        "x": g["x"].reshape(TT, P, D).transpose(1, 0, 2), "mem": g["mem_2"].reshape(TT, P, D).transpose(1, 0, 2),
        "w_gate": w_in[:, 3584:].reshape(KD, P, 8).transpose(1, 0, 2),
        "w_router": np.concatenate([g["w_rg"][0], g["w_re"][0]], axis=1).reshape(KD, P, 36).transpose(1, 0, 2),
        "w_rank": gla[:, 3072:3088].reshape(KD, P, 16).transpose(1, 0, 2), "w_up": g["gla_w_gate_up_2"][0],
        **s5_arrays(g),
    }
    nc = bacc.Bacc("TRN2", target_bir_lowering=False, num_devices=1)
    fed, dram = {}, {}
    for name, value in arrays.items():
        fed[f"in_{name}"] = np.ascontiguousarray(value)
        dram[name] = nc.dram_tensor(f"in_{name}", value.shape, mybir.dt.from_np(value.dtype), kind="ExternalInput").ap()
    out = nc.dram_tensor("out_0", (1, TOK, D), F32, kind="ExternalOutput").ap()
    build(nc, dram, out)
    return run_bass_kernel_spmd(nc, [fed], core_ids=[0]).results[0]["out_0"]
```
